# Optimizing a Trainium2 kernel written in Bass

```python
import jax, jax.numpy as jnp
from jax import lax
import numpy as np

D_MODEL = 1024
BATCH = 1
SEQ = 1024
DEPTH = 1

CHUNK = 64
D_MIX = D_MODEL
A_WIDTH = 512
A_GROUPS = 4
A_GROUP_DIM = A_WIDTH // A_GROUPS
A_BLOCK = 128
B_HEADS = 8
B_HEAD_DIM = 64
B_WIDTH = B_HEADS * B_HEAD_DIM
B_KV_DIM = B_HEAD_DIM
IDX_HEADS = 8
IDX_DIM = 64
TOPK_MAX = 256
Q_BLOCK = 128
NORM_EPS = 1e-6
NEG = -1e30
IN_SIZES = (A_WIDTH, A_WIDTH, A_WIDTH,
            B_WIDTH, B_KV_DIM, B_KV_DIM, B_WIDTH,
            IDX_HEADS * IDX_DIM, IDX_DIM, IDX_HEADS)
D_IN = 3272

kernel_name = "hybrid_sgu_dsa_chunk_causal_block"

def rmsnorm(x, g):
    x32 = x.astype(jnp.float32)
    y = x32 * lax.rsqrt(jnp.mean(x32 * x32, axis=-1, keepdims=True) + NORM_EPS)
    return (y * g.astype(jnp.float32)).astype(x.dtype)

def layernorm(x, g):
    x32 = x.astype(jnp.float32)
    mu = jnp.mean(x32, axis=-1, keepdims=True)
    var = jnp.mean(jnp.square(x32 - mu), axis=-1, keepdims=True)
    y = (x32 - mu) * lax.rsqrt(var + NORM_EPS)
    return (y * g.astype(jnp.float32)).astype(x.dtype)

def split_cols(h, sizes):
    outs, off = [], 0
    for s in sizes:
        outs.append(h[..., off:off + s])
        off += s
    return outs

def spatial_gating(u, v, v_gain, w_s, b_s):
    bsz, seq, _ = u.shape
    nb = seq // A_BLOCK
    u = jax.nn.gelu(u)
    v = jax.nn.gelu(v).reshape(bsz, nb, A_BLOCK, A_GROUPS, A_GROUP_DIM)
    v = layernorm(v, v_gain.reshape(A_GROUPS, A_GROUP_DIM))
    pos = jnp.arange(A_BLOCK)
    mask = (pos[None, :] // CHUNK) <= (pos[:, None] // CHUNK)
    w = jnp.where(mask[None], w_s, jnp.zeros_like(w_s))
    s = jnp.einsum('gij,bnjgc->bnigc', w, v) + b_s.T[None, None, :, :, None]
    return u * s.reshape(bsz, seq, A_WIDTH)

def sparse_attention(q, k, v, qi, ki, wi):
    bsz, seq = q.shape[:2]
    topk = min(TOPK_MAX, seq // 4)
    nb = seq // Q_BLOCK
    key_chunk = jnp.arange(seq) // CHUNK
    slopes = 2.0 ** (-8.0 * jnp.arange(1, B_HEADS + 1, dtype=jnp.float32) / B_HEADS)
    scale = B_HEAD_DIM ** -0.5
    ki32 = ki.astype(jnp.float32)
    gather = jax.vmap(lambda a, i: a[i])

    def to_blocks(a):
        return a.reshape(bsz, nb, Q_BLOCK, *a.shape[2:]).swapaxes(0, 1)

    def block(args):
        qb, qib, wib, qpos = args
        logits = jnp.einsum('bqhd,bsd->bqhs', qib.astype(jnp.float32), ki32)
        idx_score = jnp.einsum('bqhs,bqh->bqs', jax.nn.relu(logits), wib.astype(jnp.float32))
        qchunk = qpos // CHUNK
        admissible = key_chunk[None, :] <= qchunk[:, None]
        idx_score = jnp.where(admissible[None], idx_score, NEG)
        _, sel = lax.top_k(idx_score, topk)
        valid = (sel // CHUNK) <= qchunk[None, :, None]
        k_sel = gather(k, sel)
        v_sel = gather(v, sel)
        scores = jnp.einsum('bqhd,bqkd->bhqk', qb, k_sel).astype(jnp.float32) * scale
        dist = jnp.abs(qpos[None, :, None] - sel).astype(jnp.float32)
        scores = scores - slopes[None, :, None, None] * dist[:, None]
        scores = jnp.where(valid[:, None], scores, NEG)
        p = jax.nn.softmax(scores, axis=-1).astype(v.dtype)
        return jnp.einsum('bhqk,bqkd->bqhd', p, v_sel)

    qpos_blocks = jnp.arange(seq).reshape(nb, Q_BLOCK)
    out = lax.map(block, (to_blocks(q), to_blocks(qi), to_blocks(wi), qpos_blocks))
    return out.swapaxes(0, 1).reshape(bsz, seq, B_HEADS * B_KV_DIM)

def setup_inputs(seed: int = 0) -> dict:
    key = jax.random.key(seed)
    ks = jax.random.split(key, 11)
    f32 = jnp.float32
    return {
        "x": jax.random.normal(ks[0], (BATCH, SEQ, D_MODEL), f32),
        "norm_gain": 1.0 + 0.02 * jax.random.normal(ks[1], (DEPTH, D_MODEL), f32),
        "w_in": jax.random.normal(ks[2], (DEPTH, D_MODEL, D_IN), f32) * D_MODEL ** -0.5,
        "sgu_norm_gain": 1.0 + 0.02 * jax.random.normal(ks[3], (DEPTH, A_WIDTH), f32),
        "sgu_w": jax.random.normal(ks[4], (DEPTH, A_GROUPS, A_BLOCK, A_BLOCK), f32) * A_BLOCK ** -0.5,
        "sgu_b": 1.0 + 0.1 * jax.random.normal(ks[5], (DEPTH, A_GROUPS, A_BLOCK), f32),
        "q_norm_gain": 1.0 + 0.02 * jax.random.normal(ks[6], (DEPTH, B_HEAD_DIM), f32),
        "k_norm_gain": 1.0 + 0.02 * jax.random.normal(ks[7], (DEPTH, B_HEAD_DIM), f32),
        "idx_k_norm_gain": 1.0 + 0.02 * jax.random.normal(ks[8], (DEPTH, IDX_DIM), f32),
        "branch_norm_gain": 1.0 + 0.02 * jax.random.normal(ks[9], (DEPTH, D_MIX), f32),
        "w_out": jax.random.normal(ks[10], (DEPTH, D_MIX, D_MODEL), f32) * D_MIX ** -0.5,
    }

def reference(x, norm_gain, w_in, sgu_norm_gain, sgu_w, sgu_b, q_norm_gain, k_norm_gain,
              idx_k_norm_gain, branch_norm_gain, w_out):
    bsz, seq, _ = x.shape
    idx_w_scale = (IDX_HEADS ** -0.5) * (IDX_DIM ** -0.5)
    for l in range(DEPTH):
        h = rmsnorm(x, norm_gain[l])
        proj = jnp.einsum('bsd,de->bse', h, w_in[l])
        a_u, a_v, a_z, b_q, b_k, b_v, b_z, i_q, i_k, i_w = split_cols(proj, IN_SIZES)
        ya = spatial_gating(a_u, a_v, sgu_norm_gain[l], sgu_w[l], sgu_b[l])
        q = rmsnorm(b_q.reshape(bsz, seq, B_HEADS, B_HEAD_DIM), q_norm_gain[l])
        k = rmsnorm(b_k, k_norm_gain[l])
        qi = i_q.reshape(bsz, seq, IDX_HEADS, IDX_DIM)
        ki = layernorm(i_k, idx_k_norm_gain[l])
        wi = i_w * idx_w_scale
        yb = sparse_attention(q, k, b_v, qi, ki, wi)
        ga = branch_norm_gain[l, :A_WIDTH].reshape(A_GROUPS, A_GROUP_DIM)
        gb = branch_norm_gain[l, A_WIDTH:].reshape(B_HEADS, B_KV_DIM)
        oa = rmsnorm(ya.reshape(bsz, seq, A_GROUPS, A_GROUP_DIM), ga).reshape(bsz, seq, A_WIDTH)
        ob = rmsnorm(yb.reshape(bsz, seq, B_HEADS, B_KV_DIM), gb).reshape(bsz, seq, B_WIDTH)
        mixed = jnp.concatenate([oa * jax.nn.silu(a_z), ob * jax.nn.silu(b_z)], axis=-1)
        x = x + jnp.einsum('bse,ed->bsd', mixed, w_out[l])
    return x


_drawn_inputs = setup_inputs


def setup_inputs(seed=0):
    import zlib

    import numpy as np

    out = dict(_drawn_inputs(seed))
    spreads = {}
    factors = {'sgu_norm_gain': 8.0,
     'sgu_b': 2.994,
     'q_norm_gain': 8.0,
     'k_norm_gain': 8.0,
     'branch_norm_gain': 5.554}
    for name, (base, spread) in spreads.items():
        noise = np.random.default_rng([zlib.crc32(name.encode()), seed]).standard_normal(out[name].shape)
        drawn = base * np.exp(spread * noise) if base else spread * noise
        out[name] = __import__('jax').numpy.asarray(drawn.astype(out[name].dtype))
    for name, factor in factors.items():
        out[name] = (out[name] * factor).astype(out[name].dtype)
    return out
```

```python
from contextlib import ExitStack

import concourse.bass as bass
from concourse import mybir

F32 = mybir.dt.float32
F32R = mybir.dt.float32r
F16 = mybir.dt.float16
BF16 = mybir.dt.bfloat16
I32 = mybir.dt.int32
ALU = mybir.AluOpType
ACT = mybir.ActivationFunctionType
AX = mybir.AxisListType

P = 128
HALF = 64
BANK = 512
TOPK = 256
NEG = -1e30
EPS = 1e-6
BIG = 3.0e38


def hybrid_block(nc, x, norm_gain, w_in, sgu_norm_gain, sgu_w, sgu_b, q_norm_gain, k_norm_gain,
                 idx_k_norm_gain, branch_norm_gain, w_out, out):
    _, S, D = x.shape
    T = S // P
    KB = D // P
    G = sgu_w.shape[1]
    H = 8
    DH = q_norm_gain.shape[1]
    A_W = G * P
    B_W = H * DH
    T0 = TOPK // P
    IDX_SCALE = (H ** -0.5) * (DH ** -0.5)
    assert (S, D, G, DH, A_W, B_W) == (1024, 1024, 4, 64, 512, 512)

    o_au, o_av, o_az, o_bq = 0, A_W, 2 * A_W, 3 * A_W
    o_bk = o_bq + B_W
    o_bz = o_bk + 2 * DH
    o_iq = o_bz + B_W
    o_ik = o_iq + H * DH
    NKV = 2 * DH
    NIK = DH + H
    N0 = NKV + NIK
    KVI, IQ, AV, AU, AZ, BZ, BQ, O1, O2 = range(9)
    chunk_src = {IQ: o_iq, AV: o_av, AU: o_au, AZ: o_az, BZ: o_bz, BQ: o_bq}

    def unit(c, t):
        return t if c == KVI else T * c + t - T0

    UNITS = unit(BQ, T - 1) + 1

    def keys(t):
        return P * (t + 1)

    sc_off = {t: sum(keys(s) for s in range(T0, t)) for t in range(T0, T)}
    SC_COLS = sum(keys(t) for t in range(T0, T))

    ctx = ExitStack()
    with ctx:
        def psum(name, shape):
            return ctx.enter_context(nc.psum_tensor(name, shape, F32))

        def sem(name):
            return ctx.enter_context(nc.semaphore(name))

        base = (nc.sbuf_base + 63) // 64 * 64
        size_of = {F32: 4, F32R: 4, I32: 4, F16: 2, BF16: 2}
        top = [base]

        def place(name, shape, dt, at=None):
            n = size_of[dt]
            for s in shape[1:]:
                n *= s
            where = top[0] if at is None else at
            if at is None:
                top[0] = where + (n + 31) // 32 * 32
                assert top[0] <= nc.sbuf_usable_end, (name, top[0] - nc.sbuf_usable_end)
            return nc.alloc_sbuf_tensor_at(name, shape, dt, offset=where)

        w_hi = [place(f"w_hi{i}", [P, KB, BANK], F32R) for i in range(2)]
        w_lo = [place(f"w_lo{i}", [P, KB, BANK], F32R) for i in range(2)]
        NSTAGE = 3
        stage = place("stage", [P, NSTAGE, BANK], F32)
        zone_x = top[0]
        xT_hi = place("xT_hi", [P, KB, S], F32R)
        xT_lo = place("xT_lo", [P, KB, S], F32R)
        end_x = top[0]
        cur = [zone_x]

        def place_x(name, shape, dt):
            n = size_of[dt]
            for s in shape[1:]:
                n *= s
            t = place(name, shape, dt, at=cur[0])
            cur[0] += (n + 31) // 32 * 32
            assert cur[0] <= end_x, name
            return t

        q_stack = [place_x(f"q_stack{i}", [P, H, P], F32R) for i in range(2)]
        probs = place_x("probs", [P, 2, S], F32)
        probsT = [place_x(f"probsT{i}", [P, T, P], F32) for i in range(2)]
        q_in = place_x("q_in", [P, 2, B_W], F32)
        z_in = place_x("z_in", [P, 2, B_W], F32)
        mixT_hi = [place_x(f"mixT_hi{i}", [P, KB, P], F32R) for i in range(2)]
        mixT_lo = [place_x(f"mixT_lo{i}", [P, KB, P], F32R) for i in range(2)]
        yb = place_x("yb", [P, 2, B_W], F32)
        ysq = place_x("ysq", [P, B_W], F32)
        res = place_x("res", [P, 2, D], F32)
        zone_y = top[0]
        y_a = place("y_a", [P, T, A_W], F32)
        x_in = place("x_in", [P, 4, D], F32, at=zone_y)
        qi_stack = [place(f"qi_stack{i}", [P, H, P], F32R, at=zone_y + 4096 * i) for i in range(2)]
        relu_sb = place("relu_sb", [P, 2, S], F32, at=zone_y + 8192)
        zone_s = top[0]
        score = place("score", [P, SC_COLS], F32)
        kvi_raw = place("kvi_raw", [P, KB, N0], F32, at=zone_s)
        dist_i = place("dist_i", [P, S], I32, at=zone_s + 4 * KB * N0)
        sgu_raw = place("sgu_raw", [P, G, P], F32, at=zone_s + 4 * (KB * N0 + S))
        assert KB * N0 + S + G * P <= SC_COLS
        k_hh = place("k_hh", [P, S], F32R)
        k_ll = place("k_ll", [P, S], F32R)
        ki_hh = place("ki_hh", [P, S], F32R)
        ki_ll = place("ki_ll", [P, S], F32R)
        v_sb = place("v_sb", [P, T, DH], F32)
        negdist = place("negdist", [P, S], F32)
        ident = place("ident", [P, P], F32)
        nat = place("nat", [P, 2, BANK], F32)
        kvi = place("kvi", [P, 2, N0], F32)
        khat = place("khat", [P, 2, 2, DH], F32)
        wT_sgu = place("wT_sgu", [P, G, P], F32)
        vg_row = place("vg_row", [P, A_W], F32)
        gt = place("gt", [P, S], BF16)
        eq = place("eq", [P, S], BF16)
        rank = place("rank", [P, S], F16)
        g_in = place("g_in", [P, KB], F32)
        g_out = place("g_out", [P, KB], F32)
        gq = place("gq", [P, 1], F32)
        gk = place("gk", [P, 1], F32)
        gik = place("gik", [P, 1], F32)
        bias_s = place("bias_s", [P, G], F32)
        q_scale = place("q_scale", [P, H], F32)
        nhalf = place("nhalf", [P, H], F32)
        ss_x = place("ss_x", [P, T], F32)
        rstd_x = place("rstd_x", [P, T], F32)
        kstat = place("kstat", [P, 2, 4], F32)
        krstd = place("krstd", [P, 2, 2], F32)
        idx_w = place("idx_w", [P, T, H], F32)
        bn6 = place("bn6", [P, G, 6], F32)
        vstat = place("vstat", [P, G, 2], F32)
        vrstd = place("vrstd", [P, G], F32)
        ya_ms = place("ya_ms", [P, T, G], F32)
        ya_r = place("ya_r", [P, T, G], F32)
        cnt = place("cnt", [P, T], F32)
        delta = place("delta", [P, T], I32)
        cand = place("cand", [P, T], I32)
        room = place("room", [P, T], F32)
        qss = place("qss", [P, H], F32)
        qr = place("qr", [P, H], F32)
        negmax = place("negmax", [P, 2, H], F32)
        den = place("den", [P, 2, H], F32)
        rden = place("rden", [P, H], F32)
        yss = place("yss", [P, H], F32)
        yr = place("yr", [P, H], F32)
        bn_tmp = place("bn_tmp", [P, DH], F32)[:, :]
        q_sq_tmp = wT_sgu[:, :, :].rearrange("p g i -> p (g i)")
        ya_tmp = wT_sgu
        CONSTS = 16 * 10

        ps_proj = [psum(f"ps_proj{i}", [P, BANK]) for i in range(2)]
        ps_tp = [psum(f"ps_tp{i}", [P, BANK]) for i in range(2)]
        ps_lg = [psum(f"ps_lg{i}", [P, S]) for i in range(2)]
        ps_out, ps_pv = ps_proj

        q_dram = nc.dram_tensor("q_scratch", (S, B_W), F32, kind="Internal").ap()
        z_dram = nc.dram_tensor("z_scratch", (S, B_W), F32, kind="Internal").ap()

        x_loaded = [sem(f"x_loaded{i}") for i in range(4)]
        kvi_loaded = sem("kvi_loaded")
        stage_loaded = [sem(f"stage_loaded{i}") for i in range(NSTAGE)]
        consts_loaded = sem("consts_loaded")
        sgu_loaded = sem("sgu_loaded")
        setup_step = sem("setup_step")
        ident_ready = sem("ident_ready")
        dist_ready = sem("dist_ready")
        w_scaled = sem("w_scaled")
        w_hi_done = sem("w_hi_done")
        w_lo_done = sem("w_lo_done")
        xT_done = sem("xT_done")
        ss_done = sem("ss_done")
        ms_ready = sem("ms_ready")
        rstd_ready = sem("rstd_ready")
        x_hi_done = sem("x_hi_done")
        x_lo_done = sem("x_lo_done")
        proj_done = sem("proj_done")
        proj_evac = sem("proj_evac")
        kstat_done = sem("kstat_done")
        kms_ready = sem("kms_ready")
        krstd_done = sem("krstd_done")
        khat_done = sem("khat_done")
        kvi_used = sem("kvi_used")
        kT_done = sem("kT_done")
        k_hi_done = sem("k_hi_done")
        k_lo_done = sem("k_lo_done")
        sguT_done = sem("sguT_done")
        sguT_copied = sem("sguT_copied")
        qiT_done = sem("qiT_done")
        qi_hi_done = sem("qi_hi_done")
        qi_lo_done = sem("qi_lo_done")
        logits_done = sem("logits_done")
        relu_done = sem("relu_done")
        score_acc = sem("score_acc")
        vstat_done = sem("vstat_done")
        veps_done = sem("veps_done")
        vrstd_done = sem("vrstd_done")
        vhat_done = sem("vhat_done")
        vgain_done = sem("vgain_done")
        sgu_done = sem("sgu_done")
        gate_ready = sem("gate_ready")
        ya_done = sem("ya_done")
        ya_ms_done = sem("ya_ms_done")
        ya_eps_done = sem("ya_eps_done")
        ya_r_done = sem("ya_r_done")
        mixA_done = sem("mixA_done")
        dve_step = sem("dve_step")
        z_stored = [sem(f"z_stored{i}") for i in range(2)]
        q_stored = [sem(f"q_stored{i}") for i in range(2)]
        q_sq = sem("q_sq")
        q_ss = sem("q_ss")
        q_step = sem("q_step")
        q_normed = sem("q_normed")
        mask_ready = sem("mask_ready")
        q_loaded = [sem(f"q_loaded{i}") for i in range(2)]
        z_loaded = [sem(f"z_loaded{i}") for i in range(2)]
        res_loaded = [sem(f"res_loaded{i}") for i in range(2)]
        qT_done = sem("qT_done")
        q_hi_done = sem("q_hi_done")
        q_lo_done = sem("q_lo_done")
        s_done = sem("s_done")
        max_done = sem("max_done")
        exp_done = sem("exp_done")
        pT_done = sem("pT_done")
        pT2_done = sem("pT2_done")
        tile_counted = sem("tile_counted")
        sguT_masked = sem("sguT_masked")
        pT_act = sem("pT_act")
        pT_dve = sem("pT_dve")
        pv_done = sem("pv_done")
        rden_done = sem("rden_done")
        y_ready = sem("y_ready")
        y_sq = sem("y_sq")
        y_ss = sem("y_ss")
        y_step = sem("y_step")
        mixB_done = sem("mixB_done")
        mT_done = sem("mT_done")
        m_hi_done = sem("m_hi_done")
        m_lo_done = sem("m_lo_done")
        out_acc = sem("out_acc")
        out_ready = sem("out_ready")
        out_stored = [sem(f"out_stored{i}") for i in range(2)]

        tp_plan = []
        for t in range(T):
            tp_plan.append(("k", t))
        tp_plan.append(("w", 0))
        for t in range(T0, T):
            tp_plan.append(("qi", t))
        for t in range(T):
            tp_plan.append(("sgu", t))
        for t in range(T):
            for h in range(H):
                if h == 0 and t == 0:
                    tp_plan.append(("q", 0))
                tp_plan += [("p", t, h, g) for g in range(1 + (t >= 4))]
                if h == 1 and t > 0:
                    tp_plan += [("m", t - 1, 0), ("m", t - 1, 1)]
                if h == 4 and t + 1 < T:
                    tp_plan.append(("q", t + 1))
        tp_plan += [("m", T - 1, 0), ("m", T - 1, 1)]
        tp_slot = {key: n % 2 for n, key in enumerate(tp_plan)}

        def head_no(t, h):
            return H * t + h

        second_groups = {t: H * max(0, t - 4) for t in range(T)}

        def tp_release(key):
            kind = key[0]
            if kind == "k":
                return k_lo_done, key[1] + 1
            if kind == "w":
                return sguT_copied, 1
            if kind == "qi":
                return qi_lo_done, 2 * (key[1] - T0) + 2
            if kind == "sgu":
                return gate_ready, key[1] + 1
            if kind == "q":
                return q_lo_done, 2 * key[1] + 2
            if kind == "m":
                return m_lo_done, 2 * key[1] + key[2] + 1
            t, h, g = key[1:]
            if g == 0:
                return pT_act, head_no(t, h) + 1
            return pT_dve, second_groups[t] + h + 1

        block = ctx.enter_context(nc.Block())

        @block.sync
        def _(sp):
            def load_x(t):
                if t >= 4:
                    sp.wait_ge(xT_done, t - 3)
                    sp.wait_ge(ss_done, t - 3)
                sp.dma_start(x_in[:, t % 4, :], x[0, P * t:P * (t + 1), :]).then_inc(x_loaded[t % 4], 16)

            def load_w(c, k):
                n = KB * (c - 1) + k
                if n >= NSTAGE:
                    sp.wait_ge(w_lo_done, KB + n - NSTAGE + 1)
                if c < O1:
                    src = w_in[0, P * k:P * (k + 1), chunk_src[c]:chunk_src[c] + BANK]
                else:
                    src = w_out[0, P * k:P * (k + 1), BANK * (c - O1):BANK * (c - O1 + 1)]
                sp.dma_start(stage[:, n % NSTAGE, :], src).then_inc(stage_loaded[n % NSTAGE], 16)

            load_x(0)
            w_rows = w_in[0].rearrange("(k p) n -> p k n", p=P)
            sp.dma_start(kvi_raw[:, :, 0:NKV], w_rows[:, :, o_bk:o_bk + NKV]).then_inc(kvi_loaded, 16)
            sp.dma_start(kvi_raw[:, :, NKV:N0], w_rows[:, :, o_ik:o_ik + NIK]).then_inc(kvi_loaded, 16)
            for t in range(1, 4):
                load_x(t)
            for t in range(4, T):
                load_x(t)
                if t - 4 < NSTAGE:
                    load_w(IQ, t - 4)
            for c in range(IQ, BZ + 1):
                for k in range(NSTAGE if c == IQ else 0, KB):
                    load_w(c, k)

            def store_z(t):
                sp.wait_ge(proj_evac, unit(BZ, t) + 1)
                sp.dma_start(z_dram[P * t:P * (t + 1), :],
                             nat[:, unit(BZ, t) % 2, :]).then_inc(z_stored[t % 2], 16)

            def store_q(t):
                sp.wait_ge(q_normed, t + 1)
                sp.dma_start(q_dram[P * t:P * (t + 1), :],
                             nat[:, unit(BQ, t) % 2, :]).then_inc(q_stored[t % 2], 16)

            for t in range(T):
                load_w(BQ, t)
                store_z(t)
            for t in range(T):
                load_w(O1, t)
                store_q(t)

            def rows(t):
                return slice(P * t, P * (t + 1))

            def load_q(t):
                if t >= 2:
                    sp.wait_ge(qT_done, t - 1)
                sp.dma_start(q_in[:, t % 2, :], q_dram[rows(t), :]).then_inc(q_loaded[t % 2], 16)

            def load_z(t):
                if t >= 2:
                    sp.wait_ge(mixB_done, t - 1)
                sp.dma_start(z_in[:, t % 2, :], z_dram[rows(t), :]).then_inc(z_loaded[t % 2], 16)

            def load_res(t):
                if t >= 2:
                    sp.wait_ge(out_stored[t % 2], 16 * (t // 2))
                sp.dma_start(res[:, t % 2, :], x[0, rows(t), :]).then_inc(res_loaded[t % 2], 16)

            def store_out(t):
                sp.wait_ge(out_ready, 2 * (t + 1))
                sp.dma_start(out[0, P * t:P * (t + 1), :], res[:, t % 2, :]).then_inc(out_stored[t % 2], 16)

            sp.wait_ge(proj_done, UNITS)
            for i in range(2):
                sp.wait_ge(q_stored[i], 16 * T // 2)
                sp.wait_ge(z_stored[i], 16 * T // 2)
            for t in range(2):
                load_q(t)
                load_z(t)
                load_res(t)
            for k in range(KB):
                load_w(O2, k)
            for t in range(T):
                if t + 2 < T:
                    load_q(t + 2)
                    load_z(t + 2)
                store_out(t)
                if t + 2 < T:
                    load_res(t + 2)
            for i in range(2):
                sp.wait_ge(out_stored[i], 16 * T // 2)

        @block.gpsimd
        def _(pool):
            pool.memset(ident[:, :], 0.0).then_inc(setup_step, 1)
            pool.wait_ge(setup_step, 1)
            pool.affine_select(out=ident[:, :], in_=ident[:, :], compare_op=ALU.not_equal, fill=1.0, base=0,
                               pattern=[[-1, P]], channel_multiplier=1).then_inc(ident_ready, 1)
            pool.memset(nhalf[:, :], -0.5).then_inc(setup_step, 1)
            for h in range(H):
                pool.memset(q_scale[:, h:h + 1], (DH ** -0.5) * 2.0 ** (h + 1)).then_inc(setup_step, 1)
            pool.wait_ge(setup_step, 2 + H)

            def distances():
                pool.iota(dist_i[:, :], pattern=[[-1, S]], base=S - P,
                          channel_multiplier=1).then_inc(dist_ready, 1)
            def w_block(n):
                c, k = divmod(n, KB)
                if c == KVI:
                    return kvi_raw[:, k, :], w_hi[0][:, k, 0:N0], w_lo[0][:, k, 0:N0], k
                return stage[:, (n - KB) % NSTAGE, :], w_hi[c % 2][:, k, :], w_lo[c % 2][:, k, :], k

            def scale_w(n):
                raw, _, _, k = w_block(n)
                if n < KB:
                    if n == 0:
                        pool.wait_ge(kvi_loaded, 32)
                        pool.wait_ge(consts_loaded, CONSTS)
                else:
                    m = n - KB
                    pool.wait_ge(stage_loaded[m % NSTAGE], 16 * (m // NSTAGE + 1))
                gain = g_in if n < KB * O1 else g_out
                pool.tensor_scalar(raw, raw, gain[:, k:k + 1], None, ALU.mult).then_inc(w_scaled, 1)

            def split_w(n):
                raw, hi, lo, _ = w_block(n)
                pool.wait_ge(w_hi_done, n + 1)
                pool.tensor_tensor(lo, raw, hi.bitcast(F32), ALU.subtract).then_inc(w_lo_done, 1)

            def rstd_rows(t):
                pool.wait_ge(ss_done, t + 1)
                pool.tensor_scalar(rstd_x[:, t:t + 1], ss_x[:, t:t + 1], 1.0 / D, EPS, ALU.mult,
                                   ALU.add).then_inc(ms_ready, 1)
                pool.wait_ge(ms_ready, t + 1)
                pool.tensor_tensor(rstd_x[:, t:t + 1], rstd_x[:, t:t + 1], nhalf[:, 0:1],
                                   ALU.pow).then_inc(rstd_ready, 1)

            def k_rows(t):
                rows = kvi[:, t % 2, :]
                pool.wait_ge(proj_evac, unit(KVI, t) + 1)
                pool.tensor_copy(v_sb[:, t, :], rows[:, DH:NKV]).then_inc(kvi_used, 1)
                pool.tensor_scalar(idx_w[:, t, :], rows[:, NKV + DH:N0], IDX_SCALE, None,
                                   ALU.mult).then_inc(kvi_used, 1)
                pool.wait_ge(kstat_done, 2 * (t + 1))
                pool.tensor_scalar(krstd[:, t % 2, :], kstat[:, t % 2, 1:3], EPS, None,
                                   ALU.add).then_inc(kms_ready, 1)
                pool.wait_ge(kms_ready, t + 1)
                pool.tensor_tensor(krstd[:, t % 2, :], krstd[:, t % 2, :], nhalf[:, 0:2],
                                   ALU.pow).then_inc(krstd_done, 1)

            distances()
            scale_w(0)
            for n in range(KB):
                if n + 1 < KB:
                    scale_w(n + 1)
                split_w(n)
                if n == 1:
                    rstd_rows(0)
            pool.wait_ge(dist_ready, 2)
            pool.memset(negdist[0:HALF, S - HALF:S], NEG).then_inc(dist_ready, 1)
            for t in range(T):
                if t + 1 < T:
                    rstd_rows(t + 1)
                if t < KB:
                    scale_w(KB + t)
                k_rows(t)
                split_w(KB + t)

            def next_block(c, t):
                scale_w(KB * (c + 1) + t)
                split_w(KB * (c + 1) + t)

            for t in range(T0, T):
                next_block(IQ, t - T0)
            next_block(IQ, KB - 2)
            next_block(IQ, KB - 1)

            def av(t):
                pool.wait_ge(vstat_done, t + 1)
                pool.tensor_scalar(vrstd[:, :], vstat[:, :, 1], EPS, None, ALU.add).then_inc(veps_done, 1)
                pool.wait_ge(veps_done, t + 1)
                pool.tensor_tensor(vrstd[:, :], vrstd[:, :], nhalf[:, 0:G], ALU.pow).then_inc(vrstd_done, 1)
                rows = nat[:, unit(AV, t) % 2, :]
                pool.wait_ge(vhat_done, t + 1)
                pool.tensor_tensor(rows, rows, vg_row[:, :], ALU.mult).then_inc(vgain_done, 1)

            def au(t):
                pool.wait_ge(proj_evac, unit(AU, t) + 1)
                pool.wait_ge(gate_ready, t + 1)
                pool.tensor_tensor(y_a[:, t, :], y_a[:, t, :], nat[:, unit(AU, t) % 2, :],
                                   ALU.mult).then_inc(ya_done, 1)

            def au_r(t):
                pool.wait_ge(ya_ms_done, t + 1)
                pool.tensor_scalar(ya_r[:, t, :], ya_ms[:, t, :], EPS, None, ALU.add).then_inc(ya_eps_done, 1)
                pool.wait_ge(ya_eps_done, t + 1)
                pool.tensor_tensor(ya_r[:, t, :], ya_r[:, t, :], nhalf[:, 0:G], ALU.pow).then_inc(ya_r_done, 1)

            for t in range(T):
                av(t)
                next_block(AV, t)
            for t in range(T):
                au(t)
                next_block(AU, t)
                if t > 0:
                    au_r(t - 1)
            au_r(T - 1)
            for t in range(T):
                next_block(AZ, t)
            for t in range(T):
                next_block(BZ, t)

            def bq(t):
                rows = nat[:, unit(BQ, t) % 2, :]
                heads = rows.rearrange("p (h d) -> p h d", h=H)
                pool.wait_ge(proj_evac, unit(BQ, t) + 1)
                if t > 0:
                    pool.wait_ge(q_ss, t)
                pool.tensor_tensor(q_sq_tmp, rows, rows, ALU.mult).then_inc(q_sq, 1)
                pool.wait_ge(q_ss, t + 1)
                pool.tensor_scalar(qr[:, :], qss[:, :], 1.0 / DH, EPS, ALU.mult, ALU.add).then_inc(q_step, 1)
                pool.wait_ge(q_step, 3 * t + 1)
                pool.tensor_tensor(qr[:, :], qr[:, :], nhalf[:, :], ALU.pow).then_inc(q_step, 1)
                pool.wait_ge(q_step, 3 * t + 2)
                pool.tensor_tensor(qr[:, :], qr[:, :], q_scale[:, :], ALU.mult).then_inc(q_step, 1)
                pool.wait_ge(q_step, 3 * t + 3)
                pool.tensor_tensor(heads, heads, qr[:, :].unsqueeze(2).broadcast_to([P, H, DH]),
                                   ALU.mult).then_inc(q_normed, 1)

            for t in range(T):
                bq(t)
                next_block(BQ, t)

            def finish_b(t):
                rows = yb[:, t % 2, :]
                heads = rows.rearrange("p (h d) -> p h d", h=H)
                pool.wait_ge(y_ready, t + 1)
                if t > 0:
                    pool.wait_ge(y_ss, t)
                pool.tensor_tensor(ysq[:, :], rows, rows, ALU.mult).then_inc(y_sq, 1)
                pool.wait_ge(y_ss, t + 1)
                pool.tensor_scalar(yr[:, :], yss[:, :], 1.0 / DH, EPS, ALU.mult, ALU.add).then_inc(y_step, 1)
                pool.wait_ge(y_step, 3 * t + 1)
                pool.tensor_tensor(yr[:, :], yr[:, :], nhalf[:, :], ALU.pow).then_inc(y_step, 1)
                pool.wait_ge(y_step, 3 * t + 2)
                pool.tensor_tensor(heads, heads, yr[:, :].unsqueeze(2).broadcast_to([P, H, DH]),
                                   ALU.mult).then_inc(y_step, 1)
                pool.wait_ge(y_step, 3 * t + 3)
                pool.wait_ge(z_loaded[t % 2], 16 * (t // 2 + 1))
                pool.tensor_tensor(rows, rows, z_in[:, t % 2, :], ALU.mult).then_inc(mixB_done, 1)

            for k in range(KB):
                next_block(O1, k)
            for t in range(T):
                finish_b(t)

        @block.scalar
        def _(act):
            col = lambda v, n: v.rearrange("(k p) -> p k", p=n)
            with nc.allow_non_contiguous_dma(reason="gains as columns, a few KiB"):
                act.dma_start(g_in[:, :], col(norm_gain[0], P)).then_inc(consts_loaded, 16)
                act.dma_start(g_out[:, :], col(branch_norm_gain[0], P)).then_inc(consts_loaded, 16)
                for dst, src in ((gk, k_norm_gain), (gik, idx_k_norm_gain), (gq, q_norm_gain)):
                    for half in range(2):
                        act.dma_start(dst[DH * half:DH * (half + 1), :],
                                      col(src[0], DH)).then_inc(consts_loaded, 16)
                act.dma_start(bias_s[:, :], sgu_b[0].rearrange("g i -> i g")).then_inc(consts_loaded, 16)
            act.dma_start(vg_row[:, :], sgu_norm_gain[0].partition_broadcast(P)).then_inc(consts_loaded, 16)
            act.dma_start(sgu_raw[:, :, :], sgu_w[0].rearrange("g i j -> i g j")).then_inc(sgu_loaded, 16)

            def hi_w(n):
                c, k = divmod(n, KB)
                act.wait_ge(w_scaled, n + 1)
                if k == 0 and c >= 2:
                    act.wait_ge(proj_done, T if c == 2 else min(unit(c - 1, 0), UNITS))
                if c == KVI:
                    act.copy(w_hi[0][:, k, 0:N0], kvi_raw[:, k, :]).then_inc(w_hi_done, 1)
                else:
                    act.copy(w_hi[c % 2][:, k, :], stage[:, (n - KB) % NSTAGE, :]).then_inc(w_hi_done, 1)

            def square_x(t):
                act.wait_ge(x_loaded[t % 4], 16 * (t // 4 + 1))
                if t > 0:
                    act.wait_ge(ss_done, t)
                act.activation(gt[:, :], x_in[:, t % 4, :], ACT.Square,
                               accum_out=ss_x[:, t:t + 1]).then_inc(ss_done, 1)

            def hi_x(t):
                act.wait_ge(xT_done, t + 1)
                act.copy(xT_hi[:, :, P * t:P * (t + 1)],
                         ps_lg[t % 2][:, :].rearrange("p (k s) -> p k s", k=KB)).then_inc(x_hi_done, 1)

            def evac_kvi(t):
                u = unit(KVI, t)
                act.wait_ge(proj_done, u + 1)
                act.wait_ge(rstd_ready, t + 1)
                if t >= 2:
                    act.wait_ge(kvi_used, 2 * (t - 1))
                    act.wait_ge(khat_done, 2 * (t - 1))
                act.activation(kvi[:, t % 2, :], ps_proj[u % 2][:, 0:N0], ACT.Copy,
                               scale=rstd_x[:, t:t + 1]).then_inc(proj_evac, 1)

            def hi_k(t):
                act.wait_ge(kT_done, t + 1)
                slot = ps_tp[tp_slot[("k", t)]]
                act.activation(k_hh[:, P * t:P * (t + 1)], slot[:, 0:P], ACT.Copy,
                               scale=gk[:, 0:1]).then_inc(k_hi_done, 1)
                act.activation(ki_hh[:, P * t:P * (t + 1)], slot[:, P:2 * P], ACT.Copy,
                               scale=gik[:, 0:1]).then_inc(k_hi_done, 1)

            square_x(0)
            hi_x(0)
            for k in range(KB):
                hi_w(k)
            square_x(1)
            hi_x(1)
            for t in range(T):
                evac_kvi(t)
                if t + 2 < T:
                    square_x(t + 2)
                    hi_x(t + 2)
                hi_w(KB + t)
                if t > 0:
                    hi_k(t - 1)

            nat_free = {
                IQ: lambda t: (qiT_done, t - T0 + 1),
                AV: lambda t: (sgu_done, t + 1),
                AU: lambda t: (ya_done, t + 1),
                AZ: lambda t: (mixA_done, t + 1),
                BZ: lambda t: (z_stored[t % 2], 16 * (t // 2 + 1)),
                BQ: lambda t: (q_stored[t % 2], 16 * (t // 2 + 1)),
            }
            order = [(IQ, t) for t in range(T0, T)] + [(c, t) for c in (AV, AU, AZ, BZ, BQ) for t in range(T)]
            func = {IQ: ACT.Copy, AV: ACT.Gelu_apprx_tanh, AU: ACT.Gelu_apprx_tanh, AZ: ACT.Silu,
                    BZ: ACT.Silu, BQ: ACT.Copy}

            def evac(c, t):
                u = unit(c, t)
                act.wait_ge(proj_done, u + 1)
                i = order.index((c, t))
                if i >= 2:
                    pc, pt = order[i - 2]
                    act.wait_ge(*nat_free[pc](pt))
                act.activation(nat[:, u % 2, :], ps_proj[u % 2][:, :], func[c],
                               scale=rstd_x[:, t:t + 1]).then_inc(proj_evac, 1)

            def hi_qi(t):
                if t >= T0 + 2:
                    act.wait_ge(logits_done, H * (t - T0 - 1))
                act.wait_ge(qiT_done, t - T0 + 1)
                for odd in range(2):
                    bank = ps_tp[tp_slot[("qi", t)]][HALF * odd:HALF * (odd + 1), :]
                    act.copy(qi_stack[t % 2][0:HALF, odd:H:2, :],
                             bank.rearrange("p (h s) -> p h s", h=H // 2)).then_inc(qi_hi_done, 1)

            def relus(t):
                for h in range(H):
                    m = H * (t - T0) + h
                    act.wait_ge(logits_done, m + 1)
                    if m >= 2:
                        act.wait_ge(score_acc, m - 1)
                    act.activation(relu_sb[:, m % 2, 0:keys(t)], ps_lg[m % 2][:, 0:keys(t)],
                                   ACT.Relu).then_inc(relu_done, 1)

            for t in range(T0, T):
                evac(IQ, t)
                if t == T0:
                    hi_k(T - 1)
                    act.wait_ge(sguT_done, 1)
                    act.copy(wT_sgu[:, :, :], ps_tp[tp_slot[("w", 0)]][:, :].rearrange(
                        "p (g i) -> p g i", g=G)).then_inc(sguT_copied, 1)
                if t - T0 < 3:
                    hi_w(KB * AV + t - T0)
                if t > T0:
                    hi_qi(t - 1)
                if t > T0 + 1:
                    relus(t - 2)
                    hi_w(KB * AV + t - T0 + 1)
            hi_w(KB * AV + 7)

            def w_and(c, t):
                hi_w(KB * (c + 1) + t)

            for t in range(T):
                evac(AV, t)
                if t == 0:
                    hi_qi(T - 1)
                    relus(T - 2)
                if t == 1:
                    relus(T - 1)
                w_and(AV, t)
            for c in (AU, AZ, BZ, BQ):
                for t in range(T):
                    evac(c, t)
                    w_and(c, t)

            def hi_q(t):
                if t >= 2:
                    act.wait_ge(s_done, H * (t - 1))
                act.wait_ge(qT_done, t + 1)
                for odd in range(2):
                    half = slice(HALF * odd, HALF * (odd + 1))
                    act.activation(q_stack[t % 2][0:HALF, odd:H:2, :],
                                   ps_tp[tp_slot[("q", t)]][half, :].rearrange("p (h s) -> p h s", h=H // 2),
                                   ACT.Copy, scale=gq[half, 0:1]).then_inc(q_hi_done, 1)

            def exps(t, h):
                m = head_no(t, h)
                act.wait_ge(max_done, m + 1)
                if m >= 2 * H and h == 0:
                    act.wait_ge(rden_done, t - 1)
                act.activation(probs[:, m % 2, 0:keys(t)], probs[:, m % 2, 0:keys(t)], ACT.Exp,
                               bias=negmax[:, t % 2, h:h + 1], scale=-1.0,
                               accum_out=den[:, t % 2, h:h + 1]).then_inc(exp_done, 1)

            def copy_pT(t, h):
                m = head_no(t, h)
                nb = min(t + 1, 4)
                act.wait_ge(pT_done, m + 1)
                if m >= 2:
                    act.wait_ge(pv_done, m - 1)
                act.copy(probsT[m % 2][:, 0:nb, :],
                         ps_tp[tp_slot[("p", t, h, 0)]][:, 0:P * nb].rearrange("p (b s) -> p b s", b=nb)
                         ).then_inc(pT_act, 1)

            def hi_mix(t):
                if t >= 2:
                    act.wait_ge(out_acc, 2 * (t - 1))
                for g in range(2):
                    act.wait_ge(mT_done, 2 * t + g + 1)
                    act.copy(mixT_hi[t % 2][:, 4 * g:4 * (g + 1), :],
                             ps_tp[tp_slot[("m", t, g)]][:, :].rearrange("p (k s) -> p k s", k=4)
                             ).then_inc(m_hi_done, 1)

            hi_q(0)
            exps(0, 0)
            for t in range(T):
                for h in range(H):
                    m = head_no(t, h)
                    if m + 1 < T * H:
                        exps(*divmod(m + 1, H))
                    copy_pT(t, h)
                    if t == 0:
                        hi_w(KB * O2 + h)
                    if h == 1 and t > 0:
                        hi_mix(t - 1)
                    if h == 4 and t + 1 < T:
                        hi_q(t + 1)
            hi_mix(T - 1)

        @block.tensor
        def _(pe):
            issued = []

            def tp(key):
                assert tp_plan[len(issued)] == key
                if len(issued) >= 2:
                    pe.wait_ge(*tp_release(issued[-2]))
                issued.append(key)
                return ps_tp[tp_slot[key]]

            def xT(t):
                pe.wait_ge(x_loaded[t % 4], 16 * (t // 4 + 1))
                if t >= 2:
                    pe.wait_ge(x_lo_done, t - 1)
                for k in range(KB):
                    mm = pe.transpose(ps_lg[t % 2][:, P * k:P * (k + 1)], x_in[:, t % 4, P * k:P * (k + 1)],
                                      ident[:, :])
                mm.then_inc(xT_done, 1)

            def project(c, t):
                u = unit(c, t)
                n = N0 if c == KVI else BANK
                if c == KVI:
                    pe.wait_ge(x_lo_done, t + 1)
                if u >= 2:
                    pe.wait_ge(proj_evac, u - 1)
                first = t == (T0 if c == IQ else 0)
                hi, lo = w_hi[c % 2], w_lo[c % 2]
                for k in range(KB):
                    if first:
                        pe.wait_ge(w_lo_done, KB * c + k + 1)
                    rows = slice(P * t, P * (t + 1))
                    for i, (a, b) in enumerate(((xT_hi, hi), (xT_lo, hi), (xT_hi, lo))):
                        mm = pe.matmul(ps_proj[u % 2][:, 0:n], a[:, k, rows], b[:, k, 0:n],
                                       start=(k == 0 and i == 0), stop=(k == KB - 1 and i == 2))
                mm.then_inc(proj_done, 1)

            def kT(t):
                bank = tp(("k", t))
                for i in range(2):
                    pe.wait_ge(khat_done, 2 * t + i + 1)
                    mm = pe.transpose(bank[:, P * i:P * (i + 1)],
                                      khat[:, i, :, :].rearrange("p a d -> p (a d)"), ident[:, :])
                mm.then_inc(kT_done, 1)

            def four_pairs(bank, rows):
                for j in range(H // 2):
                    mm = pe.transpose(bank[:, P * j:P * (j + 1)], rows[:, P * j:P * (j + 1)], ident[:, :])
                return mm

            def qiT(t):
                pe.wait_ge(proj_evac, unit(IQ, t) + 1)
                four_pairs(tp(("qi", t)), nat[:, unit(IQ, t) % 2, :]).then_inc(qiT_done, 1)

            def dot_keys(bank, stack, h, hh, ll, n):
                for a in range(0, n, BANK):
                    b = min(n, a + BANK)
                    pe.matmul(bank[:, a:b], stack[:, h, :], hh[:, a:b], start=True, stop=False)
                    mm = pe.matmul(bank[:, a:b], stack[:, h, :], ll[:, a:b], start=False, stop=True)
                return mm

            def logits(t):
                if t == T0:
                    pe.wait_ge(x_lo_done, T)
                    pe.wait_ge(k_lo_done, T)
                for h in range(H):
                    m = H * (t - T0) + h
                    pe.wait_ge(qi_lo_done, 2 * (t - T0) + h % 2 + 1)
                    if m >= 2:
                        pe.wait_ge(relu_done, m - 1)
                    dot_keys(ps_lg[m % 2], qi_stack[t % 2], h, ki_hh, ki_ll, keys(t)).then_inc(logits_done, 1)

            pe.wait_ge(ident_ready, 1)
            xT(0)
            xT(1)
            for t in range(T):
                project(KVI, t)
                if t + 2 < T:
                    xT(t + 2)
                if t > 0:
                    kT(t - 1)
            for t in range(T0, T):
                project(IQ, t)
                if t == T0:
                    kT(T - 1)
                    pe.wait_ge(sgu_loaded, 16)
                    bank = tp(("w", 0))
                    for g in range(G):
                        mm = pe.transpose(bank[:, P * g:P * (g + 1)], sgu_raw[:, g, :], ident[:, :])
                    mm.then_inc(sguT_done, 1)
                if t > T0:
                    qiT(t - 1)
                if t > T0 + 1:
                    logits(t - 2)

            def sgu(t):
                pe.wait_ge(vgain_done, t + 1)
                pe.wait_ge(sguT_masked, 1)
                bank = tp(("sgu", t))
                for g in range(G):
                    mm = pe.matmul(bank[:, P * g:P * (g + 1)], wT_sgu[:, g, :],
                                   nat[:, unit(AV, t) % 2, P * g:P * (g + 1)], start=True, stop=True)
                mm.then_inc(sgu_done, 1)

            for t in range(T):
                project(AV, t)
                if t == 0:
                    qiT(T - 1)
                    logits(T - 2)
                if t == 1:
                    logits(T - 1)
                if t > 0:
                    sgu(t - 1)
            project(AU, 0)
            sgu(T - 1)
            for t in range(1, T):
                project(AU, t)
            for c in (AZ, BZ, BQ):
                for t in range(T):
                    project(c, t)

            def qT(t):
                pe.wait_ge(q_loaded[t % 2], 16 * (t // 2 + 1))
                four_pairs(tp(("q", t)), q_in[:, t % 2, :]).then_inc(qT_done, 1)

            def scores(t, h):
                m = head_no(t, h)
                if h < 2:
                    pe.wait_ge(q_lo_done, 2 * t + h + 1)
                if m >= 2:
                    pe.wait_ge(max_done, m - 1)
                dot_keys(ps_lg[m % 2], q_stack[t % 2], h, k_hh, k_ll, keys(t)).then_inc(s_done, 1)

            def pT(t, h):
                m = head_no(t, h)
                pe.wait_ge(exp_done, m + 1)
                for g in range(1 + (t >= 4)):
                    bank = tp(("p", t, h, g))
                    for b in range(4 * g, min(t + 1, 4 * g + 4)):
                        mm = pe.transpose(bank[:, P * (b % 4):P * (b % 4 + 1)],
                                          probs[:, m % 2, P * b:P * (b + 1)], ident[:, :])
                    if g == 0:
                        mm.then_inc(pT_done, 1)
                    else:
                        mm.then_inc(pT2_done, 1)

            def pv(t, h):
                m = head_no(t, h)
                pe.wait_ge(pT_act, m + 1)
                if t >= 4:
                    pe.wait_ge(pT_dve, second_groups[t] + h + 1)
                if h == 0 and t > 0:
                    pe.wait_ge(y_ready, t)
                for b in range(t + 1):
                    mm = pe.matmul(ps_pv[:, DH * h:DH * (h + 1)], probsT[m % 2][:, b, :], v_sb[:, b, :],
                                   start=(b == 0), stop=(b == t))
                mm.then_inc(pv_done, 1)

            def mT(t):
                pe.wait_ge(mixB_done, t + 1)
                for g, rows in enumerate((y_a[:, t, :], yb[:, t % 2, :])):
                    bank = tp(("m", t, g))
                    for j in range(4):
                        mm = pe.transpose(bank[:, P * j:P * (j + 1)], rows[:, P * j:P * (j + 1)], ident[:, :])
                    mm.then_inc(mT_done, 1)

            def out_half(t, n):
                pe.wait_ge(m_lo_done, 2 * t + 2)
                if 2 * t + n > 0:
                    pe.wait_ge(out_ready, 2 * t + n)
                c = O1 + n
                if t == 0:
                    pe.wait_ge(w_lo_done, KB * (c + 1))
                hi, lo = w_hi[c % 2], w_lo[c % 2]
                for k in range(KB):
                    for i, (a, b) in enumerate(((mixT_hi, hi), (mixT_lo, hi), (mixT_hi, lo))):
                        mm = pe.matmul(ps_out[:, :], a[t % 2][:, k, :], b[:, k, :],
                                       start=(k == 0 and i == 0), stop=(k == KB - 1 and i == 2))
                mm.then_inc(out_acc, 1)

            pe.wait_ge(proj_evac, UNITS)
            qT(0)
            scores(0, 0)
            scores(0, 1)
            for t in range(T):
                for h in range(H):
                    m = head_no(t, h)
                    pT(t, h)
                    if m > 0:
                        pv(*divmod(m - 1, H))
                    if h == 1 and t > 0:
                        mT(t - 1)
                    if h == 4 and t + 1 < T:
                        qT(t + 1)
                    if m + 2 < T * H:
                        scores(*divmod(m + 2, H))
                    if h == 3 and t > 0:
                        out_half(t - 1, 0)
                    if h == 5 and t > 0:
                        out_half(t - 1, 1)
            pv(T - 1, H - 1)
            mT(T - 1)
            out_half(T - 1, 0)
            out_half(T - 1, 1)

        @block.vector
        def _(dve):
            steps = [0]

            def then(ins):
                steps[0] += 1
                ins.then_inc(dve_step, 1)
                dve.wait_ge(dve_step, steps[0])

            def lo_x(t):
                dve.wait_ge(x_hi_done, t + 1)
                rows = slice(P * t, P * (t + 1))
                dve.tensor_tensor(xT_lo[:, :, rows], ps_lg[t % 2][:, :].rearrange("p (k s) -> p k s", k=KB),
                                  xT_hi[:, :, rows].bitcast(F32), ALU.subtract).then_inc(x_lo_done, 1)

            def k_stats(t):
                rows = kvi[:, t % 2, :]
                dve.wait_ge(proj_evac, unit(KVI, t) + 1)
                if t >= 2:
                    dve.wait_ge(krstd_done, t - 1)
                then(dve.bn_stats(bn6[:, 0, :], rows[:, NKV:NKV + DH]))
                dve.bn_aggr(kstat[:, t % 2, 0:2], bn6[:, 0, :]).then_inc(kstat_done, 1)
                dve.tensor_tensor_reduce(bn_tmp, rows[:, 0:DH], rows[:, 0:DH], 1.0 / DH, 0.0, ALU.mult,
                                         ALU.add, kstat[:, t % 2, 2:3]).then_inc(kstat_done, 1)

            def k_norm(t):
                rows = kvi[:, t % 2, :]
                dve.wait_ge(krstd_done, t + 1)
                if t >= 1:
                    dve.wait_ge(kT_done, t)
                twice = lambda v: v.unsqueeze(1).broadcast_to([P, 2, DH])
                dve.tensor_scalar(khat[:, 0, :, :], twice(rows[:, 0:DH]), krstd[:, t % 2, 1:2], None,
                                  ALU.mult).then_inc(khat_done, 1)
                dve.tensor_scalar(khat[:, 1, :, :], twice(rows[:, NKV:NKV + DH]), kstat[:, t % 2, 0:1],
                                  krstd[:, t % 2, 0:1], ALU.subtract, ALU.mult).then_inc(khat_done, 1)

            def lo_k(t):
                dve.wait_ge(k_hi_done, 2 * (t + 1))
                bank = ps_tp[tp_slot[("k", t)]]
                cols = slice(P * t, P * (t + 1))
                dve.scalar_tensor_tensor(out=k_ll[:, cols], in0=bank[:, 0:P], scalar=gk[:, 0:1],
                                         in1=k_hh[:, cols].bitcast(F32), op0=ALU.mult, op1=ALU.subtract)
                dve.scalar_tensor_tensor(out=ki_ll[:, cols], in0=bank[:, P:2 * P], scalar=gik[:, 0:1],
                                         in1=ki_hh[:, cols].bitcast(F32), op0=ALU.mult,
                                         op1=ALU.subtract).then_inc(k_lo_done, 1)

            dve.wait_ge(dist_ready, 1)
            dve.scalar_tensor_tensor(out=negdist[:, :], in0=dist_i[:, :], scalar=-1.0, in1=dist_i[:, :],
                                     op0=ALU.mult, op1=ALU.min).then_inc(dist_ready, 1)
            dve.wait_ge(consts_loaded, CONSTS)
            lo_x(0)
            lo_x(1)
            for t in range(T):
                k_stats(t)
                if t + 2 < T:
                    lo_x(t + 2)
                k_norm(t)
                if t > 0:
                    lo_k(t - 1)

            def lo_qi(t):
                for odd in range(2):
                    dve.wait_ge(qi_hi_done, 2 * (t - T0) + odd + 1)
                    bank = ps_tp[tp_slot[("qi", t)]][HALF * odd:HALF * (odd + 1), :]
                    dve.tensor_tensor(qi_stack[t % 2][HALF:P, odd:H:2, :],
                                      bank.rearrange("p (h s) -> p h s", h=H // 2),
                                      qi_stack[t % 2][0:HALF, odd:H:2, :].bitcast(F32),
                                      ALU.subtract).then_inc(qi_lo_done, 1)

            def sum_heads(t):
                row = score[:, sc_off[t]:sc_off[t] + keys(t)]
                for h in range(H):
                    m = H * (t - T0) + h
                    dve.wait_ge(relu_done, m + 1)
                    r = relu_sb[:, m % 2, 0:keys(t)]
                    if h == 0:
                        dve.wait_ge(kvi_used, 2 * T)
                        dve.tensor_scalar(row, r, idx_w[:, t, 0:1], None, ALU.mult).then_inc(score_acc, 1)
                    else:
                        dve.wait_ge(score_acc, m)
                        dve.scalar_tensor_tensor(out=row, in0=r, scalar=idx_w[:, t, h:h + 1], in1=row,
                                                 op0=ALU.mult, op1=ALU.add).then_inc(score_acc, 1)
                dve.wait_ge(score_acc, H * (t - T0 + 1))
                then(dve.memset(row[0:HALF, keys(t) - HALF:keys(t)], NEG))

            for t in range(T0, T):
                if t == T0:
                    lo_k(T - 1)
                    dve.wait_ge(dist_ready, 3)
                    dve.wait_ge(sguT_done, 1)
                    dve.wait_ge(w_lo_done, KB)
                if t > T0:
                    lo_qi(t - 1)
                if t > T0 + 1:
                    sum_heads(t - 2)
            dve.wait_ge(sguT_copied, 1)
            dve.memset(wT_sgu[HALF:P, :, 0:HALF], 0.0).then_inc(sguT_masked, 1)

            cand_f = cand[:, :].bitcast(F32)

            hits = (gt, eq, rank)
            counted = [0]

            def count_tile(t):
                n = counted[0]
                counted[0] += 1
                if n >= len(hits):
                    dve.wait_ge(tile_counted, n - len(hits) + 1)
                return dve.tensor_scalar(hits[n % len(hits)][:, 0:keys(t)], score[:, sc_off[t]:sc_off[t] + keys(t)],
                                         cand_f[:, t:t + 1], None, ALU.is_ge, ALU.add,
                                         accum_out=cnt[:, t:t + 1]).then_inc(tile_counted, 1)

            def topk_step(b):
                for t in range(T0, T):
                    count_tile(t)
                dve.wait_ge(tile_counted, counted[0])
                c, d = cand[:, T0:T], delta[:, T0:T]
                if b == 31:
                    then(dve.tensor_scalar(d, cnt[:, T0:T], TOPK - 0.5, -1.0, ALU.is_lt, ALU.mult))
                    then(dve.tensor_scalar(c, d, 1 << 30, None, ALU.bitwise_xor))
                else:
                    then(dve.tensor_scalar(d, cnt[:, T0:T], TOPK - 0.5, float(1 << b), ALU.is_lt, ALU.mult))
                    then(dve.scalar_tensor_tensor(out=c, in0=d, scalar=(1 << b) >> 1, in1=c,
                                                  op0=ALU.bitwise_xor, op1=ALU.bitwise_xor))

            def select(t):
                row = score[:, sc_off[t]:sc_off[t] + keys(t)]
                thr = cand_f[:, t:t + 1]
                n = keys(t)
                if t > T0:
                    dve.wait_ge(mask_ready, t - T0)
                dve.tensor_scalar(gt[:, 0:n], row, thr, None, ALU.is_gt, ALU.add, accum_out=cnt[:, t:t + 1])
                then(dve.tensor_scalar(eq[:, 0:n], row, thr, None, ALU.is_equal))
                then(dve.tensor_scalar(room[:, t:t + 1], cnt[:, t:t + 1], -1.0, float(TOPK), ALU.mult, ALU.add))
                then(dve.tensor_tensor_scan(rank[:, 0:n], eq[:, 0:n], eq[:, 0:n], 0.0, ALU.add, ALU.max))
                then(dve.scalar_tensor_tensor(out=eq[:, 0:n], in0=rank[:, 0:n], scalar=room[:, t:t + 1],
                                              in1=eq[:, 0:n], op0=ALU.is_le, op1=ALU.mult))
                then(dve.scalar_tensor_tensor(out=gt[:, 0:n], in0=gt[:, 0:n], scalar=-1.0, in1=eq[:, 0:n],
                                              op0=ALU.add, op1=ALU.add))
                dve.scalar_tensor_tensor(out=row, in0=gt[:, 0:n], scalar=-NEG, in1=negdist[:, S - n:S],
                                         op0=ALU.mult, op1=ALU.add).then_inc(mask_ready, 1)

            def av_stats(t):
                rows = nat[:, unit(AV, t) % 2, :]
                dve.wait_ge(proj_evac, unit(AV, t) + 1)
                for g in range(G):
                    last = dve.bn_stats(bn6[:, g, :], rows[:, P * g:P * (g + 1)])
                then(last)
                if t > 0:
                    dve.wait_ge(vrstd_done, t)
                for g in range(G):
                    last = dve.bn_aggr(vstat[:, g, :], bn6[:, g, :])
                last.then_inc(vstat_done, 1)

            def av_norm(t):
                rows = nat[:, unit(AV, t) % 2, :]
                dve.wait_ge(vrstd_done, t + 1)
                for g in range(G):
                    cols = rows[:, P * g:P * (g + 1)]
                    last = dve.tensor_scalar(cols, cols, vstat[:, g, 0:1], vrstd[:, g:g + 1], ALU.subtract,
                                             ALU.mult)
                last.then_inc(vhat_done, 1)

            def gate(t):
                dve.wait_ge(sgu_done, t + 1)
                dve.tensor_tensor(y_a[:, t, :].rearrange("p (g c) -> p g c", g=G),
                                  ps_tp[tp_slot[("sgu", t)]][:, :].rearrange("p (g c) -> p g c", g=G),
                                  bias_s[:, :].unsqueeze(2).broadcast_to([P, G, P]),
                                  ALU.add).then_inc(gate_ready, 1)

            def ya_square(t):
                dve.wait_ge(ya_done, t + 1)
                for g in range(G):
                    cols = y_a[:, t, P * g:P * (g + 1)]
                    last = dve.tensor_tensor_reduce(ya_tmp[:, g, :], cols, cols, 1.0 / P, 0.0, ALU.mult, ALU.add,
                                                    ya_ms[:, t, g:g + 1])
                last.then_inc(ya_ms_done, 1)

            def mix_a(t):
                dve.wait_ge(proj_evac, unit(AZ, t) + 1)
                dve.wait_ge(ya_r_done, t + 1)
                for g in range(G):
                    cols = slice(P * g, P * (g + 1))
                    last = dve.scalar_tensor_tensor(out=y_a[:, t, cols], in0=y_a[:, t, cols],
                                                    scalar=ya_r[:, t, g:g + 1],
                                                    in1=nat[:, unit(AZ, t) % 2, cols],
                                                    op0=ALU.mult, op1=ALU.mult)
                last.then_inc(mixA_done, 1)

            def q_sums(t):
                dve.wait_ge(q_sq, t + 1)
                if t > 0:
                    dve.wait_ge(q_normed, t)
                dve.tensor_reduce(qss[:, :], q_sq_tmp.rearrange("p (h d) -> p h d", h=H), AX.X,
                                  ALU.add).then_inc(q_ss, 1)

            bits = list(range(31, -1, -1))
            tiles = list(range(T0, T))

            def background(n):
                for _ in range(n):
                    if bits:
                        topk_step(bits.pop(0))
                    elif tiles:
                        select(tiles.pop(0))

            for t in range(T):
                av_stats(t)
                if t == 0:
                    lo_qi(T - 1)
                    sum_heads(T - 2)
                if t == 1:
                    sum_heads(T - 1)
                    then(dve.memset(cand_f, 0.0))
                av_norm(t)
                if t > 1:
                    background(1)
                if t > 0:
                    gate(t - 1)
            gate(T - 1)
            for t in range(T):
                ya_square(t)
                background(1)
            for t in range(T):
                mix_a(t)
                background(1)
            for t in range(T):
                background(2 if bits else 1)
            for t in range(T):
                q_sums(t)
                background(1)
            assert not bits

            def lo_q(t):
                for odd in range(2):
                    dve.wait_ge(q_hi_done, 2 * t + odd + 1)
                    half = slice(HALF * odd, HALF * (odd + 1))
                    dve.scalar_tensor_tensor(
                        out=q_stack[t % 2][HALF:P, odd:H:2, :],
                        in0=ps_tp[tp_slot[("q", t)]][half, :].rearrange("p (h s) -> p h s", h=H // 2),
                        scalar=gq[half, 0:1], in1=q_stack[t % 2][0:HALF, odd:H:2, :].bitcast(F32),
                        op0=ALU.mult, op1=ALU.subtract).then_inc(q_lo_done, 1)

            def bias_max(t, h):
                m = head_no(t, h)
                dve.wait_ge(s_done, m + 1)
                if m >= 2:
                    dve.wait_ge(pT_done, m - 1)
                    if (m - 2) // H >= 4:
                        t2, h2 = divmod(m - 2, H)
                        dve.wait_ge(pT2_done, second_groups[t2] + h2 + 1)
                if t < T0:
                    d = negdist[:, S - keys(t):S]
                else:
                    if h == 0:
                        dve.wait_ge(mask_ready, t - T0 + 1)
                    d = score[:, sc_off[t]:sc_off[t] + keys(t)]
                dve.tensor_tensor_reduce(probs[:, m % 2, 0:keys(t)], ps_lg[m % 2][:, 0:keys(t)], d,
                                         -(2.0 ** -(h + 1)), BIG, ALU.add, ALU.min,
                                         negmax[:, t % 2, h:h + 1]).then_inc(max_done, 1)

            def copy_pT2(t, h):
                if t < 4:
                    return
                m = head_no(t, h)
                nb = t + 1 - 4
                dve.wait_ge(pT2_done, second_groups[t] + h + 1)
                dve.wait_ge(pv_done, m - 1)
                dve.tensor_copy(probsT[m % 2][:, 4:t + 1, :],
                                ps_tp[tp_slot[("p", t, h, 1)]][:, 0:P * nb].rearrange("p (b s) -> p b s", b=nb)
                                ).then_inc(pT_dve, 1)

            def y_rows(t):
                dve.wait_ge(exp_done, H * (t + 1))
                dve.reciprocal(rden[:, :], den[:, t % 2, :]).then_inc(rden_done, 1)
                dve.wait_ge(rden_done, t + 1)
                dve.wait_ge(pv_done, H * (t + 1))
                if t >= 2:
                    dve.wait_ge(mT_done, 2 * (t - 1))
                dve.tensor_tensor(yb[:, t % 2, :].rearrange("p (h d) -> p h d", h=H),
                                  ps_pv[:, :].rearrange("p (h d) -> p h d", h=H),
                                  rden[:, :].unsqueeze(2).broadcast_to([P, H, DH]),
                                  ALU.mult).then_inc(y_ready, 1)

            def y_sums(t):
                dve.wait_ge(y_sq, t + 1)
                dve.tensor_reduce(yss[:, :], ysq[:, :].rearrange("p (h d) -> p h d", h=H), AX.X,
                                  ALU.add).then_inc(y_ss, 1)

            def lo_mix(t):
                for g in range(2):
                    dve.wait_ge(m_hi_done, 2 * t + g + 1)
                    part = slice(4 * g, 4 * (g + 1))
                    dve.tensor_tensor(mixT_lo[t % 2][:, part, :],
                                      ps_tp[tp_slot[("m", t, g)]][:, :].rearrange("p (k s) -> p k s", k=4),
                                      mixT_hi[t % 2][:, part, :].bitcast(F32),
                                      ALU.subtract).then_inc(m_lo_done, 1)

            def add_res(t, n):
                dve.wait_ge(out_acc, 2 * t + n + 1)
                if n == 0:
                    dve.wait_ge(res_loaded[t % 2], 16 * (t // 2 + 1))
                half = res[:, t % 2, BANK * n:BANK * (n + 1)]
                dve.tensor_tensor(half, ps_out[:, :], half, ALU.add).then_inc(out_ready, 1)

            lo_q(0)
            bias_max(0, 0)
            bias_max(0, 1)
            for t in range(T):
                for h in range(H):
                    m = head_no(t, h)
                    copy_pT2(t, h)
                    if h == 0 and t > 0:
                        y_rows(t - 1)
                        y_sums(t - 1)
                    if h == 1 and t > 0:
                        lo_mix(t - 1)
                    if h == 4 and t + 1 < T:
                        lo_q(t + 1)
                    if m + 2 < T * H:
                        bias_max(*divmod(m + 2, H))
                    if h == 3 and t > 0:
                        add_res(t - 1, 0)
                    if h == 5 and t > 0:
                        add_res(t - 1, 1)
            y_rows(T - 1)
            y_sums(T - 1)
            lo_mix(T - 1)
            add_res(T - 1, 0)
            add_res(T - 1, 1)


_INS = ["x", "norm_gain", "w_in", "sgu_norm_gain", "sgu_w", "sgu_b", "q_norm_gain", "k_norm_gain",
        "idx_k_norm_gain", "branch_norm_gain", "w_out"]
_OUTS = [((1, 1024, 1024), "float32")]


def kernel(**inputs):
    import numpy as _np
    import concourse.bacc as _bacc
    from concourse import mybir as _mybir
    from concourse.bass_utils import run_bass_kernel_spmd as _run

    nc = _bacc.Bacc("TRN2", target_bir_lowering=False, num_devices=1)
    arrays, args = {}, []
    for name in _INS:
        a = _np.ascontiguousarray(inputs[name])
        arrays[f"in_{name}_dram"] = a
        args.append(nc.dram_tensor(f"in_{name}_dram", a.shape, _mybir.dt.from_np(a.dtype), kind="ExternalInput").ap())
    for i, (shape, dtype) in enumerate(_OUTS):
        dt = _mybir.dt.from_np(_np.dtype(dtype))
        args.append(nc.dram_tensor(f"out_{i}_dram", shape, dt, kind="ExternalOutput").ap())
    hybrid_block(nc, *args)
    r = _run(nc, [arrays], core_ids=[0])
    got = tuple(r.results[0][f"out_{i}_dram"] for i in range(len(_OUTS)))
    return got[0]
```

```python
from contextlib import ExitStack

import concourse.bass as bass
from concourse import mybir

F32 = mybir.dt.float32
F32R = mybir.dt.float32r
F16 = mybir.dt.float16
BF16 = mybir.dt.bfloat16
I32 = mybir.dt.int32
I8 = mybir.dt.int8
ALU = mybir.AluOpType
ACT = mybir.ActivationFunctionType
AX = mybir.AxisListType

P = 128
HALF = 64
BANK = 512
TOPK = 256
NEG = -1e30
EPS = 1e-6
BIG = 3.0e38


def hybrid_block(nc, x, norm_gain, w_in, sgu_norm_gain, sgu_w, sgu_b, q_norm_gain, k_norm_gain,
                 idx_k_norm_gain, branch_norm_gain, w_out, out):
    _, S, D = x.shape
    T = S // P
    KB = D // P
    G = sgu_w.shape[1]
    H = 8
    DH = q_norm_gain.shape[1]
    A_W = G * P
    B_W = H * DH
    T0 = TOPK // P
    IDX_SCALE = (H ** -0.5) * (DH ** -0.5)
    assert (S, D, G, DH, A_W, B_W) == (1024, 1024, 4, 64, 512, 512)

    o_au, o_av, o_az, o_bq = 0, A_W, 2 * A_W, 3 * A_W
    o_bk = o_bq + B_W
    o_bz = o_bk + 2 * DH
    o_iq = o_bz + B_W
    o_ik = o_iq + H * DH
    NKV = 2 * DH
    NIK = DH + H
    N0 = NKV + NIK
    KVI, IQ, BQ, AV, AU, AZ, BZ, O1, O2 = range(9)
    chunk_src = {IQ: o_iq, AV: o_av, AU: o_au, AZ: o_az, BZ: o_bz, BQ: o_bq}

    def unit(c, t):
        return t if c == KVI else T * c + t - T0

    UNITS = unit(BZ, T - 1) + 1

    def keys(t):
        return P * (t + 1)

    ROUNDS_FROM = 2
    SPLIT = 5
    sc_off = {t: sum(keys(s) for s in range(T0, t)) for t in range(T0, T)}
    SC_COLS = sum(keys(t) for t in range(T0, T))

    ctx = ExitStack()
    with ctx:
        def psum(name, shape):
            return ctx.enter_context(nc.psum_tensor(name, shape, F32))

        def sem(name):
            return ctx.enter_context(nc.semaphore(name))

        base = (nc.sbuf_base + 63) // 64 * 64
        size_of = {F32: 4, F32R: 4, I32: 4, F16: 2, BF16: 2, I8: 1}
        top = [base]

        def place(name, shape, dt, at=None):
            n = size_of[dt]
            for s in shape[1:]:
                n *= s
            where = top[0] if at is None else at
            if at is None:
                top[0] = where + (n + 31) // 32 * 32
                assert top[0] <= nc.sbuf_usable_end, (name, top[0] - nc.sbuf_usable_end)
            return nc.alloc_sbuf_tensor_at(name, shape, dt, offset=where)

        w_hi = [place(f"w_hi{i}", [P, KB, BANK], F32R) for i in range(2)]
        w_lo = [place(f"w_lo{i}", [P, KB, BANK], F32R) for i in range(2)]
        NSTAGE = 3
        stage = place("stage", [P, NSTAGE, BANK], F32)
        mixT_hi = place("mixT_hi", [P, KB, P], F32R, at=top[0] - 4 * NSTAGE * BANK)
        zone_x = top[0]
        xT_hi = place("xT_hi", [P, KB, S], F32R)
        xT_lo = place("xT_lo", [P, KB, S], F32R)
        end_x = top[0]
        cur = [zone_x]

        def place_x(name, shape, dt):
            n = size_of[dt]
            for s in shape[1:]:
                n *= s
            t = place(name, shape, dt, at=cur[0])
            cur[0] += (n + 31) // 32 * 32
            assert cur[0] <= end_x, name
            return t

        q_stack = [place_x(f"q_stack{i}", [P, H, P], F32R) for i in range(2)]
        probs = place_x("probs", [P, 2, S], F32)
        probsT_hi = place_x("probsT_hi", [P, T, 4, P], F32R)
        probsT_lo = place_x("probsT_lo", [P, T, 4, P], F32R)
        z_in = place_x("z_in", [P, 2, B_W], F32)
        mixT_lo = place_x("mixT_lo", [P, KB, P], F32R)
        yb = place_x("yb", [P, 2, B_W], F32)
        res = place_x("res", [P, D], F32)
        zone_y = top[0]
        y_a = place("y_a", [P, T, A_W], F32)
        x_in = place("x_in", [P, 4, D], F32, at=zone_y)
        qi_stack = [place(f"qi_stack{i}", [P, H, P], F32R, at=zone_y + 4096 * i) for i in range(2)]
        relu_sb = place("relu_sb", [P, 2, S], F32, at=zone_y + 8192)
        zone_s = top[0]
        score = place("score", [P, SC_COLS], F32)
        kvi_raw = place("kvi_raw", [P, KB, N0], F32, at=zone_s)
        dist_i = place("dist_i", [P, S], I32, at=zone_s + 4 * KB * N0)
        sgu_raw = place("sgu_raw", [P, G, P], F32, at=zone_s + 4 * (KB * N0 + S))
        assert KB * N0 + S + G * P <= SC_COLS
        k_hh = place("k_hh", [P, S], F32R)
        k_ll = place("k_ll", [P, S], F32R)
        ki_hh = place("ki_hh", [P, S], F32R)
        ki_ll = place("ki_ll", [P, S], F32R)
        v_hl = place("v_hl", [P, T, 2 * DH], F32R)
        negdist = place("negdist", [P, S], F16)
        near = place("near", [P, TOPK], F32)
        ident = place("ident", [P, P], F32)
        fold = place("fold", [P, DH], F32)
        nat = place("nat", [P, 2, BANK], F32)
        ysq = place("ysq", [P, B_W], F32, at=top[0] - 8 * BANK)
        yz = place("yz", [P, B_W], F32, at=top[0] - 4 * BANK)
        zone_k = top[0]
        kvi = place("kvi", [P, 2, N0], F32)
        khat = place("khat", [P, 2, 2, DH], F32)
        q_sq_tmp = place("q_sq_tmp", [P, B_W], F32, at=zone_k)[:, :]
        assert zone_k + 4 * B_W <= top[0]
        yT = place("yT", [P, 4, P], F32, at=top[0])
        wT_sgu = place("wT_sgu", [P, G, P], F32)
        q_in = [place("q_in0", [P, B_W], F32, at=zone_k), place("q_in1", [P, B_W], F32, at=top[0])]
        vg_row = place("vg_row", [P, A_W], F32)
        gt = place("gt", [P, S], I8)
        eq = place("eq", [P, S], I8)
        x_sq = place("x_sq", [P, S], BF16, at=top[0])
        rank = place("rank", [P, S], F16)
        g_in = place("g_in", [P, KB], F32)
        g_out = place("g_out", [P, KB], F32)
        gq = place("gq", [P, 1], F32)
        gk = place("gk", [P, 1], F32)
        gik = place("gik", [P, 1], F32)
        bias_s = place("bias_s", [P, G], F32)
        q_scale = place("q_scale", [P, H], F32)
        nhalf = place("nhalf", [P, H], F32)
        ss_x = place("ss_x", [P, T], F32)
        rstd_x = place("rstd_x", [P, T], F32)
        kstat = place("kstat", [P, 2, 4], F32)
        krstd = place("krstd", [P, 2, 2], F32)
        idx_w = place("idx_w", [P, T, H], F32)
        bn6 = place("bn6", [P, G, 6], F32)
        vstat = place("vstat", [P, G, 2], F32)
        vrstd = place("vrstd", [P, G], F32)
        ya_ms = place("ya_ms", [P, T, G], F32)
        ya_r = place("ya_r", [P, T, G], F32)
        cnt = place("cnt", [P, T], F32)
        sign_sum = place("sign_sum", [P, T - SPLIT], F32)
        succ = place("succ", [P, T], I32)
        delta = place("delta", [P, T], I32)
        cand = place("cand", [P, T], I32)
        room = place("room", [P, T], F32)
        qss = place("qss", [P, H], F32)
        qr = place("qr", [P, H], F32)
        negmax = place("negmax", [P, 2, H], F32)
        den = place("den", [P, 2, H], F32)
        rden = place("rden", [P, H], F32)
        yss = place("yss", [P, H], F32)
        yr = place("yr", [P, H], F32)
        bn_tmp = place("bn_tmp", [P, DH], F32)[:, :]
        ya_tmp = wT_sgu
        CONSTS = 16 * 9

        ps_proj = [psum(f"ps_proj{i}", [P, BANK]) for i in range(2)]
        ps_tp = [psum(f"ps_tp{i}", [P, BANK]) for i in range(2)]
        ps_lg = [psum(f"ps_lg{i}", [P, S]) for i in range(2)]
        ps_out, ps_pv = ps_proj

        q_dram = nc.dram_tensor("q_scratch", (S, B_W), F32, kind="Internal").ap()
        z_dram = nc.dram_tensor("z_scratch", (S, B_W), F32, kind="Internal").ap()

        x_loaded = [sem(f"x_loaded{i}") for i in range(4)]
        kvi_loaded = sem("kvi_loaded")
        stage_loaded = [sem(f"stage_loaded{i}") for i in range(NSTAGE)]
        g_in_loaded = sem("g_in_loaded")
        consts_loaded = sem("consts_loaded")
        sgu_loaded = sem("sgu_loaded")
        setup_step = sem("setup_step")
        ident_ready = sem("ident_ready")
        dist_ready = sem("dist_ready")
        w_scaled = sem("w_scaled")
        w_hi_done = sem("w_hi_done")
        w_lo_done = sem("w_lo_done")
        xT_done = sem("xT_done")
        ss_done = sem("ss_done")
        ms_ready = sem("ms_ready")
        rstd_ready = sem("rstd_ready")
        x_hi_done = sem("x_hi_done")
        x_lo_done = sem("x_lo_done")
        proj_done = sem("proj_done")
        proj_evac = sem("proj_evac")
        kstat_done = sem("kstat_done")
        kms_ready = sem("kms_ready")
        krstd_done = sem("krstd_done")
        khat_done = sem("khat_done")
        kvi_used = sem("kvi_used")
        kT_done = sem("kT_done")
        k_hi_done = sem("k_hi_done")
        k_lo_done = sem("k_lo_done")
        sguT_done = sem("sguT_done")
        sguT_copied = sem("sguT_copied")
        qiT_done = sem("qiT_done")
        qi_hi_done = sem("qi_hi_done")
        qi_lo_done = sem("qi_lo_done")
        logits_done = sem("logits_done")
        relu_done = sem("relu_done")
        score_acc = sem("score_acc")
        vstat_done = sem("vstat_done")
        veps_done = sem("veps_done")
        vrstd_done = sem("vrstd_done")
        vhat_done = sem("vhat_done")
        vgain_done = sem("vgain_done")
        sgu_done = sem("sgu_done")
        gate_ready = sem("gate_ready")
        ya_done = sem("ya_done")
        ya_ms_done = sem("ya_ms_done")
        ya_eps_done = sem("ya_eps_done")
        ya_r_done = sem("ya_r_done")
        mixA_done = sem("mixA_done")
        dve_step = sem("dve_step")
        z_stored = [sem(f"z_stored{i}") for i in range(2)]
        q_stored = [sem(f"q_stored{i}") for i in range(2)]
        q_sq = sem("q_sq")
        q_ss = sem("q_ss")
        q_step = sem("q_step")
        q_normed = sem("q_normed")
        mask_ready = sem("mask_ready")
        q_loaded = [sem(f"q_loaded{i}") for i in range(2)]
        z_loaded = [sem(f"z_loaded{i}") for i in range(2)]
        res_loaded = sem("res_loaded")
        qT_done = sem("qT_done")
        q_hi_done = sem("q_hi_done")
        q_lo_done = sem("q_lo_done")
        s_done = sem("s_done")
        max_done = sem("max_done")
        exp_done = sem("exp_done")
        pT_done = sem("pT_done")
        act_counted = sem("act_counted")
        cand_ready = sem("cand_ready")
        succ_wanted = sem("succ_wanted")
        succ_ready = sem("succ_ready")
        fold_ready = sem("fold_ready")
        yT_copied = sem("yT_copied")
        yT_done = sem("yT_done")
        y_half = sem("y_half")
        y_gated = sem("y_gated")
        tile_counted = sem("tile_counted")
        sguT_masked = sem("sguT_masked")
        pT_hi_done = sem("pT_hi_done")
        pT_lo_done = sem("pT_lo_done")
        pv_done = sem("pv_done")
        rden_done = sem("rden_done")
        y_sq = sem("y_sq")
        y_ss = sem("y_ss")
        y_step = sem("y_step")
        mixB_done = sem("mixB_done")
        mT_done = sem("mT_done")
        m_hi_done = sem("m_hi_done")
        m_lo_done = sem("m_lo_done")
        out_acc = sem("out_acc")
        out_ready = sem("out_ready")
        out_stored = sem("out_stored")

        tp_plan = []
        for t in range(T):
            tp_plan.append(("k", t))
        tp_plan.append(("w", 0))
        for t in range(T0, T):
            tp_plan.append(("qi", t))
        for t in range(T):
            tp_plan.append(("sgu", t))
        Q_AT, MIX_AT, YT_AT = 2, 6, (5, 1)
        for t in range(T):
            if t == 0:
                tp_plan.append(("q", 0))
            for h in range(H):
                if h == YT_AT[0]:
                    tp_plan.append(("y", t, 0))
                if h == YT_AT[1] and t > 0:
                    tp_plan.append(("y", t - 1, 1))
                if h == MIX_AT and t > 0:
                    tp_plan += [("m", t - 1, 0), ("m", t - 1, 1)]
                if h == Q_AT and t + 1 < T:
                    tp_plan.append(("q", t + 1))
                tp_plan += [("p", t, h, g) for g in range(1 + (t >= 4))]
        tp_plan += [("y", T - 1, 1), ("m", T - 1, 0), ("m", T - 1, 1)]
        tp_slot = {key: n % 2 for n, key in enumerate(tp_plan)}

        def head_no(t, h):
            return H * t + h

        groups_before = {t: H * t + H * max(0, t - 4) for t in range(T + 1)}

        def last_group(m):
            t, h = divmod(m, H)
            return t, h, int(t >= 4)

        def group_no(t, h, g):
            return groups_before[t] + h * (1 + (t >= 4)) + g

        def tp_release(key):
            kind = key[0]
            if kind == "k":
                return k_lo_done, key[1] + 1
            if kind == "w":
                return sguT_copied, 1
            if kind == "qi":
                return qi_lo_done, 2 * (key[1] - T0) + 2
            if kind == "sgu":
                return gate_ready, key[1] + 1
            if kind == "q":
                return q_lo_done, 2 * key[1] + 2
            if kind == "m":
                return m_lo_done, 2 * key[1] + key[2] + 1
            if kind == "y":
                return y_half, 2 * key[1] + key[2] + 1
            return pT_lo_done, group_no(*key[1:]) + 1

        block = ctx.enter_context(nc.Block())

        @block.sync
        def _(sp):
            def load_x(t):
                if t >= 4:
                    sp.wait_ge(xT_done, t - 3)
                    sp.wait_ge(ss_done, t - 3)
                sp.dma_start(x_in[:, t % 4, :], x[0, P * t:P * (t + 1), :]).then_inc(x_loaded[t % 4], 16)

            def load_w(c, k):
                n = KB * (c - 1) + k
                if n >= NSTAGE:
                    sp.wait_ge(w_lo_done, KB + n - NSTAGE + 1)
                if c < O1:
                    src = w_in[0, P * k:P * (k + 1), chunk_src[c]:chunk_src[c] + BANK]
                else:
                    src = w_out[0, P * k:P * (k + 1), BANK * (c - O1):BANK * (c - O1 + 1)]
                sp.dma_start(stage[:, n % NSTAGE, :], src).then_inc(stage_loaded[n % NSTAGE], 16)

            def rows(t):
                return slice(P * t, P * (t + 1))

            def load_q(t):
                if t >= 2:
                    sp.wait_ge(qT_done, t - 1)
                sp.dma_start(q_in[t % 2][:, :], q_dram[rows(t), :]).then_inc(q_loaded[t % 2], 16)

            load_x(0)
            w_rows = w_in[0].rearrange("(k p) n -> p k n", p=P)
            sp.dma_start(kvi_raw[:, :, 0:NKV], w_rows[:, :, o_bk:o_bk + NKV]).then_inc(kvi_loaded, 16)
            sp.dma_start(kvi_raw[:, :, NKV:N0], w_rows[:, :, o_ik:o_ik + NIK]).then_inc(kvi_loaded, 16)
            load_x(1)
            load_x(2)
            col = lambda v, n: v.rearrange("(k p) -> p k", p=n)
            with nc.allow_non_contiguous_dma(reason="gains as columns, a few KiB"):
                for dst, src in ((gk, k_norm_gain), (gik, idx_k_norm_gain), (gq, q_norm_gain)):
                    for half in range(2):
                        sp.dma_start(dst[DH * half:DH * (half + 1), :],
                                     col(src[0], DH)).then_inc(consts_loaded, 16)
            load_x(3)
            load_w(IQ, 0)
            with nc.allow_non_contiguous_dma(reason="gains as columns, a few KiB"):
                sp.dma_start(g_out[:, :], col(branch_norm_gain[0], P)).then_inc(consts_loaded, 16)
                sp.dma_start(bias_s[:, :], sgu_b[0].rearrange("g i -> i g")).then_inc(consts_loaded, 16)
            sp.dma_start(vg_row[:, :], sgu_norm_gain[0].partition_broadcast(P)).then_inc(consts_loaded, 16)
            sp.dma_start(sgu_raw[:, :, :], sgu_w[0].rearrange("g i j -> i g j")).then_inc(sgu_loaded, 16)
            for t in range(4, T):
                load_x(t)
                if 0 < t - 4 < NSTAGE:
                    load_w(IQ, t - 4)
            for k in range(NSTAGE, KB):
                load_w(IQ, k)
            for k in range(KB):
                load_w(BQ, k)

            def store_z(t):
                sp.wait_ge(proj_evac, unit(BZ, t) + 1)
                sp.dma_start(z_dram[P * t:P * (t + 1), :],
                             nat[:, unit(BZ, t) % 2, :]).then_inc(z_stored[t % 2], 16)

            def store_q(t):
                sp.wait_ge(q_normed, t + 1)
                sp.dma_start(q_dram[P * t:P * (t + 1), :],
                             nat[:, unit(BQ, t) % 2, :]).then_inc(q_stored[t % 2], 16)

            for t in range(T):
                if t == 0:
                    for k in range(NSTAGE):
                        load_w(AV, k)
                elif t + NSTAGE - 1 < KB:
                    load_w(AV, t + NSTAGE - 1)
                store_q(t)
            for c in (AU, AZ, BZ):
                for k in range(KB):
                    load_w(c, k)
                if c == AZ:
                    for i in range(2):
                        sp.wait_ge(q_stored[i], 16 * T // 2)
                    sp.wait_ge(vgain_done, T)
                    for t in range(2):
                        load_q(t)
            for t in range(T):
                if t == 0:
                    for k in range(NSTAGE):
                        load_w(O1, k)
                elif t + NSTAGE - 1 < KB:
                    load_w(O1, t + NSTAGE - 1)
                store_z(t)

            def load_z(t):
                if t >= 2:
                    sp.wait_ge(y_gated, t - 1)
                sp.dma_start(z_in[:, t % 2, :], z_dram[rows(t), :]).then_inc(z_loaded[t % 2], 16)

            def load_res(t):
                if t >= 1:
                    sp.wait_ge(out_stored, 16 * t)
                sp.dma_start(res[:, :], x[0, rows(t), :]).then_inc(res_loaded, 16)

            def store_out(t):
                sp.wait_ge(out_ready, 2 * (t + 1))
                sp.dma_start(out[0, P * t:P * (t + 1), :], res[:, :]).then_inc(out_stored, 16)

            for k in range(NSTAGE):
                load_w(O2, k)
            for i in range(2):
                sp.wait_ge(z_stored[i], 16 * T // 2)
            sp.wait_ge(proj_done, UNITS)
            for t in range(2):
                load_z(t)
            load_res(0)
            for k in range(NSTAGE, KB):
                load_w(O2, k)
            for t in range(T + 2):
                if t + 2 < T:
                    load_q(t + 2)
                if 2 <= t + 1 < T:
                    load_z(t + 1)
                if t >= 2:
                    store_out(t - 2)
                if 1 <= t - 1 < T:
                    load_res(t - 1)
            sp.wait_ge(out_stored, 16 * T)

        @block.gpsimd
        def _(pool):
            pool.memset(ident[:, :], 0.0).then_inc(setup_step, 1)
            pool.wait_ge(setup_step, 1)
            pool.affine_select(out=ident[:, :], in_=ident[:, :], compare_op=ALU.not_equal, fill=1.0, base=0,
                               pattern=[[-1, P]], channel_multiplier=1).then_inc(ident_ready, 1)
            pool.wait_ge(ident_ready, 1)
            pool.tensor_tensor(fold[:, :], ident[:, 0:DH], ident[:, DH:P], ALU.add).then_inc(fold_ready, 1)
            pool.memset(nhalf[:, :], -0.5).then_inc(setup_step, 1)
            for h in range(H):
                pool.memset(q_scale[:, h:h + 1], (DH ** -0.5) * 2.0 ** (h + 1)).then_inc(setup_step, 1)
            pool.wait_ge(setup_step, 2 + H)

            pool.iota(dist_i[:, :], pattern=[[-1, S]], base=S - P,
                      channel_multiplier=1).then_inc(dist_ready, 1)

            def w_block(n):
                c, k = divmod(n, KB)
                if c == KVI:
                    return kvi_raw[:, k, :], w_hi[0][:, k, 0:N0], w_lo[0][:, k, 0:N0], k
                return stage[:, (n - KB) % NSTAGE, :], w_hi[c % 2][:, k, :], w_lo[c % 2][:, k, :], k

            def scale_w(n):
                raw, _, _, k = w_block(n)
                if n < KB:
                    if n == 0:
                        pool.wait_ge(kvi_loaded, 32)
                        pool.wait_ge(g_in_loaded, 16)
                else:
                    m = n - KB
                    pool.wait_ge(stage_loaded[m % NSTAGE], 16 * (m // NSTAGE + 1))
                if n == KB * O1:
                    pool.wait_ge(consts_loaded, CONSTS)
                gain = g_in if n < KB * O1 else g_out
                pool.tensor_scalar(raw, raw, gain[:, k:k + 1], 1.0, ALU.mult, ALU.mult).then_inc(w_scaled, 1)

            def split_w(n):
                raw, hi, lo, _ = w_block(n)
                pool.wait_ge(w_hi_done, n + 1)
                pool.tensor_tensor(lo, raw, hi.bitcast(F32), ALU.subtract).then_inc(w_lo_done, 1)

            def rstd_rows(t):
                pool.wait_ge(ss_done, t + 1)
                pool.tensor_scalar(rstd_x[:, t:t + 1], ss_x[:, t:t + 1], 1.0 / D, EPS, ALU.mult,
                                   ALU.add).then_inc(ms_ready, 1)
                pool.wait_ge(ms_ready, t + 1)
                pool.tensor_tensor(rstd_x[:, t:t + 1], rstd_x[:, t:t + 1], nhalf[:, 0:1],
                                   ALU.pow).then_inc(rstd_ready, 1)

            def k_rows(t):
                rows = kvi[:, t % 2, :]
                pool.wait_ge(proj_evac, unit(KVI, t) + 1)
                pool.tensor_copy(v_hl[:, t, 0:DH], rows[:, DH:NKV]).then_inc(kvi_used, 1)
                pool.tensor_scalar(idx_w[:, t, :], rows[:, NKV + DH:N0], IDX_SCALE, 1.0,
                                   ALU.mult, ALU.mult).then_inc(kvi_used, 1)
                pool.wait_ge(kvi_used, 3 * t + 1)
                pool.tensor_tensor(v_hl[:, t, DH:2 * DH], rows[:, DH:NKV], v_hl[:, t, 0:DH].bitcast(F32),
                                   ALU.subtract).then_inc(kvi_used, 1)
                pool.wait_ge(kstat_done, 2 * (t + 1))
                pool.tensor_scalar(krstd[:, t % 2, :], kstat[:, t % 2, 1:3], EPS, 1.0,
                                   ALU.add, ALU.mult).then_inc(kms_ready, 1)
                pool.wait_ge(kms_ready, t + 1)
                pool.tensor_tensor(krstd[:, t % 2, :], krstd[:, t % 2, :], nhalf[:, 0:2],
                                   ALU.pow).then_inc(krstd_done, 1)

            for n in range(KB):
                scale_w(n)
            rstd_rows(0)
            pool.wait_ge(dist_ready, 2)
            pool.memset(near[0:HALF, TOPK - HALF:TOPK], NEG).then_inc(dist_ready, 1)
            for t in range(T):
                if t + 1 < T:
                    rstd_rows(t + 1)
                scale_w(KB + t)
                k_rows(t)
            pool.wait_ge(w_lo_done, 2 * KB)

            def next_block(c, t):
                scale_w(KB * (c + 1) + t)
                split_w(KB * (c + 1) + t)

            for t in range(T0, T):
                next_block(IQ, t - T0)
            next_block(IQ, KB - 2)
            next_block(IQ, KB - 1)

            def av(t):
                pool.wait_ge(vstat_done, t + 1)
                pool.tensor_scalar(vrstd[:, :], vstat[:, :, 1], EPS, 1.0, ALU.add, ALU.mult).then_inc(veps_done, 1)
                pool.wait_ge(veps_done, t + 1)
                pool.tensor_tensor(vrstd[:, :], vrstd[:, :], nhalf[:, 0:G], ALU.pow).then_inc(vrstd_done, 1)

            def au(t):
                pool.wait_ge(proj_evac, unit(AU, t) + 1)
                pool.wait_ge(gate_ready, t + 1)
                pool.tensor_tensor(y_a[:, t, :], y_a[:, t, :], nat[:, unit(AU, t) % 2, :],
                                   ALU.mult).then_inc(ya_done, 1)

            def au_r(t):
                pool.wait_ge(ya_ms_done, t + 1)
                pool.tensor_scalar(ya_r[:, t, :], ya_ms[:, t, :], EPS, 1.0, ALU.add, ALU.mult).then_inc(ya_eps_done, 1)
                pool.wait_ge(ya_eps_done, t + 1)
                pool.tensor_tensor(ya_r[:, t, :], ya_r[:, t, :], nhalf[:, 0:G], ALU.pow).then_inc(ya_r_done, 1)

            def bq(t):
                rows = nat[:, unit(BQ, t) % 2, :]
                heads = rows.rearrange("p (h d) -> p h d", h=H)
                pool.wait_ge(proj_evac, unit(BQ, t) + 1)
                pool.wait_ge(q_ss, t + 1)
                pool.tensor_scalar(qr[:, :], qss[:, :], 1.0 / DH, EPS, ALU.mult, ALU.add).then_inc(q_step, 1)
                pool.wait_ge(q_step, 3 * t + 1)
                pool.tensor_tensor(qr[:, :], qr[:, :], nhalf[:, :], ALU.pow).then_inc(q_step, 1)
                pool.wait_ge(q_step, 3 * t + 2)
                pool.tensor_tensor(qr[:, :], qr[:, :], q_scale[:, :], ALU.mult).then_inc(q_step, 1)
                pool.wait_ge(q_step, 3 * t + 3)
                pool.tensor_tensor(heads, heads, qr[:, :].unsqueeze(2).broadcast_to([P, H, DH]),
                                   ALU.mult).then_inc(q_normed, 1)

            scale_w(KB * AV)
            for t in range(T):
                bq(t)
                split_w(KB * AV + t)
                scale_w(KB * AV + t + 1)
            for t in range(T):
                av(t)
                split_w(KB * AU + t)
                scale_w(KB * AU + t + 1)
            for t in range(T):
                split_w(KB * AZ + t)
                scale_w(KB * AZ + t + 1)
                au(t)
                if t > 0:
                    au_r(t - 1)
            au_r(T - 1)
            for c in (BZ, O1):
                for t in range(T):
                    split_w(KB * c + t)
                    scale_w(KB * c + t + 1)
                    if (c, t) == (O1, ROUNDS_FROM + 1):
                        pool.wait_ge(succ_wanted, 1)
                        pool.tensor_tensor(succ[:, SPLIT:T], cand[:, SPLIT:T], delta[:, SPLIT:T],
                                           ALU.add).then_inc(succ_ready, 1)

            def finish_b(t):
                pool.wait_ge(y_half, 2 * (t + 1))
                pool.wait_ge(z_loaded[t % 2], 16 * (t // 2 + 1))
                if t >= 1:
                    pool.wait_ge(mixB_done, t)
                pool.tensor_tensor(yz[:, :], yb[:, t % 2, :], z_in[:, t % 2, :], ALU.mult).then_inc(y_gated, 1)
                pool.wait_ge(y_ss, t + 1)
                pool.tensor_scalar(yr[:, :], yss[:, :], 1.0 / DH, EPS, ALU.mult, ALU.add).then_inc(y_step, 1)
                pool.wait_ge(y_step, 2 * t + 1)
                pool.tensor_tensor(yr[:, :], yr[:, :], nhalf[:, :], ALU.pow).then_inc(y_step, 1)

            for k in range(KB):
                split_w(KB * O2 + k)
                if k + 1 < KB:
                    scale_w(KB * O2 + k + 1)
            for t in range(T):
                finish_b(t)

        @block.scalar
        def _(act):
            with nc.allow_non_contiguous_dma(reason="a gain as columns, 4 KiB"):
                act.dma_start(g_in[:, :], norm_gain[0].rearrange("(k p) -> p k", p=P)).then_inc(g_in_loaded, 16)

            def hi_w(n):
                c, k = divmod(n, KB)
                act.wait_ge(w_scaled, n + 1)
                if k == 0 and c >= 2:
                    act.wait_ge(proj_done, T if c == 2 else unit(c - 1, 0))
                if c == KVI:
                    act.copy(w_hi[0][:, k, 0:N0], kvi_raw[:, k, :]).then_inc(w_hi_done, 1)
                else:
                    act.copy(w_hi[c % 2][:, k, :], stage[:, (n - KB) % NSTAGE, :]).then_inc(w_hi_done, 1)

            def square_x(t):
                act.wait_ge(x_loaded[t % 4], 16 * (t // 4 + 1))
                if t > 0:
                    act.wait_ge(ss_done, t)
                act.activation(x_sq[:, :], x_in[:, t % 4, :], ACT.Square,
                               accum_out=ss_x[:, t:t + 1]).then_inc(ss_done, 1)

            def hi_x(t):
                act.wait_ge(xT_done, t + 1)
                act.copy(xT_hi[:, :, P * t:P * (t + 1)],
                         ps_lg[t % 2][:, :].rearrange("p (k s) -> p k s", k=KB)).then_inc(x_hi_done, 1)

            def evac_kvi(t):
                u = unit(KVI, t)
                act.wait_ge(proj_done, u + 1)
                act.wait_ge(rstd_ready, t + 1)
                if t >= 2:
                    act.wait_ge(kvi_used, 3 * (t - 1))
                    act.wait_ge(khat_done, 2 * (t - 1))
                act.activation(kvi[:, t % 2, :], ps_proj[u % 2][:, 0:N0], ACT.Copy,
                               scale=rstd_x[:, t:t + 1]).then_inc(proj_evac, 1)

            def hi_k(t):
                act.wait_ge(kT_done, t + 1)
                if t == 0:
                    act.wait_ge(consts_loaded, CONSTS)
                slot = ps_tp[tp_slot[("k", t)]]
                act.activation(k_hh[:, P * t:P * (t + 1)], slot[:, 0:P], ACT.Copy,
                               scale=gk[:, 0:1]).then_inc(k_hi_done, 1)
                act.activation(ki_hh[:, P * t:P * (t + 1)], slot[:, P:2 * P], ACT.Copy,
                               scale=gik[:, 0:1]).then_inc(k_hi_done, 1)

            hi_x(0)
            for k in range(4):
                hi_w(k)
            square_x(0)
            for k in range(4, KB):
                hi_w(k)
            hi_x(1)
            square_x(1)
            for t in range(T):
                evac_kvi(t)
                if t + 2 < T:
                    hi_x(t + 2)
                    square_x(t + 2)
                hi_w(KB + t)
                if t > 0:
                    hi_k(t - 1)

            nat_free = {
                IQ: lambda t: (qiT_done, t - T0 + 1),
                AV: lambda t: (sgu_done, t + 1),
                AU: lambda t: (ya_done, t + 1),
                AZ: lambda t: (mixA_done, t + 1),
                BZ: lambda t: (z_stored[t % 2], 16 * (t // 2 + 1)),
                BQ: lambda t: (q_stored[t % 2], 16 * (t // 2 + 1)),
            }
            order = [(IQ, t) for t in range(T0, T)] + [(c, t) for c in (BQ, AV, AU, AZ, BZ) for t in range(T)]
            func = {IQ: ACT.Copy, AV: ACT.Gelu_apprx_tanh, AU: ACT.Gelu_apprx_tanh, AZ: ACT.Silu,
                    BZ: ACT.Silu, BQ: ACT.Copy}

            def evac(c, t):
                u = unit(c, t)
                act.wait_ge(proj_done, u + 1)
                i = order.index((c, t))
                if i >= 2:
                    pc, pt = order[i - 2]
                    act.wait_ge(*nat_free[pc](pt))
                if c == BQ:
                    if t == 0:
                        act.wait_ge(kT_done, T)
                    else:
                        act.wait_ge(q_ss, t)
                    act.activation(q_sq_tmp, ps_proj[u % 2][:, :], ACT.Square,
                                   scale=rstd_x[:, t:t + 1]).then_inc(q_sq, 1)
                act.activation(nat[:, u % 2, :], ps_proj[u % 2][:, :], func[c],
                               scale=rstd_x[:, t:t + 1]).then_inc(proj_evac, 1)

            def hi_qi(t):
                if t >= T0 + 2:
                    act.wait_ge(logits_done, H * (t - T0 - 1))
                act.wait_ge(qiT_done, t - T0 + 1)
                for odd in range(2):
                    bank = ps_tp[tp_slot[("qi", t)]][HALF * odd:HALF * (odd + 1), :]
                    act.copy(qi_stack[t % 2][0:HALF, odd:H:2, :],
                             bank.rearrange("p (h s) -> p h s", h=H // 2)).then_inc(qi_hi_done, 1)

            def relus(t):
                for h in range(H):
                    if h == 2 and t + 1 < T:
                        hi_qi(t + 1)
                    m = H * (t - T0) + h
                    act.wait_ge(logits_done, m + 1)
                    if m >= 2:
                        act.wait_ge(score_acc, m - 1)
                    act.activation(relu_sb[:, m % 2, 0:keys(t)], ps_lg[m % 2][:, 0:keys(t)],
                                   ACT.Relu).then_inc(relu_done, 1)

            for t in range(T0, T):
                if t == T0 + 1:
                    hi_qi(T0)
                if t > T0 + 1:
                    relus(t - 2)
                evac(IQ, t)
                if t == T0:
                    hi_k(T - 1)
                    act.wait_ge(sguT_done, 1)
                    act.copy(wT_sgu[:, :, :], ps_tp[tp_slot[("w", 0)]][:, :].rearrange(
                        "p (g i) -> p g i", g=G)).then_inc(sguT_copied, 1)
                if t - T0 < 3:
                    hi_w(KB * BQ + t - T0)
                if t > T0 + 1:
                    hi_w(KB * BQ + t - T0 + 1)
            hi_w(KB * BQ + 7)

            def w_and(c, t):
                hi_w(KB * (c + 1) + t)

            counts = T - SPLIT

            def count_round(r):
                act.wait_ge(cand_ready, r + 1)
                for i, t in enumerate(range(SPLIT, T)):
                    if i == 2:
                        act.wait_ge(act_counted, counts * r + 1)
                    act.activation(ps_lg[i % 2][:, 0:keys(t)], score[:, sc_off[t]:sc_off[t] + keys(t)], ACT.Sign,
                                   bias=cand[:, t:t + 1].bitcast(F32), scale=-1.0,
                                   accum_out=sign_sum[:, i:i + 1]).then_inc(act_counted, 1)

            def v_scale(t):
                act.wait_ge(vhat_done, t + 1)
                act.wait_ge(vrstd_done, t + 1)
                for g in range(G):
                    cols = nat[:, unit(AV, t) % 2, P * g:P * (g + 1)]
                    last = act.activation(cols, cols, ACT.Copy, scale=vrstd[:, g:g + 1])
                last.then_inc(vgain_done, 1)

            rounds = list(range(32))
            for t in range(T):
                if t < 2:
                    relus(T - 2 + t)
                evac(BQ, t)
                w_and(BQ, t)
                if t >= ROUNDS_FROM:
                    count_round(rounds.pop(0))
            for c in (AV, AU, AZ, BZ):
                for t in range(T):
                    evac(c, t)
                    w_and(c, t)
                    if rounds:
                        count_round(rounds.pop(0))
                    if c == AV:
                        v_scale(t)

            def hi_q(t):
                if t >= 2:
                    act.wait_ge(s_done, H * (t - 1))
                act.wait_ge(qT_done, t + 1)
                for odd in range(2):
                    half = slice(HALF * odd, HALF * (odd + 1))
                    act.activation(q_stack[t % 2][0:HALF, odd:H:2, :],
                                   ps_tp[tp_slot[("q", t)]][half, :].rearrange("p (h s) -> p h s", h=H // 2),
                                   ACT.Copy, scale=gq[half, 0:1]).then_inc(q_hi_done, 1)

            def exps(t, h):
                m = head_no(t, h)
                act.wait_ge(max_done, m + 1)
                if m >= 2 * H and h == 0:
                    act.wait_ge(rden_done, 2 * (t - 1))
                act.activation(probs[:, m % 2, 0:keys(t)], probs[:, m % 2, 0:keys(t)], ACT.Exp,
                               bias=negmax[:, t % 2, h:h + 1], scale=-1.0,
                               accum_out=den[:, t % 2, h:h + 1]).then_inc(exp_done, 1)

            def hi_pT(t, h):
                m = head_no(t, h)
                for g in range(1 + (t >= 4)):
                    blocks = slice(4 * g, min(t + 1, 4 * g + 4))
                    nb = blocks.stop - blocks.start
                    act.wait_ge(pT_done, group_no(t, h, g) + 1)
                    if m >= 4 and g == 0 and m % 2 == 0:
                        act.wait_ge(pv_done, m // 2 - 1)
                    act.copy(probsT_hi[:, blocks, m % 4, :],
                             ps_tp[tp_slot[("p", t, h, g)]][:, 0:P * nb].rearrange("p (b s) -> p b s", b=nb)
                             ).then_inc(pT_hi_done, 1)

            def copy_yT(t, half):
                n = 2 * t + half
                act.wait_ge(pv_done, 2 * (n + 1))
                if n > 0:
                    act.wait_ge(yT_done, n)
                act.copy(yT[:, :, :], ps_pv[:, :].rearrange("p (h s) -> p h s", h=4)).then_inc(yT_copied, 1)

            def y_square(t):
                act.wait_ge(y_half, 2 * (t + 1))
                if t > 0:
                    act.wait_ge(y_ss, t)
                act.activation(ysq[:, :], yb[:, t % 2, :], ACT.Square).then_inc(y_sq, 1)

            def hi_mix(t):
                if t >= 1:
                    act.wait_ge(out_acc, 2 * t)
                else:
                    act.wait_ge(w_lo_done, KB * (O2 + 1))
                for g in range(2):
                    act.wait_ge(mT_done, 2 * t + g + 1)
                    act.copy(mixT_hi[:, 4 * g:4 * (g + 1), :],
                             ps_tp[tp_slot[("m", t, g)]][:, :].rearrange("p (k s) -> p k s", k=4)
                             ).then_inc(m_hi_done, 1)

            hi_q(0)
            exps(0, 0)
            for t in range(T):
                for h in range(H):
                    m = head_no(t, h)
                    if m + 1 < T * H:
                        exps(*divmod(m + 1, H))
                    if h == MIX_AT and t > 0:
                        hi_mix(t - 1)
                    if h == Q_AT and t + 1 < T:
                        hi_q(t + 1)
                    if h == 0 and t > 0:
                        copy_yT(t - 1, 1)
                    if h == 4:
                        copy_yT(t, 0)
                    hi_pT(t, h)
                    if t == 0:
                        hi_w(KB * O2 + h)
                    if h == 2 and t > 0:
                        y_square(t - 1)
            copy_yT(T - 1, 1)
            y_square(T - 1)
            hi_mix(T - 1)

        @block.tensor
        def _(pe):
            issued = []

            def tp(key):
                assert tp_plan[len(issued)] == key
                if len(issued) >= 2:
                    pe.wait_ge(*tp_release(issued[-2]))
                issued.append(key)
                return ps_tp[tp_slot[key]]

            def xT(t):
                pe.wait_ge(x_loaded[t % 4], 16 * (t // 4 + 1))
                if t >= 2:
                    pe.wait_ge(x_lo_done, t - 1)
                for k in range(KB):
                    mm = pe.transpose(ps_lg[t % 2][:, P * k:P * (k + 1)], x_in[:, t % 4, P * k:P * (k + 1)],
                                      ident[:, :])
                mm.then_inc(xT_done, 1)

            def project(c, t, between=lambda k: None):
                u = unit(c, t)
                n = N0 if c == KVI else BANK
                if c == KVI:
                    pe.wait_ge(x_lo_done, t + 1)
                if u >= 2:
                    pe.wait_ge(proj_evac, u - 1)
                first = t == (T0 if c == IQ else 0)
                hi, lo = w_hi[c % 2], w_lo[c % 2]
                for k in range(KB):
                    between(k)
                    if first:
                        pe.wait_ge(w_lo_done, KB * c + k + 1)
                    rows = slice(P * t, P * (t + 1))
                    for i, (a, b) in enumerate(((xT_hi, hi), (xT_lo, hi), (xT_hi, lo))):
                        mm = pe.matmul(ps_proj[u % 2][:, 0:n], a[:, k, rows], b[:, k, 0:n],
                                       start=(k == 0 and i == 0), stop=(k == KB - 1 and i == 2))
                mm.then_inc(proj_done, 1)

            def kT(t):
                bank = tp(("k", t))
                for i in range(2):
                    pe.wait_ge(khat_done, 2 * t + i + 1)
                    mm = pe.transpose(bank[:, P * i:P * (i + 1)],
                                      khat[:, i, :, :].rearrange("p a d -> p (a d)"), ident[:, :])
                mm.then_inc(kT_done, 1)

            def four_pairs(bank, rows):
                for j in range(H // 2):
                    mm = pe.transpose(bank[:, P * j:P * (j + 1)], rows[:, P * j:P * (j + 1)], ident[:, :])
                return mm

            def qiT(t):
                pe.wait_ge(proj_evac, unit(IQ, t) + 1)
                four_pairs(tp(("qi", t)), nat[:, unit(IQ, t) % 2, :]).then_inc(qiT_done, 1)

            def dot_keys(bank, stack, h, hh, ll, n):
                for a in range(0, n, BANK):
                    b = min(n, a + BANK)
                    pe.matmul(bank[:, a:b], stack[:, h, :], hh[:, a:b], start=True, stop=False)
                    mm = pe.matmul(bank[:, a:b], stack[:, h, :], ll[:, a:b], start=False, stop=True)
                return mm

            def logit(t, h):
                if t == T0 and h == 0:
                    pe.wait_ge(x_lo_done, T)
                    pe.wait_ge(k_lo_done, T)
                m = H * (t - T0) + h
                pe.wait_ge(qi_lo_done, 2 * (t - T0) + h % 2 + 1)
                if m >= 2:
                    pe.wait_ge(relu_done, m - 1)
                dot_keys(ps_lg[m % 2], qi_stack[t % 2], h, ki_hh, ki_ll, keys(t)).then_inc(logits_done, 1)

            def index(t):
                def between(k):
                    if T0 <= t:
                        logit(t, k)
                    if k == 1 and t + 1 < T:
                        qiT(t + 1)
                return between

            pe.wait_ge(ident_ready, 1)
            xT(0)
            xT(1)
            for t in range(T):
                project(KVI, t)
                if t + 2 < T:
                    xT(t + 2)
                if t > 0:
                    kT(t - 1)
            for t in range(T0, T):
                if t == T0:
                    project(IQ, t)
                else:
                    project(IQ, t, index(t - 2))
                if t == T0:
                    kT(T - 1)
                    pe.wait_ge(sgu_loaded, 16)
                    bank = tp(("w", 0))
                    for g in range(G):
                        mm = pe.transpose(bank[:, P * g:P * (g + 1)], sgu_raw[:, g, :], ident[:, :])
                    mm.then_inc(sguT_done, 1)

            def sgu(t):
                pe.wait_ge(vgain_done, t + 1)
                pe.wait_ge(sguT_masked, 1)
                bank = tp(("sgu", t))
                for g in range(G):
                    mm = pe.matmul(bank[:, P * g:P * (g + 1)], wT_sgu[:, g, :],
                                   nat[:, unit(AV, t) % 2, P * g:P * (g + 1)], start=True, stop=True)
                mm.then_inc(sgu_done, 1)

            for t in range(T):
                if t < 2:
                    project(BQ, t, index(T - 2 + t))
                else:
                    project(BQ, t)
            for t in range(T):
                project(AV, t)
                if t > 0:
                    sgu(t - 1)
            project(AU, 0)
            sgu(T - 1)
            for t in range(1, T):
                project(AU, t)
            def qT(t):
                pe.wait_ge(q_loaded[t % 2], 16 * (t // 2 + 1))
                four_pairs(tp(("q", t)), q_in[t % 2][:, :]).then_inc(qT_done, 1)

            def scores(t, h):
                m = head_no(t, h)
                if h < 2:
                    pe.wait_ge(q_lo_done, 2 * t + h + 1)
                if m >= 2:
                    pe.wait_ge(max_done, m - 1)
                dot_keys(ps_lg[m % 2], q_stack[t % 2], h, k_hh, k_ll, keys(t)).then_inc(s_done, 1)

            def pT(t, h):
                m = head_no(t, h)
                pe.wait_ge(exp_done, m + 1)
                for g in range(1 + (t >= 4)):
                    bank = tp(("p", t, h, g))
                    for b in range(4 * g, min(t + 1, 4 * g + 4)):
                        mm = pe.transpose(bank[:, P * (b % 4):P * (b % 4 + 1)],
                                          probs[:, m % 2, P * b:P * (b + 1)], ident[:, :])
                    mm.then_inc(pT_done, 1)

            def pv(j):
                t, h = divmod(2 * j, H)
                pe.wait_ge(pT_lo_done, group_no(t, h + 1, t >= 4) + 1)
                if j == 0:
                    pe.wait_ge(proj_evac, UNITS)
                elif j % 2 == 0:
                    pe.wait_ge(yT_copied, j // 2)
                out_cols = slice(2 * P * (j % 2), 2 * P * (j % 2 + 1))
                pair = slice(2 * (j % 2), 2 * (j % 2) + 2)
                for b in range(t + 1):
                    for i, part in enumerate((probsT_hi, probsT_lo)):
                        mm = pe.matmul(ps_pv[:, out_cols].rearrange("p (h s) -> p h s", h=2), v_hl[:, b, :],
                                       part[:, b, pair, :], start=(b == 0 and i == 0), stop=(b == t and i == 1))
                mm.then_inc(pv_done, 1)

            def turn_y(t, half):
                n = 2 * t + half
                pe.wait_ge(yT_copied, n + 1)
                bank = tp(("y", t, half))
                if n == 0:
                    pe.wait_ge(fold_ready, 1)
                for h in range(4):
                    mm = pe.matmul(bank[:, DH * h:DH * (h + 1)], yT[:, h, :], fold[:, :], start=True, stop=True)
                mm.then_inc(yT_done, 1)

            def mT(t):
                pe.wait_ge(mixB_done, t + 1)
                for g, rows in enumerate((y_a[:, t, :], yb[:, t % 2, :])):
                    bank = tp(("m", t, g))
                    for j in range(4):
                        mm = pe.transpose(bank[:, P * j:P * (j + 1)], rows[:, P * j:P * (j + 1)], ident[:, :])
                    mm.then_inc(mT_done, 1)

            def out_steps(t):
                for n in range(2):
                    c = O1 + n
                    hi, lo = w_hi[c % 2], w_lo[c % 2]
                    for k in range(KB):
                        if k == 0:
                            pe.wait_ge(m_lo_done, 2 * t + 2)
                            if 2 * t + n > 0:
                                pe.wait_ge(out_ready, 2 * t + n)
                            if t == 0:
                                pe.wait_ge(w_lo_done, KB * (c + 1))
                        for i, (a, b) in enumerate(((mixT_hi, hi), (mixT_lo, hi), (mixT_hi, lo))):
                            mm = pe.matmul(ps_out[:, :], a[:, k, :], b[:, k, :],
                                           start=(k == 0 and i == 0), stop=(k == KB - 1 and i == 2))
                        if k == KB - 1:
                            mm.then_inc(out_acc, 1)
                        yield

            for c in (AZ, BZ):
                for t in range(T):
                    if (c, t) == (BZ, T - 1):
                        qT(0)
                    project(c, t)
            scores(0, 0)
            scores(0, 1)
            STEPS = {7: 3, 0: 3, 1: 2, 2: 2, 3: 2, 4: 2, 5: 2, 6: 0}
            assert sum(STEPS.values()) == 2 * KB
            pending = iter(())
            for t in range(T):
                for h in range(H):
                    m = head_no(t, h)
                    for _ in range(STEPS[h]):
                        next(pending, None)
                    if h == MIX_AT and t > 0:
                        mT(t - 1)
                        pending = out_steps(t - 1)
                    if h == Q_AT and t + 1 < T:
                        qT(t + 1)
                    if m % 2 == 0 and m > 0:
                        pv(m // 2 - 1)
                    if h == YT_AT[0]:
                        turn_y(t, 0)
                    if h == YT_AT[1] and t > 0:
                        turn_y(t - 1, 1)
                    pT(t, h)
                    if m + 2 < T * H:
                        scores(*divmod(m + 2, H))
            pv(T * H // 2 - 1)
            for _ in pending:
                pass
            turn_y(T - 1, 1)
            mT(T - 1)
            for _ in out_steps(T - 1):
                pass

        @block.vector
        def _(dve):
            steps = [0]

            def then(ins):
                steps[0] += 1
                ins.then_inc(dve_step, 1)
                dve.wait_ge(dve_step, steps[0])

            def lo_x(t):
                dve.wait_ge(x_hi_done, t + 1)
                rows = slice(P * t, P * (t + 1))
                dve.tensor_tensor(xT_lo[:, :, rows], ps_lg[t % 2][:, :].rearrange("p (k s) -> p k s", k=KB),
                                  xT_hi[:, :, rows].bitcast(F32), ALU.subtract).then_inc(x_lo_done, 1)

            def k_stats(t):
                rows = kvi[:, t % 2, :]
                dve.wait_ge(proj_evac, unit(KVI, t) + 1)
                if t >= 2:
                    dve.wait_ge(krstd_done, t - 1)
                then(dve.bn_stats(bn6[:, 0, :], rows[:, NKV:NKV + DH]))
                dve.bn_aggr(kstat[:, t % 2, 0:2], bn6[:, 0, :]).then_inc(kstat_done, 1)
                dve.tensor_tensor_reduce(bn_tmp, rows[:, 0:DH], rows[:, 0:DH], 1.0 / DH, 0.0, ALU.mult,
                                         ALU.add, kstat[:, t % 2, 2:3]).then_inc(kstat_done, 1)

            def k_norm(t):
                rows = kvi[:, t % 2, :]
                dve.wait_ge(krstd_done, t + 1)
                if t >= 1:
                    dve.wait_ge(kT_done, t)
                twice = lambda v: v.unsqueeze(1).broadcast_to([P, 2, DH])
                dve.tensor_scalar(khat[:, 0, :, :], twice(rows[:, 0:DH]), krstd[:, t % 2, 1:2], None,
                                  ALU.mult).then_inc(khat_done, 1)
                dve.tensor_scalar(khat[:, 1, :, :], twice(rows[:, NKV:NKV + DH]), kstat[:, t % 2, 0:1],
                                  krstd[:, t % 2, 0:1], ALU.subtract, ALU.mult).then_inc(khat_done, 1)

            def lo_k(t):
                dve.wait_ge(k_hi_done, 2 * (t + 1))
                bank = ps_tp[tp_slot[("k", t)]]
                cols = slice(P * t, P * (t + 1))
                dve.scalar_tensor_tensor(out=k_ll[:, cols], in0=bank[:, 0:P], scalar=gk[:, 0:1],
                                         in1=k_hh[:, cols].bitcast(F32), op0=ALU.mult, op1=ALU.subtract)
                dve.scalar_tensor_tensor(out=ki_ll[:, cols], in0=bank[:, P:2 * P], scalar=gik[:, 0:1],
                                         in1=ki_hh[:, cols].bitcast(F32), op0=ALU.mult,
                                         op1=ALU.subtract).then_inc(k_lo_done, 1)

            dve.wait_ge(dist_ready, 1)
            dve.scalar_tensor_tensor(out=negdist[:, :], in0=dist_i[:, :], scalar=-1.0, in1=dist_i[:, :],
                                     op0=ALU.mult, op1=ALU.min)
            dve.scalar_tensor_tensor(out=near[:, :], in0=dist_i[:, S - TOPK:S], scalar=-1.0,
                                     in1=dist_i[:, S - TOPK:S], op0=ALU.mult,
                                     op1=ALU.min).then_inc(dist_ready, 1)
            def lo_w(n):
                c, k = divmod(n, KB)
                dve.wait_ge(w_hi_done, n + 1)
                if c == KVI:
                    raw, hi, lo = kvi_raw[:, k, :], w_hi[0][:, k, 0:N0], w_lo[0][:, k, 0:N0]
                else:
                    raw, hi, lo = stage[:, k % NSTAGE, :], w_hi[c][:, k, :], w_lo[c][:, k, :]
                dve.tensor_tensor(lo, raw, hi.bitcast(F32), ALU.subtract).then_inc(w_lo_done, 1)

            lo_x(0)
            for k in range(KB):
                lo_w(k)
            lo_x(1)
            for t in range(T):
                if t == 1:
                    dve.wait_ge(consts_loaded, CONSTS)
                k_stats(t)
                if t + 2 < T:
                    lo_x(t + 2)
                k_norm(t)
                lo_w(KB + t)
                if t > 0:
                    lo_k(t - 1)

            def lo_qi(t):
                for odd in range(2):
                    dve.wait_ge(qi_hi_done, 2 * (t - T0) + odd + 1)
                    bank = ps_tp[tp_slot[("qi", t)]][HALF * odd:HALF * (odd + 1), :]
                    dve.tensor_tensor(qi_stack[t % 2][HALF:P, odd:H:2, :],
                                      bank.rearrange("p (h s) -> p h s", h=H // 2),
                                      qi_stack[t % 2][0:HALF, odd:H:2, :].bitcast(F32),
                                      ALU.subtract).then_inc(qi_lo_done, 1)

            def sum_heads(t):
                row = score[:, sc_off[t]:sc_off[t] + keys(t)]
                for h in range(H):
                    if h == 2 and t + 1 < T:
                        lo_qi(t + 1)
                    m = H * (t - T0) + h
                    dve.wait_ge(relu_done, m + 1)
                    r = relu_sb[:, m % 2, 0:keys(t)]
                    if h == 0:
                        dve.wait_ge(kvi_used, 3 * T)
                        dve.tensor_scalar(row, r, idx_w[:, t, 0:1], None, ALU.mult).then_inc(score_acc, 1)
                    else:
                        dve.wait_ge(score_acc, m)
                        dve.scalar_tensor_tensor(out=row, in0=r, scalar=idx_w[:, t, h:h + 1], in1=row,
                                                 op0=ALU.mult, op1=ALU.add).then_inc(score_acc, 1)
                dve.wait_ge(score_acc, H * (t - T0 + 1))
                then(dve.memset(row[0:HALF, keys(t) - HALF:keys(t)], NEG))

            for t in range(T0, T):
                if t == T0:
                    lo_k(T - 1)
                    dve.wait_ge(dist_ready, 3)
                    dve.wait_ge(sguT_done, 1)
                    dve.wait_ge(w_lo_done, KB)
                if t == T0 + 1:
                    lo_qi(T0)
                if t > T0 + 1:
                    sum_heads(t - 2)
            dve.wait_ge(sguT_copied, 1)
            dve.memset(wT_sgu[HALF:P, :, 0:HALF], 0.0).then_inc(sguT_masked, 1)

            cand_f = cand[:, :].bitcast(F32)

            hits = (gt, eq, rank)
            counted = [0]
            selected = [0]

            def count_tile(t, against=cand):
                n = counted[0]
                counted[0] += 1
                if selected[0]:
                    dve.wait_ge(mask_ready, selected[0])
                if n >= len(hits):
                    dve.wait_ge(tile_counted, n - len(hits) + 1)
                return dve.tensor_scalar(hits[n % len(hits)][:, 0:keys(t)], score[:, sc_off[t]:sc_off[t] + keys(t)],
                                         against[:, t:t + 1].bitcast(F32), None, ALU.is_ge, ALU.add,
                                         accum_out=cnt[:, t:t + 1]).then_inc(tile_counted, 1)

            def settle(b, tiles):
                c, d = cand[:, tiles], delta[:, tiles]
                if b == 31:
                    return dve.tensor_scalar(c, d, 1 << 30, None, ALU.bitwise_xor)
                return dve.scalar_tensor_tensor(out=c, in0=d, scalar=(1 << b) >> 1, in1=c,
                                                op0=ALU.bitwise_xor, op1=ALU.bitwise_xor)

            def too_few(b, counts, d, limit, op):
                return dve.tensor_scalar(d, counts, limit, -1.0 if b == 31 else float(1 << b), op, ALU.mult)

            def step_first(b):
                for t in range(T0, SPLIT):
                    count_tile(t)
                dve.wait_ge(tile_counted, counted[0])
                then(too_few(b, cnt[:, T0:SPLIT], delta[:, T0:SPLIT], TOPK - 0.5, ALU.is_lt))
                then(settle(b, slice(T0, SPLIT)))

            def step_last(b):
                dve.wait_ge(act_counted, (T - SPLIT) * (32 - b))
                for i, t in enumerate(range(SPLIT, T)):
                    last = too_few(b, sign_sum[:, i:i + 1], delta[:, t:t + 1], keys(t) - 2.0 * TOPK + 1.0,
                                   ALU.is_gt)
                then(last)
                settle(b, slice(SPLIT, T)).then_inc(cand_ready, 1)
                dve.wait_ge(cand_ready, 33 - b)

            def after_ties():
                last = slice(SPLIT, T)
                dve.tensor_scalar(delta[:, last], cand[:, last], 31, 1, ALU.arith_shift_right,
                                  ALU.bitwise_or).then_inc(succ_wanted, 1)
                dve.wait_ge(succ_ready, 1)
                for t in range(SPLIT, T):
                    count_tile(t, succ)
                dve.wait_ge(tile_counted, counted[0])
                then(dve.tensor_tensor(succ[:, last], succ[:, last], cand[:, last], ALU.bitwise_xor))
                then(dve.tensor_scalar(delta[:, last], cnt[:, last], TOPK - 0.5, -1.0, ALU.is_ge, ALU.mult))
                then(dve.tensor_tensor(succ[:, last], succ[:, last], delta[:, last], ALU.bitwise_and))
                then(dve.tensor_tensor(cand[:, last], cand[:, last], succ[:, last], ALU.bitwise_xor))

            def select(t):
                row = score[:, sc_off[t]:sc_off[t] + keys(t)]
                thr = cand_f[:, t:t + 1]
                n = keys(t)
                if selected[0]:
                    dve.wait_ge(mask_ready, selected[0])
                dve.wait_ge(tile_counted, counted[0])
                selected[0] += 1
                dve.tensor_scalar(gt[:, 0:n], row, thr, None, ALU.is_gt, ALU.add, accum_out=cnt[:, t:t + 1])
                then(dve.tensor_scalar(eq[:, 0:n], row, thr, None, ALU.is_equal))
                then(dve.tensor_scalar(room[:, t:t + 1], cnt[:, t:t + 1], -1.0, float(TOPK), ALU.mult, ALU.add))
                then(dve.tensor_tensor_scan(rank[:, 0:n], eq[:, 0:n], eq[:, 0:n], 0.0, ALU.add, ALU.max))
                then(dve.scalar_tensor_tensor(out=eq[:, 0:n], in0=rank[:, 0:n], scalar=room[:, t:t + 1],
                                              in1=eq[:, 0:n], op0=ALU.is_le, op1=ALU.mult))
                then(dve.scalar_tensor_tensor(out=gt[:, 0:n], in0=gt[:, 0:n], scalar=-1.0, in1=eq[:, 0:n],
                                              op0=ALU.add, op1=ALU.add))
                dve.scalar_tensor_tensor(out=row, in0=gt[:, 0:n], scalar=-NEG, in1=negdist[:, S - n:S],
                                         op0=ALU.mult, op1=ALU.add).then_inc(mask_ready, 1)

            def av_stats(t):
                rows = nat[:, unit(AV, t) % 2, :]
                dve.wait_ge(proj_evac, unit(AV, t) + 1)
                for g in range(G):
                    last = dve.bn_stats(bn6[:, g, :], rows[:, P * g:P * (g + 1)])
                then(last)
                if t > 0:
                    dve.wait_ge(vgain_done, t)
                for g in range(G):
                    last = dve.bn_aggr(vstat[:, g, :], bn6[:, g, :])
                last.then_inc(vstat_done, 1)

            def av_norm(t):
                rows = nat[:, unit(AV, t) % 2, :]
                dve.wait_ge(vstat_done, t + 1)
                for g in range(G):
                    cols = rows[:, P * g:P * (g + 1)]
                    last = dve.scalar_tensor_tensor(out=cols, in0=cols, scalar=vstat[:, g, 0:1],
                                                    in1=vg_row[:, P * g:P * (g + 1)],
                                                    op0=ALU.subtract, op1=ALU.mult)
                last.then_inc(vhat_done, 1)

            def gate(t):
                dve.wait_ge(sgu_done, t + 1)
                dve.tensor_tensor(y_a[:, t, :].rearrange("p (g c) -> p g c", g=G),
                                  ps_tp[tp_slot[("sgu", t)]][:, :].rearrange("p (g c) -> p g c", g=G),
                                  bias_s[:, :].unsqueeze(2).broadcast_to([P, G, P]),
                                  ALU.add).then_inc(gate_ready, 1)

            def ya_square(t):
                dve.wait_ge(ya_done, t + 1)
                for g in range(G):
                    cols = y_a[:, t, P * g:P * (g + 1)]
                    last = dve.tensor_tensor_reduce(ya_tmp[:, g, :], cols, cols, 1.0 / P, 0.0, ALU.mult, ALU.add,
                                                    ya_ms[:, t, g:g + 1])
                last.then_inc(ya_ms_done, 1)

            def mix_a(t):
                dve.wait_ge(proj_evac, unit(AZ, t) + 1)
                dve.wait_ge(ya_r_done, t + 1)
                for g in range(G):
                    cols = slice(P * g, P * (g + 1))
                    last = dve.scalar_tensor_tensor(out=y_a[:, t, cols], in0=y_a[:, t, cols],
                                                    scalar=ya_r[:, t, g:g + 1],
                                                    in1=nat[:, unit(AZ, t) % 2, cols],
                                                    op0=ALU.mult, op1=ALU.mult)
                last.then_inc(mixA_done, 1)

            def q_sums(t):
                dve.wait_ge(q_sq, t + 1)
                if t > 0:
                    dve.wait_ge(q_normed, t)
                dve.tensor_reduce(qss[:, :], q_sq_tmp.rearrange("p (h d) -> p h d", h=H), AX.X,
                                  ALU.add).then_inc(q_ss, 1)

            work = {"first": list(range(31, -1, -1)), "last": list(range(31, -1, -1)),
                    "tiles": list(range(T0, T))}

            def background(first, last):
                if first and work["first"]:
                    step_first(work["first"].pop(0))
                if last and work["last"]:
                    step_last(work["last"].pop(0))
                    if not work["last"]:
                        after_ties()
                if not work["first"] and work["tiles"] and (work["tiles"][0] < SPLIT or not work["last"]):
                    select(work["tiles"].pop(0))

            for t in range(T):
                if t == 0:
                    sum_heads(T - 2)
                    then(dve.memset(cand[:, :].bitcast(F32), 0.0))
                if t == 1:
                    sum_heads(T - 1)
                    dve.memset(delta[:, T - 1:T], 0).then_inc(cand_ready, 1)
                q_sums(t)
                background(True, t >= ROUNDS_FROM)
            for t in range(T):
                av_stats(t)
                av_norm(t)
                if t > 0:
                    gate(t - 1)
                background(True, True)
            for t in range(T):
                if t == 0:
                    gate(T - 1)
                ya_square(t)
                background(True, True)
            for t in range(T):
                mix_a(t)
                background(True, True)
            for t in range(T):
                background(True, True)

            def lo_q(t):
                for odd in range(2):
                    dve.wait_ge(q_hi_done, 2 * t + odd + 1)
                    half = slice(HALF * odd, HALF * (odd + 1))
                    dve.scalar_tensor_tensor(
                        out=q_stack[t % 2][HALF:P, odd:H:2, :],
                        in0=ps_tp[tp_slot[("q", t)]][half, :].rearrange("p (h s) -> p h s", h=H // 2),
                        scalar=gq[half, 0:1], in1=q_stack[t % 2][0:HALF, odd:H:2, :].bitcast(F32),
                        op0=ALU.mult, op1=ALU.subtract).then_inc(q_lo_done, 1)

            def bias_max(t, h):
                m = head_no(t, h)
                dve.wait_ge(s_done, m + 1)
                if m >= 2:
                    dve.wait_ge(pT_done, group_no(*last_group(m - 2)) + 1)
                if t < T0:
                    d = near[:, TOPK - keys(t):TOPK]
                else:
                    if h == 0:
                        dve.wait_ge(mask_ready, t - T0 + 1)
                    d = score[:, sc_off[t]:sc_off[t] + keys(t)]
                dve.tensor_tensor_reduce(probs[:, m % 2, 0:keys(t)], ps_lg[m % 2][:, 0:keys(t)], d,
                                         -(2.0 ** -(h + 1)), BIG, ALU.add, ALU.min,
                                         negmax[:, t % 2, h:h + 1]).then_inc(max_done, 1)

            def lo_pT(t, h):
                m = head_no(t, h)
                for g in range(1 + (t >= 4)):
                    blocks = slice(4 * g, min(t + 1, 4 * g + 4))
                    nb = blocks.stop - blocks.start
                    dve.wait_ge(pT_hi_done, group_no(t, h, g) + 1)
                    dve.tensor_tensor(probsT_lo[:, blocks, m % 4, :],
                                      ps_tp[tp_slot[("p", t, h, g)]][:, 0:P * nb].rearrange(
                                          "p (b s) -> p b s", b=nb),
                                      probsT_hi[:, blocks, m % 4, :].bitcast(F32),
                                      ALU.subtract).then_inc(pT_lo_done, 1)

            def y_rows(t, half):
                n = 2 * t + half
                heads = slice(4 * half, 4 * half + 4)
                if half == 0 and t > 1:
                    dve.wait_ge(mT_done, 2 * (t - 1))
                rows = yb[:, t % 2, B_W // 2 * half:B_W // 2 * (half + 1)].rearrange("p (h d) -> p h d", h=4)
                dve.wait_ge(exp_done, H * t + 4 * (half + 1))
                dve.reciprocal(rden[:, heads], den[:, t % 2, heads]).then_inc(rden_done, 1)
                dve.wait_ge(yT_done, n + 1)
                dve.wait_ge(rden_done, n + 1)
                dve.tensor_tensor(rows, ps_tp[tp_slot[("y", t, half)]][:, 0:B_W // 2].rearrange(
                    "p (h d) -> p h d", h=4), rden[:, heads].unsqueeze(2).broadcast_to([P, 4, DH]),
                                  ALU.mult).then_inc(y_half, 1)

            def mix_b(t):
                dve.wait_ge(y_gated, t + 1)
                dve.wait_ge(y_step, 2 * (t + 1))
                dve.tensor_tensor(yb[:, t % 2, :].rearrange("p (h d) -> p h d", h=H),
                                  yz[:, :].rearrange("p (h d) -> p h d", h=H),
                                  yr[:, :].unsqueeze(2).broadcast_to([P, H, DH]), ALU.mult).then_inc(mixB_done, 1)

            def y_sums(t):
                dve.wait_ge(y_sq, t + 1)
                dve.tensor_reduce(yss[:, :], ysq[:, :].rearrange("p (h d) -> p h d", h=H), AX.X,
                                  ALU.add).then_inc(y_ss, 1)

            def lo_mix(t):
                for g in range(2):
                    dve.wait_ge(m_hi_done, 2 * t + g + 1)
                    part = slice(4 * g, 4 * (g + 1))
                    dve.tensor_tensor(mixT_lo[:, part, :],
                                      ps_tp[tp_slot[("m", t, g)]][:, :].rearrange("p (k s) -> p k s", k=4),
                                      mixT_hi[:, part, :].bitcast(F32),
                                      ALU.subtract).then_inc(m_lo_done, 1)

            def add_res(t, n):
                dve.wait_ge(out_acc, 2 * t + n + 1)
                if n == 0:
                    dve.wait_ge(res_loaded, 16 * (t + 1))
                half = res[:, BANK * n:BANK * (n + 1)]
                dve.tensor_tensor(half, ps_out[:, :], half, ALU.add).then_inc(out_ready, 1)

            lo_q(0)
            bias_max(0, 0)
            bias_max(0, 1)
            for t in range(T):
                for h in range(H):
                    m = head_no(t, h)
                    if h == 1 and t > 1:
                        add_res(t - 2, 0)
                    if h == 5 and t > 1:
                        add_res(t - 2, 1)
                    if h == MIX_AT and t > 0:
                        lo_mix(t - 1)
                    if h == Q_AT and t + 1 < T:
                        lo_q(t + 1)
                    if h == YT_AT[0]:
                        y_rows(t, 0)
                    if h == YT_AT[1] and t > 0:
                        y_rows(t - 1, 1)
                    if m + 2 < T * H:
                        for_tile, _ = divmod(m + 2, H)
                        while work["tiles"] and work["tiles"][0] <= for_tile:
                            background(True, True)
                        bias_max(*divmod(m + 2, H))
                    lo_pT(t, h)
                    if h == 2 and t > 0:
                        y_sums(t - 1)
                    if h == 4 and t > 0:
                        mix_b(t - 1)
                    if work["tiles"]:
                        background(True, True)
            add_res(T - 2, 0)
            add_res(T - 2, 1)
            y_rows(T - 1, 1)
            y_sums(T - 1)
            mix_b(T - 1)
            lo_mix(T - 1)
            add_res(T - 1, 0)
            add_res(T - 1, 1)


_INS = ["x", "norm_gain", "w_in", "sgu_norm_gain", "sgu_w", "sgu_b", "q_norm_gain", "k_norm_gain",
        "idx_k_norm_gain", "branch_norm_gain", "w_out"]
_OUTS = [((1, 1024, 1024), "float32")]


def kernel(**inputs):
    import numpy as _np
    import concourse.bacc as _bacc
    from concourse import mybir as _mybir
    from concourse.bass_utils import run_bass_kernel_spmd as _run

    nc = _bacc.Bacc("TRN2", target_bir_lowering=False, num_devices=1)
    arrays, args = {}, []
    for name in _INS:
        a = _np.ascontiguousarray(inputs[name])
        arrays[f"in_{name}_dram"] = a
        args.append(nc.dram_tensor(f"in_{name}_dram", a.shape, _mybir.dt.from_np(a.dtype), kind="ExternalInput").ap())
    for i, (shape, dtype) in enumerate(_OUTS):
        dt = _mybir.dt.from_np(_np.dtype(dtype))
        args.append(nc.dram_tensor(f"out_{i}_dram", shape, dt, kind="ExternalOutput").ap())
    hybrid_block(nc, *args)
    r = _run(nc, [arrays], core_ids=[0])
    got = tuple(r.results[0][f"out_{i}_dram"] for i in range(len(_OUTS)))
    return got[0]
```

```python
from contextlib import ExitStack

import concourse.bass as bass
from concourse import mybir

F32 = mybir.dt.float32
F32R = mybir.dt.float32r
F16 = mybir.dt.float16
BF16 = mybir.dt.bfloat16
I32 = mybir.dt.int32
I8 = mybir.dt.int8
ALU = mybir.AluOpType
ACT = mybir.ActivationFunctionType
AX = mybir.AxisListType

P = 128
HALF = 64
BANK = 512
TOPK = 256
NEG = -1e30
EPS = 1e-6
BIG = 3.0e38


def hybrid_block(nc, x, norm_gain, w_in, sgu_norm_gain, sgu_w, sgu_b, q_norm_gain, k_norm_gain,
                 idx_k_norm_gain, branch_norm_gain, w_out, out):
    _, S, D = x.shape
    T = S // P
    KB = D // P
    G = sgu_w.shape[1]
    H = 8
    DH = q_norm_gain.shape[1]
    A_W = G * P
    B_W = H * DH
    T0 = TOPK // P
    IDX_SCALE = (H ** -0.5) * (DH ** -0.5)
    assert (S, D, G, DH, A_W, B_W) == (1024, 1024, 4, 64, 512, 512)

    o_au, o_av, o_az, o_bq = 0, A_W, 2 * A_W, 3 * A_W
    o_bk = o_bq + B_W
    o_bz = o_bk + 2 * DH
    o_iq = o_bz + B_W
    o_ik = o_iq + H * DH
    NKV = 2 * DH
    NIK = DH + H
    N0 = NKV + NIK
    KVI, IQ, BQ, AV, AU, AZ, BZ, O1, O2 = range(9)
    chunk_src = {IQ: o_iq, AV: o_av, AU: o_au, AZ: o_az, BZ: o_bz, BQ: o_bq}

    def unit(c, t):
        return t if c == KVI else T * c + t - T0

    UNITS = unit(BZ, T - 1) + 1

    def keys(t):
        return P * (t + 1)

    WARM_0, WARM_1 = 14, 20
    ROUNDS_FROM = 2
    SPLIT = 5
    sc_off = {t: sum(keys(s) for s in range(T0, t)) for t in range(T0, T)}
    SC_COLS = sum(keys(t) for t in range(T0, T))

    ctx = ExitStack()
    with ctx:
        def psum(name, shape):
            return ctx.enter_context(nc.psum_tensor(name, shape, F32))

        def sem(name):
            return ctx.enter_context(nc.semaphore(name))

        base = (nc.sbuf_base + 63) // 64 * 64
        size_of = {F32: 4, F32R: 4, I32: 4, F16: 2, BF16: 2, I8: 1}
        top = [base]

        def place(name, shape, dt, at=None):
            n = size_of[dt]
            for s in shape[1:]:
                n *= s
            where = top[0] if at is None else at
            if at is None:
                top[0] = where + (n + 31) // 32 * 32
                assert top[0] <= nc.sbuf_usable_end, (name, top[0] - nc.sbuf_usable_end)
            return nc.alloc_sbuf_tensor_at(name, shape, dt, offset=where)

        w_hi = [place(f"w_hi{i}", [P, KB, BANK], F32R) for i in range(2)]
        w_lo = [place(f"w_lo{i}", [P, KB, BANK], F32R) for i in range(2)]
        NSTAGE = 3
        stage = place("stage", [P, NSTAGE, BANK], F32)
        mixT_hi = place("mixT_hi", [P, KB, P], F32R, at=top[0] - 4 * NSTAGE * BANK)
        zone_x = top[0]
        xT_hi = place("xT_hi", [P, KB, S], F32R)
        zone_x2 = top[0]
        xT_lo = place("xT_lo", [P, KB, S], F32R)
        hi_f32 = place("hi_f32", [P, KB, S], F32, at=zone_x)
        lo_f32 = place("lo_f32", [P, KB, S], F32, at=zone_x2)

        def column(zone, t, n=1):
            return zone[:, :, P * t:P * (t + n)]

        q_stack = [column(xT_hi, i) for i in range(2)]
        probs = [column(lo_f32, i) for i in range(2)]
        EARLY = 2
        FREE = 4
        PT_AT = (2, 3, 5, 6)

        def probsT(zone, m):
            if m < 4 * H:
                row, col = 4 * (m // 2 % 2), PT_AT[m % 2]
            else:
                row, col = 0, PT_AT[m % 4]
            return zone[:, row:KB, P * col:P * (col + 2 - m % 2)]

        yb = [hi_f32[:, 4 * i:4 * i + 4, P * 4:P * 5] for i in range(2)]
        z_in = [lo_f32[:, 4 * i:4 * i + 4, P * 4:P * 5] for i in range(2)]
        mixT_lo = column(xT_hi, 7)
        res = [column(lo_f32, 7)] * (T - 1)
        last_raw = [zone[:, 2 * j:2 * j + 2, P * 5:P * 7] for zone in (hi_f32, lo_f32) for j in range(KB // 2)]
        zone_y = top[0]
        y_a = place("y_a", [P, T, A_W], F32)
        x_in = place("x_in", [P, 4, D], F32, at=zone_y)
        qi_stack = [place(f"qi_stack{i}", [P, H, P], F32R, at=zone_y + 4096 * i) for i in range(2)]
        relu_sb = place("relu_sb", [P, 2, S], F32, at=zone_y + 8192)
        zone_s = top[0]
        score = place("score", [P, SC_COLS], F32)
        kvi_raw = place("kvi_raw", [P, KB, N0], F32, at=zone_s)
        dist_i = place("dist_i", [P, S], I32, at=zone_s + 4 * KB * N0)
        sgu_raw = place("sgu_raw", [P, G, P], F32, at=zone_s + 4 * (KB * N0 + S))
        assert KB * N0 + S + G * P <= SC_COLS
        res.append(place("res_last", [P, KB, P], F32, at=zone_s)[:, :, :])
        assert D <= sc_off[5]
        k_hh = place("k_hh", [P, S], F32R)
        k_ll = place("k_ll", [P, S], F32R)
        ki_hh = place("ki_hh", [P, S], F32R)
        ki_ll = place("ki_ll", [P, S], F32R)
        v_hl = place("v_hl", [P, T, 2 * DH], F32R)
        negdist = place("negdist", [P, S], F16)
        near = place("near", [P, TOPK], F32)
        ident = place("ident", [P, P], F32)
        fold = place("fold", [P, DH], F32)
        nat = place("nat", [P, 2, BANK], F32)
        ysq = place("ysq", [P, B_W], F32, at=top[0] - 8 * BANK)
        yz = place("yz", [P, B_W], F32, at=top[0] - 4 * BANK)
        zone_k = top[0]
        kvi = place("kvi", [P, 2, N0], F32)
        khat = place("khat", [P, 2, 2, DH], F32)
        q_sq_tmp = place("q_sq_tmp", [P, B_W], F32, at=zone_k)[:, :]
        assert zone_k + 4 * B_W <= top[0]
        yT = place("yT", [P, 4, P], F32, at=top[0])
        wT_sgu = place("wT_sgu", [P, G, P], F32)
        q_in = [place("q_in0", [P, B_W], F32, at=zone_k), place("q_in1", [P, B_W], F32, at=top[0])]
        vg_row = place("vg_row", [P, A_W], F32)
        gt = place("gt", [P, S], I8)
        eq = place("eq", [P, S], I8)
        x_sq = place("x_sq", [P, S], BF16, at=top[0])
        rank = place("rank", [P, S], F16)
        g_in = place("g_in", [P, KB], F32)
        g_out = place("g_out", [P, KB], F32)
        gq = place("gq", [P, 1], F32)
        gk = place("gk", [P, 1], F32)
        gik = place("gik", [P, 1], F32)
        bias_s = place("bias_s", [P, G], F32)
        q_scale = place("q_scale", [P, H], F32)
        nhalf = place("nhalf", [P, H], F32)
        ss_x = place("ss_x", [P, T], F32)
        rstd_x = place("rstd_x", [P, T], F32)
        half_rstd = place("half_rstd", [P, T], F32)
        kstat = place("kstat", [P, 2, 4], F32)
        krstd = place("krstd", [P, 2, 2], F32)
        idx_w = place("idx_w", [P, T, H], F32)
        bn6 = place("bn6", [P, G, 6], F32)
        vstat = place("vstat", [P, G, 2], F32)
        vrstd = place("vrstd", [P, G], F32)
        ya_ms = place("ya_ms", [P, T, G], F32)
        ya_r = place("ya_r", [P, T, G], F32)
        cnt = place("cnt", [P, T], F32)
        sign_sum = place("sign_sum", [P, T - SPLIT], F32)
        succ = place("succ", [P, T], I32)
        delta = place("delta", [P, T], I32)
        cand = place("cand", [P, T], I32)
        room = place("room", [P, T], F32)
        qss = place("qss", [P, H], F32)
        qr = place("qr", [P, H], F32)
        negmax = place("negmax", [P, 2, H], F32)
        den = place("den", [P, 2, H], F32)
        rden = place("rden", [P, H], F32)
        yss = place("yss", [P, H], F32)
        yr = place("yr", [P, H], F32)
        bn_tmp = place("bn_tmp", [P, DH], F32)[:, :]
        ya_tmp = wT_sgu
        CONSTS = 16 * 9

        ps_proj = [psum(f"ps_proj{i}", [P, BANK]) for i in range(2)]
        ps_tp = [psum(f"ps_tp{i}", [P, BANK]) for i in range(2)]
        ps_lg = [psum(f"ps_lg{i}", [P, S]) for i in range(2)]
        ps_out, ps_pv = ps_proj

        def out_bank(t, n):
            return ps_out[:, :] if t < T - 1 else ps_lg[0][:, BANK * n:BANK * (n + 1)]

        q_dram = nc.dram_tensor("q_scratch", (S, B_W), F32, kind="Internal").ap()
        z_dram = nc.dram_tensor("z_scratch", (S, B_W), F32, kind="Internal").ap()

        x_loaded = [sem(f"x_loaded{i}") for i in range(4)]
        kvi_loaded = [sem(f"kvi_loaded{i}") for i in range(2)]
        stage_loaded = [sem(f"stage_loaded{i}") for i in range(NSTAGE)]
        g_in_loaded = sem("g_in_loaded")
        consts_loaded = sem("consts_loaded")
        sgu_loaded = sem("sgu_loaded")
        last_w_loaded = [sem(f"last_w_loaded{i}") for i in range(2)]
        setup_step = sem("setup_step")
        ident_ready = sem("ident_ready")
        dist_ready = sem("dist_ready")
        w_scaled = sem("w_scaled")
        w_hi_done = sem("w_hi_done")
        w_lo_done = sem("w_lo_done")
        xT_done = sem("xT_done")
        ss_done = sem("ss_done")
        ms_ready = sem("ms_ready")
        rstd_ready = sem("rstd_ready")
        x_hi_done = sem("x_hi_done")
        x_lo_done = sem("x_lo_done")
        proj_done = sem("proj_done")
        proj_evac = sem("proj_evac")
        half_rstd_ready = sem("half_rstd_ready")
        z_tanh = sem("z_tanh")
        kstat_done = sem("kstat_done")
        kms_ready = sem("kms_ready")
        krstd_done = sem("krstd_done")
        khat_done = sem("khat_done")
        kvi_used = sem("kvi_used")
        kT_done = sem("kT_done")
        k_hi_done = sem("k_hi_done")
        k_lo_done = sem("k_lo_done")
        sguT_done = sem("sguT_done")
        sguT_copied = sem("sguT_copied")
        qiT_done = sem("qiT_done")
        qi_hi_done = sem("qi_hi_done")
        qi_lo_done = sem("qi_lo_done")
        logits_done = sem("logits_done")
        relu_done = sem("relu_done")
        score_acc = sem("score_acc")
        vstat_done = sem("vstat_done")
        veps_done = sem("veps_done")
        vrstd_done = sem("vrstd_done")
        vhat_done = sem("vhat_done")
        vgain_done = sem("vgain_done")
        sgu_done = sem("sgu_done")
        gate_ready = sem("gate_ready")
        ya_done = sem("ya_done")
        ya_ms_done = sem("ya_ms_done")
        ya_eps_done = sem("ya_eps_done")
        ya_r_done = sem("ya_r_done")
        mixA_done = sem("mixA_done")
        dve_step = sem("dve_step")
        z_stored = [sem(f"z_stored{i}") for i in range(2)]
        q_stored = [sem(f"q_stored{i}") for i in range(2)]
        q_sq = sem("q_sq")
        q_ss = sem("q_ss")
        q_step = sem("q_step")
        q_normed = sem("q_normed")
        mask_ready = sem("mask_ready")
        q_loaded = [sem(f"q_loaded{i}") for i in range(2)]
        z_loaded = [sem(f"z_loaded{i}") for i in range(2)]
        res_loaded = sem("res_loaded")
        last_res_loaded = sem("last_res_loaded")
        qT_done = sem("qT_done")
        q_hi_done = sem("q_hi_done")
        q_lo_done = sem("q_lo_done")
        s_done = sem("s_done")
        max_done = sem("max_done")
        exp_done = sem("exp_done")
        pT_done = sem("pT_done")
        act_counted = sem("act_counted")
        cand_ready = sem("cand_ready")
        succ_wanted = sem("succ_wanted")
        succ_ready = sem("succ_ready")
        fold_ready = sem("fold_ready")
        yT_copied = sem("yT_copied")
        yT_done = sem("yT_done")
        y_half = sem("y_half")
        y_gated = sem("y_gated")
        tile_counted = sem("tile_counted")
        sguT_masked = sem("sguT_masked")
        pT_hi_done = sem("pT_hi_done")
        pT_lo_done = sem("pT_lo_done")
        pv_done = sem("pv_done")
        rden_done = sem("rden_done")
        y_sq = sem("y_sq")
        y_ss = sem("y_ss")
        y_step = sem("y_step")
        mixB_done = sem("mixB_done")
        mT_done = sem("mT_done")
        m_hi_done = sem("m_hi_done")
        m_lo_done = sem("m_lo_done")
        out_acc = sem("out_acc")
        out_ready = sem("out_ready")
        out_stored = sem("out_stored")

        tp_plan = []
        for t in range(T):
            tp_plan.append(("k", t))
        tp_plan.append(("w", 0))
        for t in range(T0, T):
            tp_plan.append(("qi", t))
        for t in range(T):
            tp_plan.append(("sgu", t))
        Q_AT, MIX_AT, YT_AT = 2, 6, (5, 1)
        for t in range(T):
            if t == 0:
                tp_plan.append(("q", 0))
            for h in range(H):
                if h == YT_AT[0]:
                    tp_plan.append(("y", t, 0))
                if h == YT_AT[1] and t > 0:
                    tp_plan.append(("y", t - 1, 1))
                if h == MIX_AT and t > 0:
                    tp_plan += [("m", t - 1, 0), ("m", t - 1, 1)]
                if h == Q_AT and t + 1 < T:
                    tp_plan.append(("q", t + 1))
                tp_plan += [("p", t, h, g) for g in range(1 + (t >= 4))]
        tp_plan += [("y", T - 1, 1), ("m", T - 1, 0), ("m", T - 1, 1)]
        tp_slot = {key: n % 2 for n, key in enumerate(tp_plan)}

        STEPS_BZ = [3] * 10 + [2]
        assert sum(STEPS_BZ) == KB * (T - FREE)
        last_units = {}
        for m in range(len(STEPS_BZ)):
            for n in range(sum(STEPS_BZ[:m]), sum(STEPS_BZ[:m + 1])):
                if n % KB == KB - 1:
                    last_units[m] = FREE + n // KB
        W_FROM = len(STEPS_BZ)

        def pv_bank(n):
            return ps_lg[1][:, BANK:2 * BANK] if n < 2 * EARLY else ps_pv[:, :]

        def head_no(t, h):
            return H * t + h

        groups_before = {t: H * t + H * max(0, t - 4) for t in range(T + 1)}

        def last_group(m):
            t, h = divmod(m, H)
            return t, h, int(t >= 4)

        def group_no(t, h, g):
            return groups_before[t] + h * (1 + (t >= 4)) + g

        def tp_release(key):
            kind = key[0]
            if kind == "k":
                return k_lo_done, key[1] + 1
            if kind == "w":
                return sguT_copied, 1
            if kind == "qi":
                return qi_lo_done, 2 * (key[1] - T0) + 2
            if kind == "sgu":
                return gate_ready, key[1] + 1
            if kind == "q":
                return q_lo_done, 2 * key[1] + 2
            if kind == "m":
                return m_lo_done, 2 * key[1] + key[2] + 1
            if kind == "y":
                return y_half, 2 * key[1] + key[2] + 1
            return pT_lo_done, group_no(*key[1:]) + 1

        block = ctx.enter_context(nc.Block())

        @block.sync
        def _(sp):
            def load_x(t):
                if t >= 4:
                    sp.wait_ge(xT_done, t - 3)
                    sp.wait_ge(ss_done, t - 3)
                sp.dma_start(x_in[:, t % 4, :], x[0, P * t:P * (t + 1), :]).then_inc(x_loaded[t % 4], 16)

            def load_w(c, k):
                c, k = c + k // KB, k % KB
                n = KB * (c - 1) + k
                if n >= NSTAGE:
                    sp.wait_ge(w_lo_done, KB + n - NSTAGE + 1)
                if c < O1:
                    src = w_in[0, P * k:P * (k + 1), chunk_src[c]:chunk_src[c] + BANK]
                else:
                    src = w_out[0, P * k:P * (k + 1), BANK * (c - O1):BANK * (c - O1 + 1)]
                sp.dma_start(stage[:, n % NSTAGE, :], src).then_inc(stage_loaded[n % NSTAGE], 16)

            def rows(t):
                return slice(P * t, P * (t + 1))

            def load_q(t):
                if t >= 2:
                    sp.wait_ge(qT_done, t - 1)
                sp.dma_start(q_in[t % 2][:, :], q_dram[rows(t), :]).then_inc(q_loaded[t % 2], 16)

            load_x(0)
            w_rows = w_in[0].rearrange("(k p) n -> p k n", p=P)
            for i in range(2):
                if i == 1:
                    load_x(1)
                half = slice(KB // 2 * i, KB // 2 * (i + 1))
                sp.dma_start(kvi_raw[:, half, 0:NKV], w_rows[:, half, o_bk:o_bk + NKV]).then_inc(kvi_loaded[i], 16)
                sp.dma_start(kvi_raw[:, half, NKV:N0], w_rows[:, half, o_ik:o_ik + NIK]).then_inc(kvi_loaded[i], 16)
            load_x(2)
            col = lambda v, n: v.rearrange("(k p) -> p k", p=n)
            with nc.allow_non_contiguous_dma(reason="gains as columns, a few KiB"):
                for dst, src in ((gk, k_norm_gain), (gik, idx_k_norm_gain), (gq, q_norm_gain)):
                    for half in range(2):
                        sp.dma_start(dst[DH * half:DH * (half + 1), :],
                                     col(src[0], DH)).then_inc(consts_loaded, 16)
            load_x(3)
            load_w(IQ, 0)
            with nc.allow_non_contiguous_dma(reason="gains as columns, a few KiB"):
                sp.dma_start(g_out[:, :], col(branch_norm_gain[0], P)).then_inc(consts_loaded, 16)
                sp.dma_start(bias_s[:, :], sgu_b[0].rearrange("g i -> i g")).then_inc(consts_loaded, 16)
            sp.dma_start(vg_row[:, :], sgu_norm_gain[0].partition_broadcast(P)).then_inc(consts_loaded, 16)
            sp.dma_start(sgu_raw[:, :, :], sgu_w[0].rearrange("g i j -> i g j")).then_inc(sgu_loaded, 16)
            for t in range(4, T):
                load_x(t)
                if 0 < t - 4 < NSTAGE:
                    load_w(IQ, t - 4)
            for k in range(NSTAGE, KB):
                load_w(IQ, k)
            for k in range(KB):
                load_w(BQ, k)

            def store_z(t):
                sp.wait_ge(proj_evac, unit(BZ, t) + 1)
                sp.dma_start(z_dram[P * t:P * (t + 1), :],
                             nat[:, unit(BZ, t) % 2, :]).then_inc(z_stored[t % 2], 16)

            def store_q(t):
                sp.wait_ge(q_normed, t + 1)
                sp.dma_start(q_dram[P * t:P * (t + 1), :],
                             nat[:, unit(BQ, t) % 2, :]).then_inc(q_stored[t % 2], 16)

            for t in range(T):
                if t == 0:
                    for k in range(NSTAGE):
                        load_w(AV, k)
                else:
                    load_w(AV, t + NSTAGE - 1)
                store_q(t)
            for c in (AU, AZ, BZ):
                for k in range(NSTAGE - 1 if c == AU else 0, KB):
                    load_w(c, k)
                if c == AZ:
                    for i in range(2):
                        sp.wait_ge(q_stored[i], 16 * T // 2)
                    sp.wait_ge(vgain_done, T)
                    for t in range(2):
                        load_q(t)
            def load_z(t):
                if t >= 2:
                    sp.wait_ge(y_gated, t - 1)
                sp.dma_start(z_in[t % 2], z_dram[rows(t), :].rearrange("p (k c) -> p k c", c=P)
                             ).then_inc(z_loaded[t % 2], 16)

            for t in range(T):
                if t == 0:
                    for k in range(NSTAGE):
                        load_w(O1, k)
                elif t + NSTAGE - 1 < KB:
                    load_w(O1, t + NSTAGE - 1)
                store_z(t)
                if t == 4:
                    load_z(0)
                    load_z(1)
                if t in (5, 6):
                    load_q(t - 3)
                if t == 6:
                    for k in range(KB):
                        sp.dma_start(last_raw[k], w_out[0, P * k:P * (k + 1), BANK:2 * BANK].rearrange(
                            "p (a c) -> p a c", a=2)).then_inc(last_w_loaded[k // 4], 16)

            def res_signal(t):
                return last_res_loaded if t == T - 1 else res_loaded, 16

            def load_res(t):
                if t == T - 1:
                    sp.wait_ge(max_done, H * 5)
                elif t >= 1:
                    sp.wait_ge(out_stored, 16 * t)
                sp.dma_start(res[t], x[0, rows(t), :].rearrange("p (k c) -> p k c", c=P)
                             ).then_inc(*res_signal(t))

            def store_out(t):
                sp.wait_ge(out_ready, 2 * (t + 1))
                sp.dma_start(out[0, rows(t), :].rearrange("p (k c) -> p k c", c=P),
                             res[t]).then_inc(out_stored, 16)

            sp.wait_ge(proj_done, UNITS)
            load_res(0)
            for i in range(2):
                sp.wait_ge(z_stored[i], 16 * T // 2)
            for t in range(T + 2):
                if 2 <= t < T - 2:
                    load_q(t + 2)
                if 2 <= t + 1 < T:
                    load_z(t + 1)
                if 2 <= t < T + 1:
                    store_out(t - 2)
                if 1 <= t - 1 < T - 1:
                    load_res(t - 1)
                if t == T - 1:
                    load_res(T - 1)
            for n in range(2):
                sp.wait_ge(out_ready, 2 * T - 1 + n)
                sp.dma_start(out[0, rows(T - 1), BANK * n:BANK * (n + 1)].rearrange("p (k c) -> p k c", c=P),
                             res[T - 1][:, 4 * n:4 * n + 4, :]).then_inc(out_stored, 16)
            sp.wait_ge(out_stored, 16 * (T + 1))

        @block.gpsimd
        def _(pool):
            pool.memset(ident[:, :], 0.0).then_inc(setup_step, 1)
            pool.wait_ge(setup_step, 1)
            pool.affine_select(out=ident[:, :], in_=ident[:, :], compare_op=ALU.not_equal, fill=1.0, base=0,
                               pattern=[[-1, P]], channel_multiplier=1).then_inc(ident_ready, 1)
            pool.wait_ge(ident_ready, 1)
            pool.tensor_tensor(fold[:, :], ident[:, 0:DH], ident[:, DH:P], ALU.add).then_inc(fold_ready, 1)
            pool.memset(nhalf[:, :], -0.5).then_inc(setup_step, 1)
            for h in range(H):
                pool.memset(q_scale[:, h:h + 1], (DH ** -0.5) * 2.0 ** (h + 1)).then_inc(setup_step, 1)
            pool.wait_ge(setup_step, 2 + H)

            pool.iota(dist_i[:, :], pattern=[[-1, S]], base=S - P,
                      channel_multiplier=1).then_inc(dist_ready, 1)

            def w_block(n):
                c, k = divmod(n, KB)
                if c == KVI:
                    return kvi_raw[:, k, :], w_hi[0][:, k, 0:N0], w_lo[0][:, k, 0:N0], k
                if c == O2:
                    return (last_raw[k], w_hi[0][:, k, :].rearrange("p (a c) -> p a c", a=2),
                            w_lo[0][:, k, :].rearrange("p (a c) -> p a c", a=2), k)
                return stage[:, (n - KB) % NSTAGE, :], w_hi[c % 2][:, k, :], w_lo[c % 2][:, k, :], k

            def scale_w(n):
                raw, _, _, k = w_block(n)
                if n < KB:
                    if n % (KB // 2) == 0:
                        pool.wait_ge(kvi_loaded[n // (KB // 2)], 32)
                    if n == 0:
                        pool.wait_ge(g_in_loaded, 16)
                elif n >= KB * O2:
                    pool.wait_ge(last_w_loaded[k // 4], 64)
                else:
                    m = n - KB
                    pool.wait_ge(stage_loaded[m % NSTAGE], 16 * (m // NSTAGE + 1))
                if n == KB * O1:
                    pool.wait_ge(consts_loaded, CONSTS)
                gain = g_in if n < KB * O1 else g_out
                pool.tensor_scalar(raw, raw, gain[:, k:k + 1], 1.0, ALU.mult, ALU.mult).then_inc(w_scaled, 1)

            def split_w(n):
                raw, hi, lo, _ = w_block(n)
                pool.wait_ge(w_hi_done, n + 1)
                pool.tensor_tensor(lo, raw, hi.bitcast(F32), ALU.subtract).then_inc(w_lo_done, 1)

            def rstd_rows(t):
                pool.wait_ge(ss_done, t + 1)
                pool.tensor_scalar(rstd_x[:, t:t + 1], ss_x[:, t:t + 1], 1.0 / D, EPS, ALU.mult,
                                   ALU.add).then_inc(ms_ready, 1)
                pool.wait_ge(ms_ready, t + 1)
                pool.tensor_tensor(rstd_x[:, t:t + 1], rstd_x[:, t:t + 1], nhalf[:, 0:1],
                                   ALU.pow).then_inc(rstd_ready, 1)

            def k_rows(t):
                rows = kvi[:, t % 2, :]
                pool.wait_ge(proj_evac, unit(KVI, t) + 1)
                pool.tensor_copy(v_hl[:, t, 0:DH], rows[:, DH:NKV]).then_inc(kvi_used, 1)
                pool.tensor_scalar(idx_w[:, t, :], rows[:, NKV + DH:N0], IDX_SCALE, 1.0,
                                   ALU.mult, ALU.mult).then_inc(kvi_used, 1)
                pool.wait_ge(kvi_used, 3 * t + 1)
                pool.tensor_tensor(v_hl[:, t, DH:2 * DH], rows[:, DH:NKV], v_hl[:, t, 0:DH].bitcast(F32),
                                   ALU.subtract).then_inc(kvi_used, 1)
                pool.wait_ge(kstat_done, 2 * (t + 1))
                pool.tensor_scalar(krstd[:, t % 2, :], kstat[:, t % 2, 1:3], EPS, 1.0,
                                   ALU.add, ALU.mult).then_inc(kms_ready, 1)
                pool.wait_ge(kms_ready, t + 1)
                pool.tensor_tensor(krstd[:, t % 2, :], krstd[:, t % 2, :], nhalf[:, 0:2],
                                   ALU.pow).then_inc(krstd_done, 1)

            for n in range(KB):
                scale_w(n)
            rstd_rows(0)
            pool.wait_ge(dist_ready, 2)
            pool.memset(near[0:HALF, TOPK - HALF:TOPK], NEG).then_inc(dist_ready, 1)
            for t in range(T):
                if t + 1 < T:
                    rstd_rows(t + 1)
                scale_w(KB + t)
                k_rows(t)
            pool.wait_ge(rstd_ready, T)
            pool.tensor_scalar(half_rstd[:, :], rstd_x[:, :], 0.5, 1.0, ALU.mult, ALU.mult).then_inc(half_rstd_ready, 1)
            pool.wait_ge(w_lo_done, 2 * KB)

            def next_block(n):
                split_w(n)
                if n + 2 != KB * O2 and n + 2 != KB * O2 + 1 and n + 2 < KB * (O2 + 1):
                    scale_w(n + 2)

            scale_w(KB * BQ)
            scale_w(KB * BQ + 1)
            for k in range(KB):
                next_block(KB * BQ + k)

            def av(t):
                pool.wait_ge(vstat_done, t + 1)
                pool.tensor_scalar(vrstd[:, :], vstat[:, :, 1], EPS, 1.0, ALU.add, ALU.mult).then_inc(veps_done, 1)
                pool.wait_ge(veps_done, t + 1)
                pool.tensor_tensor(vrstd[:, :], vrstd[:, :], nhalf[:, 0:G], ALU.pow).then_inc(vrstd_done, 1)

            def au(t):
                pool.wait_ge(proj_evac, unit(AU, t) + 1)
                pool.wait_ge(gate_ready, t + 1)
                pool.tensor_tensor(y_a[:, t, :], y_a[:, t, :], nat[:, unit(AU, t) % 2, :],
                                   ALU.mult).then_inc(ya_done, 1)

            def au_r(t):
                pool.wait_ge(ya_ms_done, t + 1)
                pool.tensor_scalar(ya_r[:, t, :], ya_ms[:, t, :], EPS, 1.0, ALU.add, ALU.mult).then_inc(ya_eps_done, 1)
                pool.wait_ge(ya_eps_done, t + 1)
                pool.tensor_tensor(ya_r[:, t, :], ya_r[:, t, :], nhalf[:, 0:G], ALU.pow).then_inc(ya_r_done, 1)

            def bq(t):
                pool.wait_ge(q_ss, t + 1)
                if t > 0:
                    pool.wait_ge(q_normed, t)
                pool.tensor_scalar(qr[:, :], qss[:, :], 1.0 / DH, EPS, ALU.mult, ALU.add).then_inc(q_step, 1)
                pool.wait_ge(q_step, 3 * t + 1)
                pool.tensor_tensor(qr[:, :], qr[:, :], nhalf[:, :], ALU.pow).then_inc(q_step, 1)
                pool.wait_ge(q_step, 3 * t + 2)
                pool.tensor_tensor(qr[:, :], qr[:, :], q_scale[:, :], ALU.mult).then_inc(q_step, 1)

            for t in range(T):
                bq(t)
                next_block(KB * AV + t)
            for t in range(T):
                av(t)
                next_block(KB * AU + t)
            for t in range(T):
                next_block(KB * AZ + t)
                au(t)
                if t > 0:
                    au_r(t - 1)
            au_r(T - 1)
            for c in (BZ, O1):
                for t in range(T):
                    next_block(KB * c + t)
                    if (c, t) == (O1, ROUNDS_FROM - 1):
                        pool.wait_ge(succ_wanted, 1)
                        pool.tensor_tensor(succ[:, SPLIT:T], cand[:, SPLIT:T], delta[:, SPLIT:T],
                                           ALU.add).then_inc(succ_ready, 1)

            def finish_b(t):
                pool.wait_ge(y_half, 2 * (t + 1))
                pool.wait_ge(z_loaded[t % 2], 16 * (t // 2 + 1))
                if t >= 1:
                    pool.wait_ge(mixB_done, t)
                else:
                    pool.wait_ge(z_stored[1], 16 * T // 2)
                pool.tensor_tensor(yz[:, :].rearrange("p (k c) -> p k c", c=P), yb[t % 2], z_in[t % 2],
                                   ALU.mult).then_inc(y_gated, 1)
                pool.wait_ge(y_ss, t + 1)
                pool.tensor_scalar(yr[:, :], yss[:, :], 1.0 / DH, EPS, ALU.mult, ALU.add).then_inc(y_step, 1)
                pool.wait_ge(y_step, 3 * t + 1)
                pool.tensor_tensor(yr[:, :], yr[:, :], nhalf[:, :], ALU.pow).then_inc(y_step, 1)
                pool.wait_ge(y_step, 3 * t + 2)
                factor = half_rstd[:, t:t + 1] if t >= FREE else 1.0
                pool.tensor_scalar(yr[:, :], yr[:, :], factor, 1.0, ALU.mult, ALU.mult).then_inc(y_step, 1)

            scale_w(KB * O2)
            scale_w(KB * O2 + 1)
            finish_b(0)
            for k in range(KB):
                next_block(KB * O2 + k)
            for t in range(1, T):
                finish_b(t)

        @block.scalar
        def _(act):
            with nc.allow_non_contiguous_dma(reason="a gain as columns, 4 KiB"):
                act.dma_start(g_in[:, :], norm_gain[0].rearrange("(k p) -> p k", p=P)).then_inc(g_in_loaded, 16)

            def hi_w(n):
                c, k = divmod(n, KB)
                act.wait_ge(w_scaled, n + 1)
                if k == 0 and c >= 2:
                    act.wait_ge(proj_done, T if c == 2 else unit(c - 1, 0))
                if c == KVI:
                    act.copy(w_hi[0][:, k, 0:N0], kvi_raw[:, k, :]).then_inc(w_hi_done, 1)
                elif c == O2:
                    act.copy(w_hi[0][:, k, :].rearrange("p (a c) -> p a c", a=2), last_raw[k]).then_inc(w_hi_done, 1)
                else:
                    act.copy(w_hi[c % 2][:, k, :], stage[:, (n - KB) % NSTAGE, :]).then_inc(w_hi_done, 1)

            def square_x(t):
                act.wait_ge(x_loaded[t % 4], 16 * (t // 4 + 1))
                if t > 0:
                    act.wait_ge(ss_done, t)
                act.activation(x_sq[:, :], x_in[:, t % 4, :], ACT.Square,
                               accum_out=ss_x[:, t:t + 1]).then_inc(ss_done, 1)

            def hi_x(t):
                act.wait_ge(xT_done, t + 1)
                act.copy(xT_hi[:, :, P * t:P * (t + 1)],
                         ps_lg[t % 2][:, :].rearrange("p (k s) -> p k s", k=KB)).then_inc(x_hi_done, 1)

            def evac_kvi(t):
                u = unit(KVI, t)
                act.wait_ge(proj_done, u + 1)
                act.wait_ge(rstd_ready, t + 1)
                if t >= 2:
                    act.wait_ge(kvi_used, 3 * (t - 1))
                    act.wait_ge(khat_done, 2 * (t - 1))
                act.activation(kvi[:, t % 2, :], ps_proj[u % 2][:, 0:N0], ACT.Copy,
                               scale=rstd_x[:, t:t + 1]).then_inc(proj_evac, 1)

            def hi_k(t):
                act.wait_ge(kT_done, t + 1)
                if t == 0:
                    act.wait_ge(consts_loaded, CONSTS)
                slot = ps_tp[tp_slot[("k", t)]]
                act.activation(k_hh[:, P * t:P * (t + 1)], slot[:, 0:P], ACT.Copy,
                               scale=gk[:, 0:1]).then_inc(k_hi_done, 1)
                act.activation(ki_hh[:, P * t:P * (t + 1)], slot[:, P:2 * P], ACT.Copy,
                               scale=gik[:, 0:1]).then_inc(k_hi_done, 1)

            hi_x(0)
            for k in range(KB // 2):
                hi_w(k)
            hi_x(1)
            for k in range(KB // 2, KB):
                hi_w(k)
            square_x(0)
            square_x(1)
            for t in range(T):
                evac_kvi(t)
                if t + 2 < T:
                    hi_x(t + 2)
                    square_x(t + 2)
                hi_w(KB + t)
                if t > 0:
                    hi_k(t - 1)

            nat_free = {
                IQ: lambda t: (qiT_done, t - T0 + 1),
                AV: lambda t: (sgu_done, t + 1),
                AU: lambda t: (ya_done, t + 1),
                AZ: lambda t: (mixA_done, t + 1),
                BZ: lambda t: (z_stored[t % 2], 16 * (t // 2 + 1)),
                BQ: lambda t: (q_stored[t % 2], 16 * (t // 2 + 1)),
            }
            order = [(IQ, t) for t in range(T0, T)] + [(c, t) for c in (BQ, AV, AU, AZ, BZ) for t in range(T)]
            func = {IQ: ACT.Copy, AV: ACT.Gelu_apprx_tanh, AU: ACT.Gelu_apprx_tanh, AZ: ACT.Silu,
                    BZ: ACT.Silu, BQ: ACT.Copy}

            def evac(c, t):
                u = unit(c, t)
                act.wait_ge(proj_done, u + 1)
                i = order.index((c, t))
                if i >= 2:
                    pc, pt = order[i - 2]
                    act.wait_ge(*nat_free[pc](pt))
                if c == BQ:
                    if t == 0:
                        act.wait_ge(kT_done, T)
                    else:
                        act.wait_ge(q_ss, t)
                    act.activation(q_sq_tmp, ps_proj[u % 2][:, :], ACT.Square,
                                   scale=rstd_x[:, t:t + 1]).then_inc(q_sq, 1)
                act.activation(nat[:, u % 2, :], ps_proj[u % 2][:, :], func[c],
                               scale=rstd_x[:, t:t + 1]).then_inc(proj_evac, 1)

            def tanh_z(t):
                u = unit(BZ, t)
                act.wait_ge(proj_done, u + 1)
                act.wait_ge(half_rstd_ready, 1)
                act.wait_ge(z_stored[t % 2], 16 * (t // 2))
                act.activation(nat[:, u % 2, :], ps_proj[u % 2][:, :], ACT.Tanh,
                               scale=half_rstd[:, t:t + 1]).then_inc(z_tanh, 1)

            def hi_qi(t):
                if t >= T0 + 2:
                    act.wait_ge(logits_done, H * (t - T0 - 1))
                act.wait_ge(qiT_done, t - T0 + 1)
                for odd in range(2):
                    bank = ps_tp[tp_slot[("qi", t)]][HALF * odd:HALF * (odd + 1), :]
                    act.copy(qi_stack[t % 2][0:HALF, odd:H:2, :],
                             bank.rearrange("p (h s) -> p h s", h=H // 2)).then_inc(qi_hi_done, 1)

            def relus(t, n):
                for h in range(H):
                    if h == 2 and t + 1 < T:
                        hi_qi(t + 1)
                    if h == 4:
                        hi_w(n)
                    m = H * (t - T0) + h
                    act.wait_ge(logits_done, m + 1)
                    if m >= 2:
                        act.wait_ge(score_acc, m - 1)
                    act.activation(relu_sb[:, m % 2, 0:keys(t)], ps_lg[m % 2][:, 0:keys(t)],
                                   ACT.Relu).then_inc(relu_done, 1)

            for t in range(T0, T):
                if t == T0 + 1:
                    hi_qi(T0)
                if t > T0 + 1:
                    relus(t - 2, KB * BQ + t - T0 + 2)
                evac(IQ, t)
                if t == T0:
                    hi_k(T - 1)
                    act.wait_ge(sguT_done, 1)
                    act.copy(wT_sgu[:, :, :], ps_tp[tp_slot[("w", 0)]][:, :].rearrange(
                        "p (g i) -> p g i", g=G)).then_inc(sguT_copied, 1)
                if t < T0 + 2:
                    hi_w(KB * BQ + 2 * (t - T0))
                    hi_w(KB * BQ + 2 * (t - T0) + 1)

            def w_and(c, t):
                hi_w(KB * (c + 1) + t)

            counts = T - SPLIT

            def count_round(r):
                act.wait_ge(cand_ready, r + 1)
                for i, t in enumerate(range(SPLIT, T)):
                    if i == 2:
                        act.wait_ge(act_counted, counts * r + 1)
                    act.activation(ps_lg[i % 2][:, 0:keys(t)], score[:, sc_off[t]:sc_off[t] + keys(t)], ACT.Sign,
                                   bias=cand[:, t:t + 1].bitcast(F32), scale=-1.0,
                                   accum_out=sign_sum[:, i:i + 1]).then_inc(act_counted, 1)

            def v_scale(t):
                act.wait_ge(vhat_done, t + 1)
                act.wait_ge(vrstd_done, t + 1)
                for g in range(G):
                    cols = nat[:, unit(AV, t) % 2, P * g:P * (g + 1)]
                    last = act.activation(cols, cols, ACT.Copy, scale=vrstd[:, g:g + 1])
                last.then_inc(vgain_done, 1)

            def hi_q(t):
                if t >= 2:
                    act.wait_ge(s_done, H * (t - 1))
                act.wait_ge(qT_done, t + 1)
                for odd in range(2):
                    half = slice(HALF * odd, HALF * (odd + 1))
                    act.activation(q_stack[t % 2][0:HALF, odd:H:2, :],
                                   ps_tp[tp_slot[("q", t)]][half, :].rearrange("p (h s) -> p h s", h=H // 2),
                                   ACT.Copy, scale=gq[half, 0:1]).then_inc(q_hi_done, 1)

            rounds = list(range(32))
            for t in range(T):
                if t < 2:
                    relus(T - 2 + t, KB * AV + t)
                evac(BQ, t)
                if t >= 2:
                    w_and(BQ, t)
                if t >= ROUNDS_FROM:
                    count_round(rounds.pop(0))
            for c in (AV, AU, AZ, BZ):
                for t in range(T if c != BZ else FREE):
                    evac(c, t)
                    w_and(c, t)
                    if (c, t) == (BZ, 2):
                        hi_q(0)
                    if rounds:
                        count_round(rounds.pop(0))
                    if c == AV:
                        v_scale(t)

            def exps(t, h):
                m = head_no(t, h)
                act.wait_ge(max_done, m + 1)
                if m >= 2 * H and h == 0:
                    act.wait_ge(rden_done, 2 * (t - 1))
                rows = probs[m % 2][:, 0:t + 1, :]
                act.activation(rows, rows, ACT.Exp,
                               bias=negmax[:, t % 2, h:h + 1], scale=-1.0,
                               accum_out=den[:, t % 2, h:h + 1]).then_inc(exp_done, 1)

            def hi_pT(t, h):
                m = head_no(t, h)
                for g in range(1 + (t >= 4)):
                    blocks = slice(4 * g, min(t + 1, 4 * g + 4))
                    nb = blocks.stop - blocks.start
                    act.wait_ge(pT_done, group_no(t, h, g) + 1)
                    if g == 0 and m == 4 * H:
                        act.wait_ge(pv_done, m // 2)
                    elif m >= 4 and g == 0 and m % 2 == 0:
                        act.wait_ge(pv_done, m // 2 - 1)
                    if g == 0 and m == 4 * H + 2:
                        act.wait_ge(w_lo_done, KB * (O2 + 1))
                    act.copy(probsT(xT_hi, m)[:, blocks, 0:P],
                             ps_tp[tp_slot[("p", t, h, g)]][:, 0:P * nb].rearrange("p (b s) -> p b s", b=nb)
                             ).then_inc(pT_hi_done, 1)

            def copy_yT(t, half):
                n = 2 * t + half
                act.wait_ge(pv_done, 2 * (n + 1))
                if n > 0:
                    act.wait_ge(yT_done, n)
                act.copy(yT[:, :, :], pv_bank(n).rearrange("p (h s) -> p h s", h=4)).then_inc(yT_copied, 1)

            def y_square(t):
                act.wait_ge(y_half, 2 * (t + 1))
                if t > 0:
                    act.wait_ge(y_ss, t)
                else:
                    act.wait_ge(z_stored[0], 16 * T // 2)
                act.activation(ysq[:, :].rearrange("p (k c) -> p k c", c=P), yb[t % 2], ACT.Square).then_inc(y_sq, 1)

            def hi_mix(t):
                for g in range(2):
                    if t == 0 and g == 0:
                        act.wait_ge(w_lo_done, KB * O2)
                    elif t == T - 1 and g == 1 or 0 < t < T - 1:
                        act.wait_ge(out_acc, 2 * t)
                    act.wait_ge(mT_done, 2 * t + g + 1)
                    act.copy(mixT_hi[:, 4 * g:4 * (g + 1), :],
                             ps_tp[tp_slot[("m", t, g)]][:, :].rearrange("p (k s) -> p k s", k=4)
                             ).then_inc(m_hi_done, 1)

            exps(0, 0)
            for t in range(T):
                for h in range(H):
                    m = head_no(t, h)
                    if m in last_units:
                        tanh_z(last_units[m])
                        w_and(BZ, last_units[m])
                    if h == MIX_AT and t > 0:
                        hi_mix(t - 1)
                    if h == Q_AT and t + 1 < T:
                        hi_q(t + 1)
                    if h == 0 and t > 0:
                        copy_yT(t - 1, 1)
                    if h == 4:
                        copy_yT(t, 0)
                    hi_pT(t, h)
                    if m + 1 < T * H:
                        exps(*divmod(m + 1, H))
                    if W_FROM <= m < W_FROM + KB:
                        hi_w(KB * O2 + m - W_FROM)
                    if h == 2 and t > 0:
                        y_square(t - 1)
            copy_yT(T - 1, 1)
            y_square(T - 1)
            hi_mix(T - 1)

        @block.tensor
        def _(pe):
            issued = []

            def tp(key):
                assert tp_plan[len(issued)] == key
                if len(issued) >= 2:
                    pe.wait_ge(*tp_release(issued[-2]))
                issued.append(key)
                return ps_tp[tp_slot[key]]

            def xT(t):
                pe.wait_ge(x_loaded[t % 4], 16 * (t // 4 + 1))
                if t >= 2:
                    pe.wait_ge(x_lo_done, t - 1)
                for k in range(KB):
                    mm = pe.transpose(ps_lg[t % 2][:, P * k:P * (k + 1)], x_in[:, t % 4, P * k:P * (k + 1)],
                                      ident[:, :])
                mm.then_inc(xT_done, 1)

            def project(c, t, between=lambda k: None):
                for k in range(KB):
                    between(k)
                    project_block(c, t, k)

            def project_block(c, t, k):
                u = unit(c, t)
                n = N0 if c == KVI else BANK
                if k == 0:
                    if c == KVI:
                        pe.wait_ge(x_lo_done, t + 1)
                    if u >= 2:
                        pe.wait_ge(proj_evac, u - 1)
                if t == (T0 if c == IQ else 0):
                    pe.wait_ge(w_lo_done, KB * c + k + 1)
                hi, lo = w_hi[c % 2], w_lo[c % 2]
                rows = slice(P * t, P * (t + 1))
                for i, (a, b) in enumerate(((xT_hi, hi), (xT_lo, hi), (xT_hi, lo))):
                    mm = pe.matmul(ps_proj[u % 2][:, 0:n], a[:, k, rows], b[:, k, 0:n],
                                   start=(k == 0 and i == 0), stop=(k == KB - 1 and i == 2))
                if k == KB - 1:
                    mm.then_inc(proj_done, 1)

            def kT(t):
                bank = tp(("k", t))
                for i in range(2):
                    pe.wait_ge(khat_done, 2 * t + i + 1)
                    mm = pe.transpose(bank[:, P * i:P * (i + 1)],
                                      khat[:, i, :, :].rearrange("p a d -> p (a d)"), ident[:, :])
                mm.then_inc(kT_done, 1)

            def four_pairs(bank, rows):
                for j in range(H // 2):
                    mm = pe.transpose(bank[:, P * j:P * (j + 1)], rows[:, P * j:P * (j + 1)], ident[:, :])
                return mm

            def qiT(t):
                pe.wait_ge(proj_evac, unit(IQ, t) + 1)
                four_pairs(tp(("qi", t)), nat[:, unit(IQ, t) % 2, :]).then_inc(qiT_done, 1)

            def dot_keys(bank, stack, h, hh, ll, n):
                for a in range(0, n, BANK):
                    b = min(n, a + BANK)
                    pe.matmul(bank[:, a:b], stack[:, h, :], hh[:, a:b], start=True, stop=False)
                    mm = pe.matmul(bank[:, a:b], stack[:, h, :], ll[:, a:b], start=False, stop=True)
                return mm

            def logit(t, h):
                if t == T0 and h == 0:
                    pe.wait_ge(x_lo_done, T)
                    pe.wait_ge(k_lo_done, T)
                m = H * (t - T0) + h
                pe.wait_ge(qi_lo_done, 2 * (t - T0) + h % 2 + 1)
                if m >= 2:
                    pe.wait_ge(relu_done, m - 1)
                dot_keys(ps_lg[m % 2], qi_stack[t % 2], h, ki_hh, ki_ll, keys(t)).then_inc(logits_done, 1)

            def index(t):
                def between(k):
                    if T0 <= t:
                        logit(t, k)
                    if k == 1 and t + 1 < T:
                        qiT(t + 1)
                return between

            def keep_busy(n):
                for _ in range(n):
                    pe.transpose(ps_tp[0][:, 0:P], ident[:, :], ident[:, :])

            pe.wait_ge(ident_ready, 1)
            keep_busy(WARM_0)
            xT(0)
            keep_busy(WARM_1)
            xT(1)
            for t in range(T):
                project(KVI, t)
                if t + 2 < T:
                    xT(t + 2)
                if t > 0:
                    kT(t - 1)
            for t in range(T0, T):
                if t == T0:
                    project(IQ, t)
                else:
                    project(IQ, t, index(t - 2))
                if t == T0:
                    kT(T - 1)
                    pe.wait_ge(sgu_loaded, 16)
                    bank = tp(("w", 0))
                    for g in range(G):
                        mm = pe.transpose(bank[:, P * g:P * (g + 1)], sgu_raw[:, g, :], ident[:, :])
                    mm.then_inc(sguT_done, 1)

            def sgu(t):
                pe.wait_ge(vgain_done, t + 1)
                pe.wait_ge(sguT_masked, 1)
                bank = tp(("sgu", t))
                for g in range(G):
                    mm = pe.matmul(bank[:, P * g:P * (g + 1)], wT_sgu[:, g, :],
                                   nat[:, unit(AV, t) % 2, P * g:P * (g + 1)], start=True, stop=True)
                mm.then_inc(sgu_done, 1)

            for t in range(T):
                if t < 2:
                    project(BQ, t, index(T - 2 + t))
                else:
                    project(BQ, t)
            for t in range(T):
                project(AV, t)
                if t > 0:
                    sgu(t - 1)
            project(AU, 0)
            sgu(T - 1)
            for t in range(1, T):
                project(AU, t)
            def qT(t):
                pe.wait_ge(q_loaded[t % 2], 16 * (t // 2 + 1))
                four_pairs(tp(("q", t)), q_in[t % 2][:, :]).then_inc(qT_done, 1)

            def scores(t, h):
                m = head_no(t, h)
                if h < 2:
                    pe.wait_ge(q_lo_done, 2 * t + h + 1)
                if m >= 2:
                    pe.wait_ge(max_done, m - 1)
                dot_keys(ps_lg[m % 2], q_stack[t % 2], h, k_hh, k_ll, keys(t)).then_inc(s_done, 1)

            def pT(t, h):
                m = head_no(t, h)
                pe.wait_ge(exp_done, m + 1)
                for g in range(1 + (t >= 4)):
                    bank = tp(("p", t, h, g))
                    for b in range(4 * g, min(t + 1, 4 * g + 4)):
                        mm = pe.transpose(bank[:, P * (b % 4):P * (b % 4 + 1)], probs[m % 2][:, b, :],
                                          ident[:, :])
                    mm.then_inc(pT_done, 1)

            def pv(j):
                t, h = divmod(2 * j, H)
                pe.wait_ge(pT_lo_done, group_no(t, h + 1, t >= 4) + 1)
                if j == 4 * EARLY:
                    pe.wait_ge(proj_evac, UNITS)
                if j > 0 and j % 2 == 0:
                    pe.wait_ge(yT_copied, j // 2)
                out_cols = slice(2 * P * (j % 2), 2 * P * (j % 2 + 1))
                for b in range(t + 1):
                    for i, part in enumerate((xT_hi, xT_lo)):
                        mm = pe.matmul(pv_bank(j // 2)[:, out_cols], v_hl[:, b, :],
                                       probsT(part, 2 * j)[:, b, :], start=(b == 0 and i == 0),
                                       stop=(b == t and i == 1))
                mm.then_inc(pv_done, 1)

            def turn_y(t, half):
                n = 2 * t + half
                pe.wait_ge(yT_copied, n + 1)
                bank = tp(("y", t, half))
                if n == 0:
                    pe.wait_ge(fold_ready, 1)
                for h in range(4):
                    mm = pe.matmul(bank[:, DH * h:DH * (h + 1)], yT[:, h, :], fold[:, :], start=True, stop=True)
                mm.then_inc(yT_done, 1)

            def mT(t, g):
                if g == 1:
                    pe.wait_ge(mixB_done, t + 1)
                bank = tp(("m", t, g))
                for j in range(4):
                    rows = y_a[:, t, P * j:P * (j + 1)] if g == 0 else yb[t % 2][:, j, :]
                    mm = pe.transpose(bank[:, P * j:P * (j + 1)], rows, ident[:, :])
                mm.then_inc(mT_done, 1)

            def out_block(t, n, k):
                hi, lo = w_hi[(O1 + n) % 2], w_lo[(O1 + n) % 2]
                for i, (a, b) in enumerate(((mixT_hi, hi), (mixT_lo, hi), (mixT_hi, lo))):
                    mm = pe.matmul(out_bank(t, n), a[:, k, :], b[:, k, :],
                                   start=(k == 0 and i == 0), stop=(k == KB - 1 and i == 2))
                return mm

            def out_steps(t):
                for n in range(2):
                    for k in range(KB):
                        if k == 0:
                            pe.wait_ge(m_lo_done, 2 * t + 2)
                            if 2 * t + n > 0:
                                pe.wait_ge(out_ready, 2 * t + n)
                        if t == 0:
                            pe.wait_ge(w_lo_done, KB * (O1 + n) + k + 1)
                            if n == 0 and k == 0:
                                pe.wait_ge(proj_evac, UNITS)
                        mm = out_block(t, n, k)
                        if k == KB - 1:
                            mm.then_inc(out_acc, 1)
                        yield

            for t in range(T):
                project(AZ, t)
            for t in range(FREE):
                if t == 2:
                    qT(0)
                project(BZ, t)

            def last_projections():
                for t in range(FREE, T):
                    for k in range(KB):
                        project_block(BZ, t, k)
                        yield

            pe.wait_ge(act_counted, (T - SPLIT) * 32)
            scores(0, 0)
            scores(0, 1)
            STEPS = {7: 3, 0: 3, 1: 2, 2: 2, 3: 2, 4: 2, 5: 1, 6: 1}
            assert sum(STEPS.values()) == 2 * KB
            pending = last_projections()
            for t in range(T):
                for h in range(H):
                    m = head_no(t, h)
                    if h == Q_AT and t + 1 < T:
                        qT(t + 1)
                    steps = STEPS[h]
                    if m < 8 + MIX_AT:
                        steps = STEPS_BZ[m] if m < len(STEPS_BZ) else 0
                    for _ in range(steps):
                        next(pending, None)
                    if h == YT_AT[0]:
                        turn_y(t, 0)
                    if h == YT_AT[1] and t > 0:
                        turn_y(t - 1, 1)
                    if h == MIX_AT and t > 0:
                        mT(t - 1, 0)
                        mT(t - 1, 1)
                        pending = out_steps(t - 1)
                    if m % 2 == 0 and m > 0:
                        pv(m // 2 - 1)
                    pT(t, h)
                    if m + 2 < T * H:
                        scores(*divmod(m + 2, H))
            pv(T * H // 2 - 1)
            left = 2 * KB - STEPS[7]
            for i in range(left):
                if i == 2:
                    turn_y(T - 1, 1)
                if i == left - 4:
                    mT(T - 1, 0)
                next(pending)
            mT(T - 1, 1)
            for blocks in (range(4), range(4, KB)):
                for n in range(2):
                    for k in blocks:
                        pe.wait_ge(m_lo_done, 2 * T - 1 + (k >= 4))
                        last = out_block(T - 1, n, k)
                    if k == KB - 1:
                        last.then_inc(out_acc, 1)

        @block.vector
        def _(dve):
            steps = [0]

            def then(ins):
                steps[0] += 1
                ins.then_inc(dve_step, 1)
                dve.wait_ge(dve_step, steps[0])

            def lo_x(t):
                dve.wait_ge(x_hi_done, t + 1)
                rows = slice(P * t, P * (t + 1))
                dve.tensor_tensor(xT_lo[:, :, rows], ps_lg[t % 2][:, :].rearrange("p (k s) -> p k s", k=KB),
                                  xT_hi[:, :, rows].bitcast(F32), ALU.subtract).then_inc(x_lo_done, 1)

            def k_stats(t):
                rows = kvi[:, t % 2, :]
                dve.wait_ge(proj_evac, unit(KVI, t) + 1)
                if t >= 2:
                    dve.wait_ge(krstd_done, t - 1)
                then(dve.bn_stats(bn6[:, 0, :], rows[:, NKV:NKV + DH]))
                dve.bn_aggr(kstat[:, t % 2, 0:2], bn6[:, 0, :]).then_inc(kstat_done, 1)
                dve.tensor_tensor_reduce(bn_tmp, rows[:, 0:DH], rows[:, 0:DH], 1.0 / DH, 0.0, ALU.mult,
                                         ALU.add, kstat[:, t % 2, 2:3]).then_inc(kstat_done, 1)

            def k_norm(t):
                rows = kvi[:, t % 2, :]
                dve.wait_ge(krstd_done, t + 1)
                if t >= 1:
                    dve.wait_ge(kT_done, t)
                twice = lambda v: v.unsqueeze(1).broadcast_to([P, 2, DH])
                dve.tensor_scalar(khat[:, 0, :, :], twice(rows[:, 0:DH]), krstd[:, t % 2, 1:2], None,
                                  ALU.mult).then_inc(khat_done, 1)
                dve.tensor_scalar(khat[:, 1, :, :], twice(rows[:, NKV:NKV + DH]), kstat[:, t % 2, 0:1],
                                  krstd[:, t % 2, 0:1], ALU.subtract, ALU.mult).then_inc(khat_done, 1)

            def lo_k(t):
                dve.wait_ge(k_hi_done, 2 * (t + 1))
                bank = ps_tp[tp_slot[("k", t)]]
                cols = slice(P * t, P * (t + 1))
                dve.scalar_tensor_tensor(out=k_ll[:, cols], in0=bank[:, 0:P], scalar=gk[:, 0:1],
                                         in1=k_hh[:, cols].bitcast(F32), op0=ALU.mult, op1=ALU.subtract)
                dve.scalar_tensor_tensor(out=ki_ll[:, cols], in0=bank[:, P:2 * P], scalar=gik[:, 0:1],
                                         in1=ki_hh[:, cols].bitcast(F32), op0=ALU.mult,
                                         op1=ALU.subtract).then_inc(k_lo_done, 1)

            dve.wait_ge(dist_ready, 1)
            dve.scalar_tensor_tensor(out=negdist[:, :], in0=dist_i[:, :], scalar=-1.0, in1=dist_i[:, :],
                                     op0=ALU.mult, op1=ALU.min)
            dve.scalar_tensor_tensor(out=near[:, :], in0=dist_i[:, S - TOPK:S], scalar=-1.0,
                                     in1=dist_i[:, S - TOPK:S], op0=ALU.mult,
                                     op1=ALU.min).then_inc(dist_ready, 1)
            def lo_w(n):
                c, k = divmod(n, KB)
                dve.wait_ge(w_hi_done, n + 1)
                if c == KVI:
                    raw, hi, lo = kvi_raw[:, k, :], w_hi[0][:, k, 0:N0], w_lo[0][:, k, 0:N0]
                else:
                    raw, hi, lo = stage[:, k % NSTAGE, :], w_hi[c][:, k, :], w_lo[c][:, k, :]
                dve.tensor_tensor(lo, raw, hi.bitcast(F32), ALU.subtract).then_inc(w_lo_done, 1)

            lo_x(0)
            for k in range(KB // 2):
                lo_w(k)
            lo_x(1)
            for k in range(KB // 2, KB):
                lo_w(k)
            for t in range(T):
                if t == 1:
                    dve.wait_ge(consts_loaded, CONSTS)
                k_stats(t)
                if t + 2 < T:
                    lo_x(t + 2)
                k_norm(t)
                lo_w(KB + t)
                if t > 0:
                    lo_k(t - 1)

            def lo_qi(t):
                for odd in range(2):
                    dve.wait_ge(qi_hi_done, 2 * (t - T0) + odd + 1)
                    bank = ps_tp[tp_slot[("qi", t)]][HALF * odd:HALF * (odd + 1), :]
                    dve.tensor_tensor(qi_stack[t % 2][HALF:P, odd:H:2, :],
                                      bank.rearrange("p (h s) -> p h s", h=H // 2),
                                      qi_stack[t % 2][0:HALF, odd:H:2, :].bitcast(F32),
                                      ALU.subtract).then_inc(qi_lo_done, 1)

            def sum_heads(t):
                row = score[:, sc_off[t]:sc_off[t] + keys(t)]
                for h in range(H):
                    if h == 2 and t + 1 < T:
                        lo_qi(t + 1)
                    m = H * (t - T0) + h
                    dve.wait_ge(relu_done, m + 1)
                    r = relu_sb[:, m % 2, 0:keys(t)]
                    if h == 0:
                        dve.wait_ge(kvi_used, 3 * T)
                        dve.tensor_scalar(row, r, idx_w[:, t, 0:1], None, ALU.mult).then_inc(score_acc, 1)
                    else:
                        dve.wait_ge(score_acc, m)
                        dve.scalar_tensor_tensor(out=row, in0=r, scalar=idx_w[:, t, h:h + 1], in1=row,
                                                 op0=ALU.mult, op1=ALU.add).then_inc(score_acc, 1)
                dve.wait_ge(score_acc, H * (t - T0 + 1))
                then(dve.memset(row[0:HALF, keys(t) - HALF:keys(t)], NEG))

            for t in range(T0, T):
                if t == T0:
                    lo_k(T - 1)
                    dve.wait_ge(dist_ready, 3)
                    dve.wait_ge(sguT_done, 1)
                    dve.wait_ge(w_lo_done, KB)
                if t == T0 + 1:
                    lo_qi(T0)
                if t > T0 + 1:
                    sum_heads(t - 2)
            dve.wait_ge(sguT_copied, 1)
            dve.memset(wT_sgu[HALF:P, :, 0:HALF], 0.0).then_inc(sguT_masked, 1)

            cand_f = cand[:, :].bitcast(F32)

            hits = (gt, eq, rank)
            counted = [0]
            selected = [0]

            def count_tile(t, against=cand):
                n = counted[0]
                counted[0] += 1
                if selected[0]:
                    dve.wait_ge(mask_ready, selected[0])
                if n >= len(hits):
                    dve.wait_ge(tile_counted, n - len(hits) + 1)
                return dve.tensor_scalar(hits[n % len(hits)][:, 0:keys(t)], score[:, sc_off[t]:sc_off[t] + keys(t)],
                                         against[:, t:t + 1].bitcast(F32), None, ALU.is_ge, ALU.add,
                                         accum_out=cnt[:, t:t + 1]).then_inc(tile_counted, 1)

            def settle(b, tiles):
                c, d = cand[:, tiles], delta[:, tiles]
                if b == 31:
                    return dve.tensor_scalar(c, d, 1 << 30, None, ALU.bitwise_xor)
                return dve.scalar_tensor_tensor(out=c, in0=d, scalar=(1 << b) >> 1, in1=c,
                                                op0=ALU.bitwise_xor, op1=ALU.bitwise_xor)

            def too_few(b, counts, d, limit, op):
                return dve.tensor_scalar(d, counts, limit, -1.0 if b == 31 else float(1 << b), op, ALU.mult)

            def step_first(b):
                for t in range(T0, SPLIT):
                    count_tile(t)
                dve.wait_ge(tile_counted, counted[0])
                then(too_few(b, cnt[:, T0:SPLIT], delta[:, T0:SPLIT], TOPK - 0.5, ALU.is_lt))
                then(settle(b, slice(T0, SPLIT)))

            def step_last(b):
                dve.wait_ge(act_counted, (T - SPLIT) * (32 - b))
                for i, t in enumerate(range(SPLIT, T)):
                    last = too_few(b, sign_sum[:, i:i + 1], delta[:, t:t + 1], keys(t) - 2.0 * TOPK + 1.0,
                                   ALU.is_gt)
                then(last)
                settle(b, slice(SPLIT, T)).then_inc(cand_ready, 1)
                dve.wait_ge(cand_ready, 33 - b)

            def after_ties():
                last = slice(SPLIT, T)
                dve.wait_ge(succ_ready, 1)
                for t in range(SPLIT, T):
                    count_tile(t, succ)
                    yield
                dve.wait_ge(tile_counted, counted[0])
                then(dve.tensor_tensor(succ[:, last], succ[:, last], cand[:, last], ALU.bitwise_xor))
                then(dve.tensor_scalar(delta[:, last], cnt[:, last], TOPK - 0.5, -1.0, ALU.is_ge, ALU.mult))
                then(dve.tensor_tensor(succ[:, last], succ[:, last], delta[:, last], ALU.bitwise_and))
                then(dve.tensor_tensor(cand[:, last], cand[:, last], succ[:, last], ALU.bitwise_xor))

            def select(t):
                row = score[:, sc_off[t]:sc_off[t] + keys(t)]
                thr = cand_f[:, t:t + 1]
                n = keys(t)
                if selected[0]:
                    dve.wait_ge(mask_ready, selected[0])
                dve.wait_ge(tile_counted, counted[0])
                selected[0] += 1
                dve.tensor_scalar(gt[:, 0:n], row, thr, None, ALU.is_gt, ALU.add, accum_out=cnt[:, t:t + 1])
                yield
                then(dve.tensor_scalar(eq[:, 0:n], row, thr, None, ALU.is_equal))
                then(dve.tensor_scalar(room[:, t:t + 1], cnt[:, t:t + 1], -1.0, float(TOPK), ALU.mult, ALU.add))
                yield
                then(dve.tensor_tensor_scan(rank[:, 0:n], eq[:, 0:n], eq[:, 0:n], 0.0, ALU.add, ALU.max))
                yield
                then(dve.scalar_tensor_tensor(out=eq[:, 0:n], in0=rank[:, 0:n], scalar=room[:, t:t + 1],
                                              in1=eq[:, 0:n], op0=ALU.is_le, op1=ALU.mult))
                yield
                then(dve.scalar_tensor_tensor(out=gt[:, 0:n], in0=gt[:, 0:n], scalar=-1.0, in1=eq[:, 0:n],
                                              op0=ALU.add, op1=ALU.add))
                yield
                dve.scalar_tensor_tensor(out=row, in0=gt[:, 0:n], scalar=-NEG, in1=negdist[:, S - n:S],
                                         op0=ALU.mult, op1=ALU.add).then_inc(mask_ready, 1)

            def av_stats(t):
                rows = nat[:, unit(AV, t) % 2, :]
                dve.wait_ge(proj_evac, unit(AV, t) + 1)
                for g in range(G):
                    last = dve.bn_stats(bn6[:, g, :], rows[:, P * g:P * (g + 1)])
                then(last)
                if t > 0:
                    dve.wait_ge(vgain_done, t)
                for g in range(G):
                    last = dve.bn_aggr(vstat[:, g, :], bn6[:, g, :])
                last.then_inc(vstat_done, 1)

            def av_norm(t):
                rows = nat[:, unit(AV, t) % 2, :]
                dve.wait_ge(vstat_done, t + 1)
                for g in range(G):
                    cols = rows[:, P * g:P * (g + 1)]
                    last = dve.scalar_tensor_tensor(out=cols, in0=cols, scalar=vstat[:, g, 0:1],
                                                    in1=vg_row[:, P * g:P * (g + 1)],
                                                    op0=ALU.subtract, op1=ALU.mult)
                last.then_inc(vhat_done, 1)

            def gate(t):
                dve.wait_ge(sgu_done, t + 1)
                dve.tensor_tensor(y_a[:, t, :].rearrange("p (g c) -> p g c", g=G),
                                  ps_tp[tp_slot[("sgu", t)]][:, :].rearrange("p (g c) -> p g c", g=G),
                                  bias_s[:, :].unsqueeze(2).broadcast_to([P, G, P]),
                                  ALU.add).then_inc(gate_ready, 1)

            def ya_square(t):
                dve.wait_ge(ya_done, t + 1)
                for g in range(G):
                    cols = y_a[:, t, P * g:P * (g + 1)]
                    last = dve.tensor_tensor_reduce(ya_tmp[:, g, :], cols, cols, 1.0 / P, 0.0, ALU.mult, ALU.add,
                                                    ya_ms[:, t, g:g + 1])
                last.then_inc(ya_ms_done, 1)

            def mix_a(t):
                dve.wait_ge(proj_evac, unit(AZ, t) + 1)
                dve.wait_ge(ya_r_done, t + 1)
                for g in range(G):
                    cols = slice(P * g, P * (g + 1))
                    last = dve.scalar_tensor_tensor(out=y_a[:, t, cols], in0=y_a[:, t, cols],
                                                    scalar=ya_r[:, t, g:g + 1],
                                                    in1=nat[:, unit(AZ, t) % 2, cols],
                                                    op0=ALU.mult, op1=ALU.mult)
                last.then_inc(mixA_done, 1)

            def q_norm(t):
                heads = nat[:, unit(BQ, t) % 2, :].rearrange("p (h d) -> p h d", h=H)
                dve.wait_ge(proj_evac, unit(BQ, t) + 1)
                dve.wait_ge(q_step, 3 * t + 3)
                dve.tensor_tensor(heads, heads, qr[:, :].unsqueeze(2).broadcast_to([P, H, DH]),
                                  ALU.mult).then_inc(q_normed, 1)

            def q_sums(t):
                dve.wait_ge(q_sq, t + 1)
                if t > 0:
                    dve.wait_ge(q_step, 3 * t)
                dve.tensor_reduce(qss[:, :], q_sq_tmp.rearrange("p (h d) -> p h d", h=H), AX.X,
                                  ALU.add).then_inc(q_ss, 1)

            work = {"first": list(range(31, -1, -1)), "last": list(range(31, -1, -1)),
                    "tiles": list(range(T0, T))}

            LATE = 4

            def background(first, last):
                if first and work["first"]:
                    step_first(work["first"].pop(0))
                if last and work["last"]:
                    step_last(work["last"].pop(0))
                    if not work["last"]:
                        dve.tensor_scalar(delta[:, SPLIT:T], cand[:, SPLIT:T], 31, 1, ALU.arith_shift_right,
                                          ALU.bitwise_or).then_inc(succ_wanted, 1)
                if not work["first"] and work["tiles"][0] < LATE:
                    for _ in select(work["tiles"].pop(0)):
                        pass

            for t in range(T):
                if t == 0:
                    sum_heads(T - 2)
                    then(dve.memset(cand[:, :].bitcast(F32), 0.0))
                if t == 1:
                    sum_heads(T - 1)
                    dve.memset(delta[:, T - 1:T], 0).then_inc(cand_ready, 1)
                q_sums(t)
                background(True, False)
                q_norm(t)
                background(False, t >= ROUNDS_FROM)
            for t in range(T):
                av_stats(t)
                av_norm(t)
                if t > 0:
                    gate(t - 1)
                background(True, True)
            for t in range(T):
                if t == 0:
                    gate(T - 1)
                ya_square(t)
                background(True, True)
            for t in range(T):
                mix_a(t)
                background(True, True)
            while work["last"] or work["tiles"][0] < LATE:
                background(True, True)

            def late_steps():
                for t in range(LATE, SPLIT):
                    yield from select(t)
                    yield
                yield from after_ties()
                yield
                for t in range(SPLIT, T):
                    yield from select(t)
                    yield

            late = late_steps()

            def twice_silu(t):
                u = unit(BZ, t)
                rows = nat[:, u % 2, :]
                dve.wait_ge(z_tanh, t - FREE + 1)
                dve.scalar_tensor_tensor(out=rows, in0=rows, scalar=1.0, in1=ps_proj[u % 2][:, :],
                                         op0=ALU.add, op1=ALU.mult).then_inc(proj_evac, 1)

            def lo_q(t):
                for odd in range(2):
                    dve.wait_ge(q_hi_done, 2 * t + odd + 1)
                    half = slice(HALF * odd, HALF * (odd + 1))
                    dve.scalar_tensor_tensor(
                        out=q_stack[t % 2][HALF:P, odd:H:2, :],
                        in0=ps_tp[tp_slot[("q", t)]][half, :].rearrange("p (h s) -> p h s", h=H // 2),
                        scalar=gq[half, 0:1], in1=q_stack[t % 2][0:HALF, odd:H:2, :].bitcast(F32),
                        op0=ALU.mult, op1=ALU.subtract).then_inc(q_lo_done, 1)

            def bias_max(t, h):
                m = head_no(t, h)
                dve.wait_ge(s_done, m + 1)
                if m >= 2:
                    dve.wait_ge(pT_done, group_no(*last_group(m - 2)) + 1)
                if t < T0:
                    d = near[:, TOPK - keys(t):TOPK]
                else:
                    if h == 0:
                        dve.wait_ge(mask_ready, t - T0 + 1)
                    d = score[:, sc_off[t]:sc_off[t] + keys(t)]
                blocks = lambda v: v.rearrange("p (b s) -> p b s", s=P)
                dve.tensor_tensor_reduce(probs[m % 2][:, 0:t + 1, :], blocks(ps_lg[m % 2][:, 0:keys(t)]), blocks(d),
                                         -(2.0 ** -(h + 1)), BIG, ALU.add, ALU.min,
                                         negmax[:, t % 2, h:h + 1]).then_inc(max_done, 1)

            def lo_pT(t, h):
                m = head_no(t, h)
                for g in range(1 + (t >= 4)):
                    blocks = slice(4 * g, min(t + 1, 4 * g + 4))
                    nb = blocks.stop - blocks.start
                    dve.wait_ge(pT_hi_done, group_no(t, h, g) + 1)
                    dve.tensor_tensor(probsT(xT_lo, m)[:, blocks, 0:P],
                                      ps_tp[tp_slot[("p", t, h, g)]][:, 0:P * nb].rearrange(
                                          "p (b s) -> p b s", b=nb),
                                      probsT(xT_hi, m)[:, blocks, 0:P].bitcast(F32),
                                      ALU.subtract).then_inc(pT_lo_done, 1)

            def y_rows(t, half):
                n = 2 * t + half
                heads = slice(4 * half, 4 * half + 4)
                if half == 0 and t > 1:
                    dve.wait_ge(mT_done, 2 * (t - 1))
                rows = yb[t % 2][:, 2 * half:2 * half + 2, :].rearrange("p k (a d) -> p k a d", d=DH)
                dve.wait_ge(exp_done, H * t + 4 * (half + 1))
                dve.reciprocal(rden[:, heads], den[:, t % 2, heads]).then_inc(rden_done, 1)
                dve.wait_ge(yT_done, n + 1)
                dve.wait_ge(rden_done, n + 1)
                dve.tensor_tensor(
                    rows, ps_tp[tp_slot[("y", t, half)]][:, 0:B_W // 2].rearrange("p (k a d) -> p k a d", a=2, d=DH),
                    rden[:, heads].rearrange("p (k a) -> p k a", a=2).unsqueeze(3).broadcast_to([P, 2, 2, DH]),
                    ALU.mult).then_inc(y_half, 1)

            def mix_b(t):
                dve.wait_ge(y_gated, t + 1)
                dve.wait_ge(y_step, 3 * (t + 1))
                dve.tensor_tensor(yb[t % 2].rearrange("p k (a d) -> p k a d", d=DH),
                                  yz[:, :].rearrange("p (k a d) -> p k a d", a=2, d=DH),
                                  yr[:, :].rearrange("p (k a) -> p k a", a=2).unsqueeze(3).broadcast_to(
                                      [P, 4, 2, DH]), ALU.mult).then_inc(mixB_done, 1)

            def y_sums(t):
                dve.wait_ge(y_sq, t + 1)
                dve.tensor_reduce(yss[:, :], ysq[:, :].rearrange("p (h d) -> p h d", h=H), AX.X,
                                  ALU.add).then_inc(y_ss, 1)

            def lo_mix(t, g):
                dve.wait_ge(m_hi_done, 2 * t + g + 1)
                part = slice(4 * g, 4 * (g + 1))
                dve.tensor_tensor(mixT_lo[:, part, :],
                                  ps_tp[tp_slot[("m", t, g)]][:, :].rearrange("p (k s) -> p k s", k=4),
                                  mixT_hi[:, part, :].bitcast(F32), ALU.subtract).then_inc(m_lo_done, 1)

            def add_res(t, n):
                dve.wait_ge(out_acc, 2 * t + n + 1)
                if n == 0:
                    if t < T - 1:
                        dve.wait_ge(res_loaded, 16 * (t + 1))
                    else:
                        dve.wait_ge(last_res_loaded, 16)
                half = res[t][:, 4 * n:4 * n + 4, :]
                dve.tensor_tensor(half, out_bank(t, n).rearrange("p (k c) -> p k c", c=P), half,
                                  ALU.add).then_inc(out_ready, 1)

            lo_q(0)
            bias_max(0, 0)
            bias_max(0, 1)
            for t in range(T):
                for h in range(H):
                    m = head_no(t, h)
                    if m in last_units:
                        twice_silu(last_units[m])
                    if h == YT_AT[0]:
                        y_rows(t, 0)
                    if h == YT_AT[1] and t > 0:
                        y_rows(t - 1, 1)
                    if h == 1 and t > 1:
                        add_res(t - 2, 0)
                    if h == 6 and t > 1:
                        add_res(t - 2, 1)
                    if h == MIX_AT and t > 0:
                        lo_mix(t - 1, 0)
                        lo_mix(t - 1, 1)
                    if h == Q_AT and t + 1 < T:
                        lo_q(t + 1)
                    if m + 2 < T * H:
                        if t < 4:
                            bias_max(*divmod(m + 2, H))
                    lo_pT(t, h)
                    if t >= 4 and m + 2 < T * H:
                        bias_max(*divmod(m + 2, H))
                    if h == 2 and t > 0:
                        y_sums(t - 1)
                    if h == 4 and t > 0:
                        mix_b(t - 1)
                    if h in (1, 3, 7) or t >= 1 and h in (0, 6):
                        next(late, None)
            y_rows(T - 1, 1)
            y_sums(T - 1)
            add_res(T - 2, 0)
            mix_b(T - 1)
            lo_mix(T - 1, 0)
            add_res(T - 2, 1)
            lo_mix(T - 1, 1)
            add_res(T - 1, 0)
            add_res(T - 1, 1)


_INS = ["x", "norm_gain", "w_in", "sgu_norm_gain", "sgu_w", "sgu_b", "q_norm_gain", "k_norm_gain",
        "idx_k_norm_gain", "branch_norm_gain", "w_out"]
_OUTS = [((1, 1024, 1024), "float32")]


def kernel(**inputs):
    import numpy as _np
    import concourse.bacc as _bacc
    from concourse import mybir as _mybir
    from concourse.bass_utils import run_bass_kernel_spmd as _run

    nc = _bacc.Bacc("TRN2", target_bir_lowering=False, num_devices=1)
    arrays, args = {}, []
    for name in _INS:
        a = _np.ascontiguousarray(inputs[name])
        arrays[f"in_{name}_dram"] = a
        args.append(nc.dram_tensor(f"in_{name}_dram", a.shape, _mybir.dt.from_np(a.dtype), kind="ExternalInput").ap())
    for i, (shape, dtype) in enumerate(_OUTS):
        dt = _mybir.dt.from_np(_np.dtype(dtype))
        args.append(nc.dram_tensor(f"out_{i}_dram", shape, dt, kind="ExternalOutput").ap())
    hybrid_block(nc, *args)
    r = _run(nc, [arrays], core_ids=[0])
    got = tuple(r.results[0][f"out_{i}_dram"] for i in range(len(_OUTS)))
    return got[0]
```
